# Optimizing a Trainium2 kernel written in Bass

```python
import math
import jax
import jax.numpy as jnp
from jax import lax
import numpy as np
import jax, jax.numpy as jnp

D_MODEL = 1024
BATCH = 1
SEQ = 512
DEPTH = 1

EPS = 1e-6
D_MIX = D_MODEL

GLA_HEADS = 4
GLA_DK = 64
GLA_DV = 128
GLA_WIDTH = GLA_HEADS * GLA_DV
GLA_QK_WIDTH = GLA_HEADS * GLA_DK
GLA_GATE_RANK = 16
GLA_GATE_NORMALIZER = 16.0
GLA_CHUNK = 64

SSD_HEADS = 8
SSD_HEAD_DIM = 64
SSD_WIDTH = SSD_HEADS * SSD_HEAD_DIM
SSD_GROUPS = 2
SSD_STATE = 64
SSD_CONV = 4
SSD_CHUNK = 128
SSD_BC_WIDTH = SSD_GROUPS * SSD_STATE
SSD_CONV_DIM = SSD_WIDTH + 2 * SSD_BC_WIDTH

IN_SIZES = (GLA_QK_WIDTH, GLA_QK_WIDTH, GLA_WIDTH, GLA_GATE_RANK, GLA_WIDTH,
            SSD_WIDTH, SSD_CONV_DIM, SSD_HEADS)
IN_TOTAL = (2 * GLA_QK_WIDTH + 2 * GLA_WIDTH + GLA_GATE_RANK
            + SSD_WIDTH + SSD_CONV_DIM + SSD_HEADS)

PEER_HEADS = 8
PEER_KEYS = 128
PEER_EXPERTS = PEER_KEYS * PEER_KEYS
PEER_TOPK = 16
PEER_DQ = 256
PEER_HALF = PEER_DQ // 2
PEER_BLOCK = 128


def rmsnorm(x, w):
    xf = x.astype(jnp.float32)
    xf = xf * lax.rsqrt(jnp.mean(xf * xf, axis=-1, keepdims=True) + EPS)
    return xf * w.astype(jnp.float32)

def split_cols(proj):
    out, start = [], 0
    for size in IN_SIZES:
        out.append(proj[..., start:start + size])
        start += size
    return out

def gla_mixer(q, k, v, gate_lr, g_out, w_gate2, b_gate, norm_w):
    f32 = jnp.float32
    b, l, _ = q.shape
    nc, C, H = l // GLA_CHUNK, GLA_CHUNK, GLA_HEADS
    q = q.astype(f32).reshape(b, nc, C, H, GLA_DK) * (GLA_DK ** -0.5)
    k = k.astype(f32).reshape(b, nc, C, H, GLA_DK)
    v = v.astype(f32).reshape(b, nc, C, H, GLA_DV)
    log_a = jax.nn.log_sigmoid((gate_lr.astype(f32) @ w_gate2.astype(f32)
                                + b_gate.astype(f32))) / GLA_GATE_NORMALIZER
    log_a = log_a.reshape(b, nc, C, H, GLA_DK)
    G = jnp.cumsum(log_a, axis=2)
    G_last = G[:, :, -1:]
    q_in = q * jnp.exp(G)
    k_in = k * jnp.exp(-G)
    k_end = k * jnp.exp(G_last - G)
    causal = jnp.tril(jnp.ones((C, C), dtype=bool))
    att = jnp.einsum('bcihd,bcjhd->bchij', q_in, k_in)
    att = jnp.where(causal, att, 0.0)
    o_intra = jnp.einsum('bchij,bcjhv->bcihv', att, v)
    chunk_state = jnp.einsum('bcjhd,bcjhv->bchdv', k_end, v)
    chunk_decay = jnp.exp(G_last[:, :, 0])

    def step(S, inp):
        dec, st = inp
        return dec[..., None] * S + st, S

    S0 = jnp.zeros((b, H, GLA_DK, GLA_DV), f32)
    _, S_prev = lax.scan(step, S0, (jnp.moveaxis(chunk_decay, 1, 0),
                                    jnp.moveaxis(chunk_state, 1, 0)))
    S_prev = jnp.moveaxis(S_prev, 0, 1)
    o_inter = jnp.einsum('bcihd,bchdv->bcihv', q_in, S_prev)
    o = (o_intra + o_inter).reshape(b, l, H, GLA_DV)
    o = rmsnorm(o, norm_w)
    return o.reshape(b, l, GLA_WIDTH) * jax.nn.silu(g_out.astype(f32))

def causal_depthwise_conv(x, w, bias):
    c = x.shape[-1]
    out = lax.conv_general_dilated(
        x, w.astype(x.dtype)[:, None, :], window_strides=(1,),
        padding=[(SSD_CONV - 1, 0)], dimension_numbers=('NWC', 'WIO', 'NWC'),
        feature_group_count=c)
    return out + bias.astype(x.dtype)

def ssd_mixer(z, xbc, dt_raw, conv_w, conv_b, dt_bias, a_log, d_skip, norm_w):
    f32 = jnp.float32
    b, l, _ = z.shape
    nc, C = l // SSD_CHUNK, SSD_CHUNK
    G, J, P, N = SSD_GROUPS, SSD_HEADS // SSD_GROUPS, SSD_HEAD_DIM, SSD_STATE
    xbc = jax.nn.silu(causal_depthwise_conv(xbc.astype(f32), conv_w, conv_b))
    xs = xbc[..., :SSD_WIDTH]
    Bm = xbc[..., SSD_WIDTH:SSD_WIDTH + SSD_BC_WIDTH].reshape(b, nc, C, G, N)
    Cm = xbc[..., SSD_WIDTH + SSD_BC_WIDTH:].reshape(b, nc, C, G, N)
    X = xs.reshape(b, nc, C, G, J, P)
    dt = jax.nn.softplus(dt_raw.astype(f32) + dt_bias.astype(f32)).reshape(b, nc, C, G, J)
    A = -jnp.exp(a_log.astype(f32)).reshape(G, J)
    a = dt * A
    a_cum = jnp.cumsum(a, axis=2)
    seg = a_cum[:, :, :, None] - a_cum[:, :, None]
    causal = jnp.tril(jnp.ones((C, C), dtype=bool))[:, :, None, None]
    Lmat = jnp.exp(jnp.where(causal, seg, -jnp.inf))
    Xdt = X * dt[..., None]
    scores = jnp.einsum('bclgn,bcsgn->bclsg', Cm, Bm)
    y_diag = jnp.einsum('bclsg,bclsgj,bcsgjp->bclgjp', scores, Lmat, Xdt)
    decay_to_end = jnp.exp(a_cum[:, :, -1:] - a_cum)
    states = jnp.einsum('bclgn,bclgj,bclgjp->bcgjpn', Bm, decay_to_end, Xdt)
    chunk_decay = jnp.exp(a_cum[:, :, -1])

    def step(S, inp):
        dec, st = inp
        return dec[..., None, None] * S + st, S

    S0 = jnp.zeros((b, G, J, P, N), f32)
    _, S_prev = lax.scan(step, S0, (jnp.moveaxis(chunk_decay, 1, 0),
                                    jnp.moveaxis(states, 1, 0)))
    S_prev = jnp.moveaxis(S_prev, 0, 1)
    y_off = jnp.einsum('bclgn,bcgjpn,bclgj->bclgjp', Cm, S_prev, jnp.exp(a_cum))
    y = y_diag + y_off + X * d_skip.astype(f32).reshape(G, J)[..., None]
    y = y.reshape(b, l, SSD_WIDTH) * jax.nn.silu(z.astype(f32))
    y = y.reshape(b, l, G, SSD_WIDTH // G)
    y = y * lax.rsqrt(jnp.mean(y * y, axis=-1, keepdims=True) + EPS)
    return y.reshape(b, l, SSD_WIDTH) * norm_w.astype(f32)

def peer_ffn(xn, w_query, sub_keys, u, v):
    f32 = jnp.float32
    b, l, d = xn.shape
    T = b * l
    H, K = PEER_HEADS, PEER_TOPK
    xt = xn.reshape(T, d).astype(u.dtype)
    q = (xt @ w_query).reshape(T, H, 2, PEER_HALF)
    s = jnp.einsum('thpd,hpkd->thpk', q, sub_keys).astype(f32)
    top_s, top_i = lax.top_k(s, K)
    cand_s = (top_s[:, :, 0, :, None] + top_s[:, :, 1, None, :]).reshape(T, H, K * K)
    cand_i = (top_i[:, :, 0, :, None] * PEER_KEYS + top_i[:, :, 1, None, :]).reshape(T, H, K * K)
    best_s, best_pos = lax.top_k(cand_s, K)
    expert_idx = jnp.take_along_axis(cand_i, best_pos, axis=-1)
    gate = jax.nn.softmax(best_s, axis=-1)
    nb = T // PEER_BLOCK
    xb = xt.reshape(nb, PEER_BLOCK, d)
    ib = expert_idx.reshape(nb, PEER_BLOCK, H * K)
    gb = gate.reshape(nb, PEER_BLOCK, H * K)

    def block(args):
        x_blk, i_blk, g_blk = args
        act = jnp.einsum('td,ted->te', x_blk, u[i_blk]).astype(f32)
        hid = jax.nn.gelu(act, approximate=False) * g_blk
        return jnp.einsum('te,ted->td', hid.astype(v.dtype), v[i_blk])

    out = lax.map(block, (xb, ib, gb))
    return out.reshape(b, l, d)

def first_inputs(seed: int = 0) -> dict:
    key = jax.random.key(seed)
    ks = jax.random.split(key, 24)
    f32 = jnp.float32
    nrm = lambda k, shape, scale: jax.random.normal(k, shape, f32) * scale
    dt0 = jnp.exp(jax.random.uniform(ks[10], (DEPTH, SSD_HEADS), f32,
                                     math.log(1e-3), math.log(1e-1)))
    return {
        "x": jax.random.normal(ks[0], (BATCH, SEQ, D_MODEL), f32),
        "norm_mix_w": 1.0 + nrm(ks[1], (DEPTH, D_MODEL), 0.02),
        "w_in": nrm(ks[2], (DEPTH, D_MODEL, IN_TOTAL), D_MODEL ** -0.5),
        "gla_w_gate2": nrm(ks[3], (DEPTH, GLA_GATE_RANK, GLA_QK_WIDTH), GLA_GATE_RANK ** -0.5),
        "gla_b_gate": nrm(ks[4], (DEPTH, GLA_QK_WIDTH), 0.1),
        "gla_norm_w": 1.0 + nrm(ks[5], (DEPTH, GLA_DV), 0.02),
        "ssd_conv_w": nrm(ks[6], (DEPTH, SSD_CONV, SSD_CONV_DIM), SSD_CONV ** -0.5),
        "ssd_conv_b": nrm(ks[7], (DEPTH, SSD_CONV_DIM), 0.02),
        "ssd_dt_bias": dt0 + jnp.log(-jnp.expm1(-dt0)),
        "ssd_a_log": jnp.log(jax.random.uniform(ks[8], (DEPTH, SSD_HEADS), f32, 1.0, 16.0)),
        "ssd_d": 1.0 + nrm(ks[9], (DEPTH, SSD_HEADS), 0.1),
        "ssd_norm_w": 1.0 + nrm(ks[11], (DEPTH, SSD_WIDTH), 0.02),
        "w_out": nrm(ks[12], (DEPTH, D_MIX, D_MODEL), D_MIX ** -0.5),
        "norm_ffn_w": 1.0 + nrm(ks[13], (DEPTH, D_MODEL), 0.02),
        "peer_w_query": nrm(ks[14], (DEPTH, D_MODEL, PEER_HEADS * PEER_DQ), D_MODEL ** -0.5),
        "peer_sub_keys": nrm(ks[15], (DEPTH, PEER_HEADS, 2, PEER_KEYS, PEER_HALF), PEER_HALF ** -0.5),
        "peer_u": nrm(ks[16], (DEPTH, PEER_EXPERTS, D_MODEL), D_MODEL ** -0.5),
        "peer_v": nrm(ks[17], (DEPTH, PEER_EXPERTS, D_MODEL), PEER_HEADS ** -0.5),
        "norm_final_w": 1.0 + nrm(ks[18], (D_MODEL,), 0.02),
    }

def first_block(x, norm_mix_w, w_in, gla_w_gate2, gla_b_gate, gla_norm_w,
              ssd_conv_w, ssd_conv_b, ssd_dt_bias, ssd_a_log, ssd_d, ssd_norm_w,
              w_out, norm_ffn_w, peer_w_query, peer_sub_keys, peer_u, peer_v,
              norm_final_w):
    h = x
    for i in range(DEPTH):
        n = rmsnorm(h, norm_mix_w[i]).astype(w_in.dtype)
        proj = n @ w_in[i]
        q, k, v, gate_lr, g_out, z, xbc, dt_raw = split_cols(proj)
        o_gla = gla_mixer(q, k, v, gate_lr, g_out, gla_w_gate2[i], gla_b_gate[i], gla_norm_w[i])
        o_ssd = ssd_mixer(z, xbc, dt_raw, ssd_conv_w[i], ssd_conv_b[i], ssd_dt_bias[i],
                          ssd_a_log[i], ssd_d[i], ssd_norm_w[i])
        mixed = jnp.concatenate([o_gla, o_ssd], axis=-1).astype(w_out.dtype)
        h = h + (mixed @ w_out[i]).astype(h.dtype)
        n2 = rmsnorm(h, norm_ffn_w[i])
        h = h + peer_ffn(n2, peer_w_query[i], peer_sub_keys[i], peer_u[i], peer_v[i]).astype(h.dtype)
    return rmsnorm(h, norm_final_w).astype(x.dtype)


DEPTH_2 = 2

CHUNK = 64
N_A_LAYERS = DEPTH_2 // 2
N_B_LAYERS = DEPTH_2 - N_A_LAYERS
GMLP_BLOCK = 128
GMLP_WIDTH = D_MODEL
GMLP_GROUPS = 8
GMLP_GROUP_DIM = GMLP_WIDTH // GMLP_GROUPS
ATTN_HEADS = 16
HEAD_DIM = D_MODEL // ATTN_HEADS
LEFT_CHUNKS = 8
BAND_CHUNKS = LEFT_CHUNKS + 1
BAND = BAND_CHUNKS * CHUNK
REL_CLIP = 256
FFN_HIDDEN = 4 * D_MODEL
RMS_EPS = 1e-6
LN_EPS = 1e-5
NEG_INF = -1e30


def rms_norm(x, g):
    xf = x.astype(jnp.float32)
    y = xf * lax.rsqrt(jnp.mean(xf * xf, axis=-1, keepdims=True) + RMS_EPS)
    return (y * g.astype(jnp.float32)).astype(x.dtype)

def layer_norm(x, g, b):
    xf = x.astype(jnp.float32)
    mu = jnp.mean(xf, axis=-1, keepdims=True)
    xc = xf - mu
    var = jnp.mean(xc * xc, axis=-1, keepdims=True)
    y = xc * lax.rsqrt(var + LN_EPS) * g.astype(jnp.float32) + b.astype(jnp.float32)
    return y.astype(x.dtype)

def gmlp_spatial_gating(h, w_in, ln_g, ln_b, w_s, b_s, w_out):
    bsz, seq, _ = h.shape
    nblk = seq // GMLP_BLOCK
    uv = jax.nn.gelu(h @ w_in)
    u, v = jnp.split(uv, 2, axis=-1)
    v = layer_norm(v, ln_g, ln_b)
    v = v.reshape(bsz, nblk, GMLP_BLOCK, GMLP_GROUPS, GMLP_GROUP_DIM)
    chunk_id = jnp.arange(GMLP_BLOCK) // CHUNK
    mask = chunk_id[:, None] >= chunk_id[None, :]
    w_masked = jnp.where(mask[None], w_s, jnp.zeros((), w_s.dtype))
    sv = jnp.einsum('gij,bnjgd->bnigd', w_masked, v)
    sv = sv + jnp.transpose(b_s)[None, None, :, :, None]
    gate = sv.reshape(bsz, seq, GMLP_WIDTH)
    return (u * gate) @ w_out

def shared_kv_band(h, kv_norm_g, w_k, w_v):
    bsz, seq, _ = h.shape
    nc = seq // CHUNK
    hn = rms_norm(h, kv_norm_g)
    k = (hn @ w_k).reshape(bsz, nc, CHUNK, ATTN_HEADS, HEAD_DIM)
    v = (hn @ w_v).reshape(bsz, nc, CHUNK, ATTN_HEADS, HEAD_DIM)

    def band(t):
        tp = jnp.pad(t, ((0, 0), (LEFT_CHUNKS, 0), (0, 0), (0, 0), (0, 0)))
        tb = jnp.stack([tp[:, o:o + nc] for o in range(BAND_CHUNKS)], axis=2)
        return tb.reshape(bsz, nc, BAND, ATTN_HEADS, HEAD_DIM)

    key_chunk = jnp.arange(nc)[:, None] + jnp.arange(BAND_CHUNKS)[None, :] - LEFT_CHUNKS
    valid = jnp.repeat(key_chunk >= 0, CHUNK, axis=1)
    return band(k), band(v), valid

def relative_bias(table):
    q_pos = jnp.arange(CHUNK)[:, None] + LEFT_CHUNKS * CHUNK
    k_pos = jnp.arange(BAND)[None, :]
    idx = jnp.clip(q_pos - k_pos, -REL_CLIP, REL_CLIP) + REL_CLIP
    return table[:, idx]

def chunk_band_attention(h, w_q, rel_table, w_o, k_band, v_band, valid):
    bsz, seq, _ = h.shape
    nc = seq // CHUNK
    q = (h @ w_q).reshape(bsz, nc, CHUNK, ATTN_HEADS, HEAD_DIM)
    s = jnp.einsum('bcqhd,bckhd->bchqk', q, k_band).astype(jnp.float32)
    s = s * (HEAD_DIM ** -0.5) + relative_bias(rel_table).astype(jnp.float32)[None, None]
    s = jnp.where(valid[None, :, None, None, :], s, NEG_INF)
    p = jax.nn.softmax(s, axis=-1).astype(h.dtype)
    o = jnp.einsum('bchqk,bckhd->bcqhd', p, v_band).reshape(bsz, seq, D_MODEL)
    return o @ w_o

def sq_relu_mlp(h, w_up, w_down):
    return jnp.square(jax.nn.relu(h @ w_up)) @ w_down

def second_inputs(seed: int = 0) -> dict:
    key = jax.random.key(seed)
    ks = jax.random.split(key, 16)
    nrm = jax.random.normal
    D, W, G, H = D_MODEL, GMLP_WIDTH, GMLP_GROUPS, ATTN_HEADS
    return {
        "x": nrm(ks[0], (BATCH, SEQ, D), jnp.float32),
        "norm_g": 1.0 + 0.1 * nrm(ks[1], (DEPTH_2, 4, D), jnp.float32),
        "a_w_in": nrm(ks[2], (N_A_LAYERS, D, 2 * W), jnp.float32) * D ** -0.5,
        "a_ln_g": 1.0 + 0.1 * nrm(ks[3], (N_A_LAYERS, W), jnp.float32),
        "a_ln_b": 0.02 * nrm(ks[4], (N_A_LAYERS, W), jnp.float32),
        "a_w_s": nrm(ks[5], (N_A_LAYERS, G, GMLP_BLOCK, GMLP_BLOCK), jnp.float32) * GMLP_BLOCK ** -0.5,
        "a_b_s": 1.0 + 0.1 * nrm(ks[6], (N_A_LAYERS, G, GMLP_BLOCK), jnp.float32),
        "a_w_out": nrm(ks[7], (N_A_LAYERS, W, D), jnp.float32) * W ** -0.5,
        "kv_norm_g": 1.0 + 0.1 * nrm(ks[8], (D,), jnp.float32),
        "w_k": nrm(ks[9], (D, D), jnp.float32) * D ** -0.5,
        "w_v": nrm(ks[10], (D, D), jnp.float32) * D ** -0.5,
        "b_w_q": nrm(ks[11], (N_B_LAYERS, D, D), jnp.float32) * D ** -0.5,
        "b_rel_bias": 0.5 * nrm(ks[12], (N_B_LAYERS, H, 2 * REL_CLIP + 1), jnp.float32),
        "b_w_o": nrm(ks[13], (N_B_LAYERS, D, D), jnp.float32) * D ** -0.5,
        "w_up": nrm(ks[14], (DEPTH_2, D, FFN_HIDDEN), jnp.float32) * D ** -0.5,
        "w_down": nrm(ks[15], (DEPTH_2, FFN_HIDDEN, D), jnp.float32) * FFN_HIDDEN ** -0.5,
    }

def second_block(x, norm_g, a_w_in, a_ln_g, a_ln_b, a_w_s, a_b_s, a_w_out,
              kv_norm_g, w_k, w_v, b_w_q, b_rel_bias, b_w_o, w_up, w_down):
    h = x
    k_band = v_band = valid = None
    for layer in range(DEPTH_2):
        g = norm_g[layer]
        if layer < N_A_LAYERS:
            m = gmlp_spatial_gating(rms_norm(h, g[0]), a_w_in[layer], a_ln_g[layer],
                                    a_ln_b[layer], a_w_s[layer], a_b_s[layer], a_w_out[layer])
        else:
            if layer == N_A_LAYERS:
                k_band, v_band, valid = shared_kv_band(h, kv_norm_g, w_k, w_v)
            j = layer - N_A_LAYERS
            m = chunk_band_attention(rms_norm(h, g[0]), b_w_q[j], b_rel_bias[j], b_w_o[j],
                                     k_band, v_band, valid)
        h = h + rms_norm(m, g[1])
        f = sq_relu_mlp(rms_norm(h, g[2]), w_up[layer], w_down[layer])
        h = h + rms_norm(f, g[3])
    return h


def setup_inputs(seed=0):
    out = dict(first_inputs(seed))
    for name, value in second_inputs(seed + 1).items():
        if name != "x":
            out[name + "_2"] = value
    return out


def reference(
    x, norm_mix_w, w_in, gla_w_gate2, gla_b_gate, gla_norm_w, ssd_conv_w, ssd_conv_b,
    ssd_dt_bias, ssd_a_log, ssd_d, ssd_norm_w, w_out, norm_ffn_w, peer_w_query, peer_sub_keys,
    peer_u, peer_v, norm_final_w, norm_g_2, a_w_in_2, a_ln_g_2, a_ln_b_2, a_w_s_2, a_b_s_2,
    a_w_out_2, kv_norm_g_2, w_k_2, w_v_2, b_w_q_2, b_rel_bias_2, b_w_o_2, w_up_2, w_down_2,
):
    x = first_block(
        x, norm_mix_w, w_in, gla_w_gate2, gla_b_gate, gla_norm_w, ssd_conv_w, ssd_conv_b,
        ssd_dt_bias, ssd_a_log, ssd_d, ssd_norm_w, w_out, norm_ffn_w, peer_w_query,
        peer_sub_keys, peer_u, peer_v, norm_final_w,
    )
    return second_block(
        x, norm_g_2, a_w_in_2, a_ln_g_2, a_ln_b_2, a_w_s_2, a_b_s_2, a_w_out_2, kv_norm_g_2,
        w_k_2, w_v_2, b_w_q_2, b_rel_bias_2, b_w_o_2, w_up_2, w_down_2,
    )


_drawn_inputs = setup_inputs


def setup_inputs(seed=0):
    import zlib

    import numpy as np

    out = dict(_drawn_inputs(seed))
    spreads = {}
    factors = {'gla_norm_w': 3.313,
     'a_ln_b_2': 6.16,
     'ssd_conv_b': 3.333,
     'ssd_norm_w': 4.134,
     'norm_ffn_w': 3.382}
    for name, (base, spread) in spreads.items():
        noise = np.random.default_rng([zlib.crc32(name.encode()), seed]).standard_normal(out[name].shape)
        drawn = base * np.exp(spread * noise) if base else spread * noise
        out[name] = jnp.asarray(drawn.astype(out[name].dtype))
    for name, factor in factors.items():
        out[name] = (out[name] * factor).astype(out[name].dtype)
    return out
```

```python
import numpy as np
import concourse.bass as bass
from concourse import mybir
from contextlib import ExitStack

F32 = mybir.dt.float32
F32R = mybir.dt.float32r
I32 = mybir.dt.int32
U32 = mybir.dt.uint32
ALU = mybir.AluOpType
ACT = mybir.ActivationFunctionType
AX = mybir.AxisListType

T = 512
WR = 4
EPS = 1e-6
LN_EPS = 1e-5
NEG = -3.0e38

COLS = {}
_n = 0
for _name, _k in (("mix", 8), ("ffn", 8), ("fin", 8), ("g2", 64), ("kv", 8), ("glab", 2), ("glan", 1),
                  ("cw", 24), ("cb", 6), ("dskip", 4), ("ssdn", 4), ("dtb", 1), ("alog", 1)):
    COLS[_name] = _n
    _n += _k
NVEC = _n


class Lane:

    def __init__(self, sem):
        self.sem, self.count, self.items = sem, 0, []

    def put(self, fns, after, sem=None, by=1):
        if sem is None:
            self.count += 1
            token = (self.sem, self.count)
        else:
            token = None
        self.items.append((fns, after, sem or self.sem, by))
        return token

    def emit(self, eng):
        seen = {}
        for fns, after, sem, by in self.items:
            for s, v in after:
                if seen.get(s.name, 0) < v:
                    seen[s.name] = v
                    eng.wait_ge(s, v)
            for fn in fns[:-1]:
                fn(eng)
            last = fns[-1]
            if last is not None:
                last(eng).then_inc(sem, by)


class Ring:

    def __init__(self, bufs):
        self.bufs, self.free, self.at = bufs, [[] for _ in bufs], 0

    def take(self):
        i = self.at % len(self.bufs)
        self.at += 1
        return i, self.bufs[i], list(self.free[i])

    def release(self, i, *tokens):
        self.free[i] = list(tokens)


def build_program(nc, A, out):
    ctx = ExitStack()

    def sb(name, shape, dt=F32, scope=None):
        return (scope or ctx).enter_context(nc.sbuf_tensor(name, shape, dt))

    def sem(name):
        return ctx.enter_context(nc.semaphore(name))

    pe_l, act_l, dve_l, pool_l, sp_l = (Lane(sem(n)) for n in ("s_pe", "s_act", "s_dve", "s_pool", "s_sp"))

    def pe(fns, *after):
        return pe_l.put(fns if isinstance(fns, list) else [fns], after)

    def act(fn, *after):
        return act_l.put([fn], after)

    def dve(fn, *after):
        return dve_l.put([fn], after)

    after_part = []

    def pool(fn, *after):
        t = pool_l.put([fn], (*after, *after_part))
        after_part.clear()
        return t

    def pool_part(fn, *after):
        t = pool(fn, *after, (pool_l.sem, pool_l.count))
        after_part.append(t)
        return t

    dma_counts = {}

    def dma(dst, src, s, *after, lane=None):
        (lane or sp_l).put([lambda e: e.dma_start(dst, src)], after, sem=s, by=16)
        dma_counts[s.name] = dma_counts.get(s.name, 0) + 16
        return s, dma_counts[s.name]

    def lasts():
        return [(l.sem, l.count) for l in (pe_l, act_l, dve_l, pool_l) if l.count]

    gA = nc.dram_tensor("gA_scratch", (128, 128, T), F32, kind="Internal").ap()
    gG = nc.dram_tensor("gG_scratch", (128, 128, T), F32, kind="Internal").ap()

    hT = sb("hT", [128, 8, T])
    Xh = sb("Xh", [128, 8, T], F32R)
    Xl = sb("Xl", [128, 8, T], F32R)
    wraw = sb("wraw", [128, 4, 1024])
    wh = sb("wh", [128, WR, 1024], F32R)
    wl = sb("wl", [128, WR, 1024], F32R)
    tmpb = sb("tmpb", [128, 4, T])
    sqb = sb("sqb", [128, 2, T])
    sqacc = sb("sqacc", [128, T])
    rs = sb("rs", [128, T])
    stdb = sb("stdb", [128, T])
    ident = sb("ident", [128, 128])
    ones = sb("ones", [128, 128])
    iota = sb("iota", [128, 128])
    vec = sb("vec", [128, NVEC])
    ps = [ctx.enter_context(nc.psum_tensor(f"ps{i}", [128, T], F32)) for i in range(8)]

    def col(name, i=0, lo=0, hi=128):
        c = COLS[name] + i
        return vec[lo:hi, c:c + 1]

    tmp = Ring([tmpb[:, i, :] for i in range(4)])
    sq = Ring([sqb[:, i, :] for i in range(2)])
    banks = Ring(ps)

    s_in = sem("s_in")
    d_vec = dma(vec[:, :], A["vec"], s_in)
    c0 = pool(lambda e: e.memset(ident[:, :], 0.0))
    c_ident = pool(lambda e: e.affine_select(out=ident[:, :], in_=ident[:, :], compare_op=ALU.not_equal, fill=1.0,
                                             base=0, pattern=[[-1, 128]], channel_multiplier=1), c0)
    c_ones = pool(lambda e: e.memset(ones[:, :], 1.0))
    c_iota = pool(lambda e: e.iota(iota[:, :], [[1, 128]], base=0, channel_multiplier=0,
                                   allow_small_or_imprecise_dtypes=True))
    s_x = sem("s_x")
    xt = A["xT"].rearrange("(c p) t -> p c t", p=128)
    d_x = dma(hT[:, :, :], xt, s_x)

    wsem = [sem(f"s_w{i}") for i in range(4)]
    tiles = []
    for name in ("w_in", "w_out", "w_q", "uT"):
        tiles += [A[name][i, :, :] for i in range(A[name].shape[0])]
    v3 = A["v"].rearrange("(a b) d -> a b d", b=128)
    tiles += [v3[:, i, :] for i in range(128)]
    for name in ("a_in", "a_out", "up0", "w_k", "w_v2", "w_q2", "w_o2", "up1"):
        tiles += [A[name][i, :, :] for i in range(A[name].shape[0])]
    raw_ready, w_ready, w_used = {}, {}, {}
    state = {"dma": 0, "split": 0, "use": 0}

    def load_tile():
        n = state["dma"]
        if n < len(tiles):
            after = w_ready.get(n - 4, ())
            raw_ready[n] = dma(wraw[:, n % 4, :], tiles[n], wsem[n % 4], *after)
            state["dma"] += 1

    def split_tile():
        n = state["split"]
        if n >= len(tiles):
            return
        r, s = n % 4, n % WR
        free = w_used.get(n - WR, ())
        th = act(lambda e: e.activation(wh[:, s, :], wraw[:, r, :], ACT.Copy), raw_ready[n], *free)
        tl = pool(lambda e: e.tensor_tensor(wl[:, s, :], wraw[:, r, :], wh[:, s, :].bitcast(F32), ALU.subtract),
                  raw_ready[n], th, *free)
        w_ready[n] = (th, tl)
        state["split"] += 1
        load_tile()

    def next_tile():
        n = state["use"]
        state["use"] += 1
        return n, n % WR, w_ready[n]

    def tile_used(n, token):
        w_used[n] = (token,)
        split_tile()

    for _ in range(4):
        load_tile()
    for _ in range(WR):
        split_tile()

    def three(o, ah, al, bh, bl, start, stop):
        return [lambda e: e.matmul(o, ah, bh, start=start, stop=False),
                lambda e: e.matmul(o, ah, bl, start=False, stop=False),
                lambda e: e.matmul(o, al, bh, start=False, stop=stop)]

    def linear(m_tiles, ready, evac, tiles_each=1, xh=None, xl=None, kcs=8, side=None):
        xh, xl = xh or Xh, xl or Xl
        last = None
        for m in range(m_tiles):
            b, bank, free = banks.take()
            for q in range(tiles_each):
                n, s, wtok = next_tile()
                per = kcs // tiles_each
                for k in range(per):
                    kc = q * per + k
                    o = bank[:, :]
                    mm = three(o, wh[:, s, k * 128:(k + 1) * 128], wl[:, s, k * 128:(k + 1) * 128],
                               xh[:, kc, :], xl[:, kc, :], kc == 0, kc == kcs - 1)
                    last = pe(mm, *wtok, *free, *ready[kc])
                tile_used(n, last)
            banks.release(b, *evac(m, bank, last))
            if side is not None:
                side(m)
        return last

    def linear_tok(ntiles, ready, evac):
        last = None
        for half in range(ntiles // 4):
            bs = [banks.take() for _ in range(4)]
            for q in range(4):
                n, s, wtok = next_tile()
                for k in range(2):
                    kc = 2 * q + k
                    for tc in range(4):
                        mm = three(bs[tc][1][:, :], Xh[:, kc, tc * 128:(tc + 1) * 128],
                                   Xl[:, kc, tc * 128:(tc + 1) * 128], wh[:, s, k * 512:(k + 1) * 512],
                                   wl[:, s, k * 512:(k + 1) * 512], kc == 0, kc == 7)
                        last = pe(mm, *wtok, *bs[tc][2], *ready[kc])
                tile_used(n, last)
            for tc in range(4):
                banks.release(bs[tc][0], *evac(half, tc, bs[tc][1], last))
        return last

    def split_x(c, src, tok, after, use_pool):
        th = act(lambda e: e.activation(Xh[:, c, :], src, ACT.Copy), tok, *after)
        eng = pool if use_pool else dve
        tl = eng(lambda e: e.tensor_tensor(Xl[:, c, :], src, Xh[:, c, :].bitcast(F32), ALU.subtract), th, tok, *after)
        return th, tl

    rs_free = []

    def inv_rms(chunks, scale, acc_ready=None):
        nonlocal rs_free
        t_acc = None
        if len(chunks) == 1:
            src, toks = chunks[0]
            t_acc = act(lambda e: e.activation(sqacc[:, :], src, ACT.Square), *toks, *rs_free)
        else:
            for i, (src, toks) in enumerate(chunks):
                j, buf, free = sq.take()
                ts = act(lambda e, b=buf, s=src: e.activation(b, s, ACT.Square), *toks, *free)
                if i == 0:
                    t_acc = dve(lambda e, b=buf: e.tensor_copy(sqacc[:, :], b), ts, *rs_free)
                else:
                    t_acc = dve(lambda e, b=buf: e.tensor_tensor(sqacc[:, :], sqacc[:, :], b, ALU.add), ts, t_acc)
                sq.release(j, t_acc)
        b, bank, free = banks.take()
        tm = pe(lambda e: e.matmul(bank[:, :], ones[:, :], sqacc[:, :], start=True, stop=True), t_acc, c_ones, *free)
        tq = act(lambda e: e.activation(stdb[:, :], bank[:, :], ACT.Sqrt, bias=epsc[:, 0:1], scale=scale),
                 tm, c_eps, *rs_free)
        banks.release(b, tq)
        tr = dve(lambda e: e.reciprocal(rs[:, :], stdb[:, :]), tq, *rs_free)
        rs_free = [tr]
        return tr

    epsc = sb("epsc", [128, 1])
    c_eps = pool(lambda e: e.memset(epsc[:, :], EPS))

    def norm_split(src, toks, w, i0, tr, after):
        nonlocal rs_free
        ready = []
        for c in range(8):
            j, buf, free = tmp.take()
            t = dve(lambda e, b=buf, c=c: e.scalar_tensor_tensor(out=b, in0=src[:, c, :], scalar=col(w, i0 + c),
                                                                 in1=rs[:, :], op0=ALU.mult, op1=ALU.mult),
                    tr, d_vec, *toks[c], *free)
            r = split_x(c, buf, t, after, c % 2 == 0)
            tmp.release(j, *r)
            ready.append(r)
            last = t
        rs_free = [last]
        return ready

    def norm(src, toks, w, i0, after):
        tr = inv_rms([(src[:, c, :], toks[c]) for c in range(8)], 1.0 / 1024)
        return norm_split(src, toks, w, i0, tr, after)

    def add_norm(m, mtoks, w, i0, htoks):
        nonlocal rs_free
        tr = inv_rms([(m[:, c, :], mtoks[c]) for c in range(8)], 1.0 / 1024)
        new = []
        for c in range(8):
            t = dve(lambda e, c=c: e.scalar_tensor_tensor(out=m[:, c, :], in0=m[:, c, :], scalar=col(w, i0 + c),
                                                          in1=rs[:, :], op0=ALU.mult, op1=ALU.mult), tr, *mtoks[c])
            t2 = pool(lambda e, c=c: e.tensor_tensor(hT[:, c, :], hT[:, c, :], m[:, c, :], ALU.add), t, *htoks[c])
            new.append((t2,))
            last = t
        rs_free = [last]
        return new

    htoks = [(d_x,)] * 8
    ready = norm(hT, htoks, "mix", 0, [])

    s_c = sem("s_c")
    mixer = ExitStack()
    xs = sb("xs", [128, 6, T], scope=mixer)
    zs = sb("zs", [128, 4, T], scope=mixer)
    misc = sb("misc", [128, T], scope=mixer)
    gla = ExitStack()
    xp = sb("xp", [128, 2, T + 4], scope=gla)
    cacc = sb("cacc", [128, 2, T], scope=gla)
    qT = sb("qT", [128, 2, T], scope=gla)
    kT = sb("kT", [128, 2, T], scope=gla)
    vt = sb("vt", [128, 4, T], scope=gla)
    gs = sb("gs", [128, 4, T], scope=gla)
    w2 = sb("w2", [128, 256], scope=gla)
    d_w2 = dma(w2[32:48, :], A["w_gate2"], s_c)
    xpr = Ring([xp[:, i, :] for i in range(2)])
    car = Ring([cacc[:, i, :] for i in range(2)])
    t_xp0 = dve(lambda e: e.memset(xp[:, :, 0:4], 0.0))

    xs_tok, z_tok, q_tok, k_tok, g_tok, v_tok = {}, {}, {}, {}, {}, {}
    misc_tok = []

    def evac_in(m, bank, tok):
        if m == 0:
            misc_tok.append(act(lambda e: e.activation(misc[:, :], bank[:, :], ACT.Copy), tok))
            return misc_tok
        if m < 7:
            c = m - 1
            i, buf, free = xpr.take()
            t = act(lambda e: e.activation(buf[:, 3:3 + T], bank[:, :], ACT.Copy), tok, t_xp0, *free)
            j, acc, free2 = car.take()
            t1 = dve(lambda e: e.tensor_scalar(acc, buf[:, 0:T], col("cw", c), None, ALU.mult), t, d_vec, *free2)
            for k in range(1, 4):
                t1 = dve(lambda e, k=k: e.scalar_tensor_tensor(out=acc, in0=buf[:, k:k + T],
                                                               scalar=col("cw", 6 * k + c), in1=acc,
                                                               op0=ALU.mult, op1=ALU.add), t1)
            xpr.release(i, t1)
            xs_tok[c] = act(lambda e: e.activation(xs[:, c, :], acc, ACT.Silu, bias=col("cb", c)), t1, d_vec)
            car.release(j, xs_tok[c])
            return [t]
        if m < 11:
            z_tok[m - 7] = act(lambda e: e.activation(zs[:, m - 7, :], bank[:, :], ACT.Silu), tok)
            return [z_tok[m - 7]]
        if m < 13:
            q_tok[m - 11] = act(lambda e: e.activation(qT[:, m - 11, :], bank[:, :], ACT.Copy), tok)
            return [q_tok[m - 11]]
        if m < 15:
            k_tok[m - 13] = act(lambda e: e.activation(kT[:, m - 13, :], bank[:, :], ACT.Copy), tok)
            return [k_tok[m - 13]]
        g_tok[m - 15] = act(lambda e: e.activation(gs[:, m - 15, :], bank[:, :], ACT.Silu), tok)
        return [g_tok[m - 15]]

    linear(19, ready, evac_in)

    def evac_v(half, tc, bank, tok):
        v_tok[tc] = dve(lambda e: e.tensor_copy(vt[:, tc, :], bank[:, :]), tok)
        return [v_tok[tc]]

    x_free = linear_tok(4, ready, evac_v)

    Gc = sb("Gc", [128, 2, T], scope=gla)
    eG = sb("eG", [128, 2, T], scope=gla)
    kin = sb("kin", [128, 2, T], scope=gla)
    kend = sb("kend", [128, 2, T], scope=gla)
    kendt = sb("kendt", [128, 4, 256], scope=gla)
    Sg = sb("Sg", [128, 2, 8, 128], scope=gla)
    att = sb("att", [128, 4, 128], scope=gla)
    rst = sb("rst", [128, T], scope=gla)
    gmask = sb("gmask", [128, 128], I32, scope=gla)
    gmf = sb("gmf", [128, 128], scope=gla)

    m0 = pool(lambda e: e.memset(gmf[:, :], 1.0))
    m1 = pool(lambda e: e.affine_select(out=gmf[:, :], in_=gmf[:, :], compare_op=ALU.is_ge, fill=0.0, base=0,
                                        pattern=[[1, 128]], channel_multiplier=-1), m0)
    m2 = pool_part(lambda e: e.memset(gmf[0:64, 64:128], 0.0), m1)
    t_gm = pool(lambda e: e.tensor_copy(gmask[:, :], gmf[:, :]), m2)
    m3 = pool(lambda e: e.memset(rst[:, :], 1.0))
    t_rst = pool(lambda e: e.memset(rst[:, :].rearrange("p (c i) -> p c i", i=64)[:, :, 0:1], 0.0), m3)
    t_att0 = pool(lambda e: e.memset(att[:, :, :], 0.0))
    t_S0 = pool(lambda e: e.memset(Sg[:, :, 0, :], 0.0))

    qin_tok, kin_tok, kend_tok, dec_tok = {}, {}, {}, {}
    for m in range(2):
        b, bank, free = banks.take()
        t = pe(lambda e, m=m, bank=bank: e.matmul(bank[:, :], w2[32:48, m * 128:(m + 1) * 128], misc[32:48, :],
                                                  start=True, stop=True), d_w2, misc_tok[0], *free)
        ja, ya, fa = tmp.take()
        t = act(lambda e, bank=bank, ya=ya, m=m: e.activation(ya, bank[:, :], ACT.Identity, bias=col("glab", m)),
                t, d_vec, *fa)
        banks.release(b, t)
        jb, yb, fb = tmp.take()
        t2 = act(lambda e, ya=ya, yb=yb: e.activation(yb, ya, ACT.Abs), t, *fb)
        t2 = act(lambda e, yb=yb: e.activation(yb, yb, ACT.Exp, scale=-1.0), t2)
        t2 = act(lambda e, yb=yb: e.activation(yb, yb, ACT.Ln, bias=1.0), t2)
        t3 = dve(lambda e, ya=ya, yb=yb: e.scalar_tensor_tensor(out=ya, in0=ya, scalar=0.0, in1=yb, op0=ALU.min,
                                                                op1=ALU.subtract), t2)
        t4 = dve(lambda e, ya=ya, m=m: e.tensor_tensor_scan(Gc[:, m, :], rst[:, :], ya, 0.0, ALU.mult, ALU.add),
                 t3, t_rst)
        tmp.release(ja, t4)
        tmp.release(jb, t3)
        g3 = Gc[:, m, :].rearrange("p (c i) -> p c i", i=64)
        t5 = act(lambda e, m=m: e.activation(eG[:, m, :], Gc[:, m, :], ACT.Exp, scale=1.0 / 16), t4)
        dec_tok[m] = t5
        qin_tok[m] = dve(lambda e, m=m: e.scalar_tensor_tensor(out=qT[:, m, :], in0=qT[:, m, :], scalar=0.125,
                                                               in1=eG[:, m, :], op0=ALU.mult, op1=ALU.mult),
                         t5, q_tok[m])
        t6 = act(lambda e, m=m: e.activation(kin[:, m, :], Gc[:, m, :], ACT.Exp, scale=-1.0 / 16), t4)
        kin_tok[m] = dve(lambda e, m=m: e.tensor_tensor(kin[:, m, :], kin[:, m, :], kT[:, m, :], ALU.mult),
                         t6, k_tok[m])
        ke3 = kend[:, m, :].rearrange("p (c i) -> p c i", i=64)
        t7 = dve(lambda e, ke3=ke3, g3=g3: e.tensor_tensor(ke3, g3[:, :, 63:64].to_broadcast([128, 8, 64]), g3,
                                                           ALU.subtract), t4)
        t7 = act(lambda e, m=m: e.activation(kend[:, m, :], kend[:, m, :], ACT.Exp, scale=1.0 / 16), t7)
        kend_tok[m] = dve(lambda e, m=m: e.tensor_tensor(kend[:, m, :], kend[:, m, :], kT[:, m, :], ALU.mult),
                          t7, k_tok[m])
    kt_tok = {}
    for tc in range(4):
        b, bank, free = banks.take()
        t = pe([lambda e, m=m, tc=tc, bank=bank: e.transpose(bank[:, m * 128:(m + 1) * 128],
                                                             kend[:, m, tc * 128:(tc + 1) * 128], ident[:, :])
                for m in range(2)], kend_tok[0], kend_tok[1], c_ident, *free)
        kt_tok[tc] = act(lambda e, tc=tc, bank=bank: e.activation(kendt[:, tc, :], bank[:, 0:256], ACT.Copy), t)
        banks.release(b, kt_tok[tc])
    s_tok = {(m, 0): t_S0 for m in range(2)}
    for c in range(7):
        tc, r = c // 2, 64 * (c % 2)
        for m in range(2):
            b, bank, free = banks.take()
            t = pe(lambda e, tc=tc, r=r, m=m, bank=bank: e.matmul(
                bank[:, 0:256], kendt[r:r + 64, tc, m * 128:(m + 1) * 128], vt[r:r + 64, tc, m * 256:(m + 1) * 256],
                start=True, stop=True), kt_tok[tc], v_tok[tc], *free)
            for p in range(2):
                q = dve(lambda e, p=p, m=m, c=c, bank=bank: e.scalar_tensor_tensor(
                    out=Sg[64 * p:64 * p + 64, m, c + 1, :], in0=Sg[64 * p:64 * p + 64, m, c, :],
                    scalar=eG[64 * p:64 * p + 64, m, 64 * c + 63:64 * c + 64],
                    in1=bank[64 * p:64 * p + 64, 128 * p:128 * p + 128], op0=ALU.mult, op1=ALU.add),
                    t, s_tok[m, c], dec_tok[m])
            s_tok[m, c + 1] = q
            banks.release(b, q)

    mix_ready = {}
    attr = Ring([att[:, i, :] for i in range(4)])
    for h in range(4):
        m, r = h // 2, 64 * (h % 2)
        bo, obank, ofree = banks.take()
        ts = []
        for tc in range(4):
            b, bank, free = banks.take()
            cols = slice(tc * 128, tc * 128 + 128)
            t = pe(lambda e, m=m, r=r, cols=cols, bank=bank: e.matmul(
                bank[:, 0:128], kin[r:r + 64, m, cols], qT[r:r + 64, m, cols], start=True, stop=True),
                kin_tok[m], qin_tok[m], *free)
            j, ab, af = attr.take()
            t = dve(lambda e, ab=ab, bank=bank: e.copy_predicated(ab, gmask[:, :], bank[:, 0:128]),
                    t, t_gm, t_att0, *af)
            banks.release(b, t)
            fns = [lambda e, tc=tc, h=h, ab=ab, cols=cols, obank=obank: e.matmul(
                obank[:, cols], vt[:, tc, h * 128:(h + 1) * 128], ab, start=True, stop=False)]
            for i in range(2):
                c = 2 * tc + i
                cc = slice(c * 64, c * 64 + 64)
                fns.append(lambda e, c=c, cc=cc, m=m, r=r, i=i, obank=obank: e.matmul(
                    obank[:, cc], Sg[r:r + 64, m, c, :], qT[r:r + 64, m, cc], start=False, stop=(i == 1)))
            t = pe(fns, t, v_tok[tc], s_tok[m, 2 * tc + 1], *ofree)
            attr.release(j, t)
            ts.append(t)
        tr = inv_rms([(obank[:, :], (ts[-1],))], 1.0 / 128)
        ja, ya, fa = tmp.take()
        t1 = dve(lambda e, obank=obank, ya=ya: e.scalar_tensor_tensor(
            out=ya, in0=obank[:, :], scalar=col("glan"), in1=rs[:, :], op0=ALU.mult, op1=ALU.mult),
            tr, d_vec, *fa)
        rs_free = [t1]
        banks.release(bo, t1)
        t2 = dve(lambda e, ya=ya, h=h: e.tensor_tensor(ya, ya, gs[:, h, :], ALU.mult), t1, g_tok[h])
        mix_ready[h] = split_x(h, ya, t2, [x_free], True)
        tmp.release(ja, *mix_ready[h])
    fence = lasts()
    gla.close()

    ssd = ExitStack()
    acB = sb("acB", [128, 8, T], scope=ssd)
    ead = sb("ead", [128, 4, 8], scope=ssd)
    sel = sb("sel", [8, 8, 128], scope=ssd)
    acT_ = sb("acT", [8, T], scope=ssd)
    rs8 = sb("rs8", [8, T], scope=ssd)
    ea1 = sb("ea1", [8, 1], scope=ssd)
    dtt = sb("dtt", [128, 4, 8], scope=ssd)
    act_ = sb("actok", [128, 4, 8], scope=ssd)
    dte = sb("dte", [128, 4, 8], scope=ssd)
    Bt = sb("Bt", [128, 4, 128], scope=ssd)
    Xd = sb("Xd", [128, 4, T], scope=ssd)
    Xw = sb("Xw", [128, 3, T], scope=ssd)
    Ss = sb("Ss", [128, 4, 256], scope=ssd)
    scm = sb("scm", [128, 2, T], scope=ssd)
    tri = sb("tri", [128, 128], scope=ssd)
    LT = sb("LT", [128, 2, T], scope=ssd)
    CE = sb("CE", [128, 2, T], scope=ssd)

    p0 = pool_part(lambda e: e.memset(sel[:, :, :], 0.0), *fence)
    t_sel = pool_part(lambda e: e.affine_select(out=sel[:, :, :], in_=sel[:, :, :], compare_op=ALU.not_equal, fill=1.0,
                                           base=0, pattern=[[-1, 8], [0, 128]], channel_multiplier=1), p0)
    p1 = pool(lambda e: e.memset(tri[:, :], 1.0))
    t_tri = pool(lambda e: e.affine_select(out=tri[:, :], in_=tri[:, :], compare_op=ALU.is_ge, fill=0.0, base=0,
                                           pattern=[[1, 128]], channel_multiplier=-1), p1)
    p2 = pool_part(lambda e: e.memset(rs8[:, :], 1.0))
    t_rs8 = pool_part(lambda e: e.memset(rs8[:, :].rearrange("p (c i) -> p c i", i=128)[:, :, 0:1], 0.0), p2)

    scratch = [tmp.take() for _ in range(3)]
    y, acT = misc[0:8, :], acT_[:, :]
    z, lnz, u1 = (x[1][0:8, :] for x in scratch)
    t = dve(lambda e: e.tensor_scalar(y, misc[0:8, :], col("dtb", 0, 0, 8), None, ALU.add),
            misc_tok[0], d_vec, *fence, *[x for q in scratch for x in q[2]])
    t1 = act(lambda e: e.activation(z, y, ACT.Abs), t)
    t1 = act(lambda e: e.activation(z, z, ACT.Exp, scale=-1.0), t1, *fence)
    t2 = dve(lambda e: e.tensor_scalar(u1, z, 1.0, None, ALU.add), t1)
    t3 = act(lambda e: e.activation(lnz, u1, ACT.Ln), t2)
    t3b = act(lambda e: e.activation(ea1[:, :], col("alog", 0, 0, 8), ACT.Exp), d_vec)
    t4 = dve(lambda e: e.scalar_tensor_tensor(out=z, in0=u1, scalar=-1.0, in1=z, op0=ALU.add, op1=ALU.subtract), t2)
    t5 = dve(lambda e: e.reciprocal(u1, u1), t4, t3)
    t5 = dve(lambda e: e.tensor_tensor(z, z, u1, ALU.mult), t5)
    t5 = dve(lambda e: e.tensor_tensor(lnz, lnz, z, ALU.subtract), t5, t3)
    t_dt = dve(lambda e: e.scalar_tensor_tensor(out=y, in0=y, scalar=0.0, in1=lnz, op0=ALU.max, op1=ALU.add), t5)
    t6 = dve(lambda e: e.tensor_scalar(z, y, ea1[:, 0:1], -1.0, ALU.mult, ALU.mult), t_dt, t3b)
    t_ac = dve(lambda e: e.tensor_tensor_scan(acT, rs8[:, :], z, 0.0, ALU.mult, ALU.add), t6, t_rs8)
    for x in scratch:
        tmp.release(x[0], t_ac)
    b, bank, free = banks.take()
    fns = []
    for tc in range(4):
        for k, src in ((0, y), (1, acT)):
            fns.append(lambda e, tc=tc, k=k, src=src, bank=bank: e.transpose(
                bank[:, (tc * 2 + k) * 8:(tc * 2 + k) * 8 + 8], src[:, tc * 128:(tc + 1) * 128], ident[0:8, 0:8]))
    t = pe(fns, t_ac, c_ident, *free)
    bv = bank[:, 0:64].rearrange("p (c k h) -> p c k h", k=2, h=8)
    t_dtt = dve(lambda e: e.tensor_copy(dtt[:, :, :], bv[:, :, 0, :]), t)
    t_act = dve(lambda e: e.tensor_copy(act_[:, :, :], bv[:, :, 1, :]), t)
    banks.release(b, t_act)
    acB_tok = {}
    for h in range(8):
        b, bank, free = banks.take()
        t = pe(lambda e, h=h, bank=bank: e.matmul(bank[:, :], sel[:, h, :], acT, start=True, stop=True),
               t_ac, t_sel, *free)
        acB_tok[h] = dve(lambda e, h=h, bank=bank: e.tensor_copy(acB[:, h, :], bank[:, :]), t)
        banks.release(b, acB_tok[h])
    acl = acB[:, :, :].rearrange("p h (c i) -> p c h i", i=128)[:, :, :, 127]
    t_ead = act(lambda e: e.activation(ead[:, :, :], acl, ACT.Exp), acB_tok[7])
    t = dve(lambda e: e.tensor_tensor(dte[:, :, :], acl, act_[:, :, :], ALU.subtract), acB_tok[7], t_act)
    t_dte = act(lambda e: e.activation(dte[:, :, :], dte[:, :, :], ACT.Exp), t)
    xd_tok, xw_tok, bt_tok = {}, {}, {}
    for tc in range(4):
        cols = slice(tc * 128, tc * 128 + 128)
        b, bank, free = banks.take()
        t = pe([lambda e, m=m, cols=cols, bank=bank: e.transpose(bank[:, m * 128:(m + 1) * 128], xs[:, m, cols],
                                                                 ident[:, :]) for m in range(4)],
               *[xs_tok[m] for m in range(4)], *free)
        xd_tok[tc] = dve(lambda e, tc=tc, bank=bank: e.tensor_tensor(
            Xd[:, tc, :].rearrange("p (h d) -> p h d", d=64), bank[:, :].rearrange("p (h d) -> p h d", d=64),
            dtt[:, tc, :].unsqueeze(2).to_broadcast([128, 8, 64]), ALU.mult), t, t_dtt)
        banks.release(b, xd_tok[tc])
        if tc == 3:
            continue
        xw_tok[tc] = dve(lambda e, tc=tc: e.tensor_tensor(
            Xw[:, tc, :].rearrange("p (h d) -> p h d", d=64), Xd[:, tc, :].rearrange("p (h d) -> p h d", d=64),
            dte[:, tc, :].unsqueeze(2).to_broadcast([128, 8, 64]), ALU.mult), xd_tok[tc], t_dte)
        b, bank, free = banks.take()
        t = pe(lambda e, cols=cols, bank=bank: e.transpose(bank[:, 0:128], xs[:, 4, cols], ident[:, :]),
               xs_tok[4], *free)
        bt_tok[tc] = act(lambda e, tc=tc, bank=bank: e.activation(Bt[:, tc, :], bank[:, 0:128], ACT.Copy), t)
        banks.release(b, bt_tok[tc])
    ss_tok = {}
    for c in range(3):
        b, bank, free = banks.take()
        t = pe(lambda e, c=c, bank=bank: e.matmul(bank[:, :], Bt[:, c, :], Xw[:, c, :], start=True, stop=True),
               bt_tok[c], xw_tok[c], *free)
        for g in range(2):
            p = slice(64 * g, 64 * g + 64)
            if c == 0:
                q = dve(lambda e, g=g, p=p, bank=bank: e.tensor_copy(Ss[p, 1, :], bank[p, g * 256:(g + 1) * 256]), t)
                continue
            for j in range(4):
                hh = 4 * g + j
                q = dve(lambda e, g=g, p=p, j=j, hh=hh, c=c, bank=bank: e.scalar_tensor_tensor(
                    out=Ss[p, c + 1, j * 64:(j + 1) * 64], in0=Ss[p, c, j * 64:(j + 1) * 64],
                    scalar=ead[p, c, hh:hh + 1],
                    in1=bank[p, g * 256 + j * 64:g * 256 + (j + 1) * 64], op0=ALU.mult, op1=ALU.add),
                    t, ss_tok[c], t_ead)
        ss_tok[c + 1] = q
        banks.release(b, q)
    scm_tok = {}
    for g in range(2):
        p = slice(64 * g, 64 * g + 64)
        b, bank, free = banks.take()
        t = pe([lambda e, p=p, c=c, bank=bank: e.matmul(bank[:, c * 128:(c + 1) * 128], xs[p, 4, c * 128:(c + 1) * 128],
                                                        xs[p, 5, c * 128:(c + 1) * 128], start=True, stop=True)
                for c in range(4)], xs_tok[4], xs_tok[5], *free)
        scm_tok[g] = dve(lambda e, g=g, bank=bank: e.tensor_tensor(
            scm[:, g, :].rearrange("p (c i) -> p c i", i=128), bank[:, :].rearrange("p (c i) -> p c i", i=128),
            tri[:, :].unsqueeze(1).to_broadcast([128, 4, 128]), ALU.mult), t, t_tri)
        banks.release(b, scm_tok[g])
    ltr = Ring([LT[:, i, :] for i in range(2)])
    cer = Ring([CE[:, i, :] for i in range(2)])
    yz_tok = {}
    for m in range(4):
        bo, obank, ofree = banks.take()
        for hp in range(2):
            h = 2 * m + hp
            g = h // 4
            j = h % 4
            p = slice(64 * g, 64 * g + 64)
            op = slice(64 * hp, 64 * hp + 64)
            jl, lt, lf = ltr.take()
            t = None
            for c in range(4):
                cols = slice(c * 128, c * 128 + 128)
                t = dve(lambda e, lt=lt, cols=cols, h=h, c=c: e.tensor_scalar(
                    lt[:, cols], acB[:, h, cols], act_[:, c, h:h + 1], 0.0, ALU.subtract, ALU.min),
                    acB_tok[h], t_act, *lf)
            t = act(lambda e, lt=lt: e.activation(lt, lt, ACT.Exp), t)
            t_m = dve(lambda e, lt=lt, g=g: e.tensor_tensor(lt, lt, scm[:, g, :], ALU.mult), t, scm_tok[g])
            jc, ce, cf = cer.take()
            t_c = act(lambda e, ce=ce, p=p, h=h: e.activation(ce[p, :], acB[p, h, :], ACT.Exp), acB_tok[h], *cf)
            t_c = dve(lambda e, ce=ce, p=p: e.tensor_tensor(ce[p, :], ce[p, :], xs[p, 5, :], ALU.mult),
                      t_c, xs_tok[5])
            fns = []
            for c in range(4):
                cols = slice(c * 128, c * 128 + 128)
                fns.append(lambda e, c=c, cols=cols, h=h, op=op, lt=lt, obank=obank: e.matmul(
                    obank[op, cols], Xd[:, c, h * 64:(h + 1) * 64], lt[:, cols], start=True, stop=(c == 0)))
                if c:
                    fns.append(lambda e, c=c, cols=cols, j=j, op=op, p=p, ce=ce, obank=obank: e.matmul(
                        obank[op, cols], Ss[p, c, j * 64:(j + 1) * 64], ce[p, cols], start=False, stop=True))
            t = pe(fns, t_m, t_c, ss_tok[3], *xd_tok.values(), *ofree)
            ltr.release(jl, t)
            cer.release(jc, t)
        t1 = dve(lambda e, m=m, obank=obank: e.scalar_tensor_tensor(
            out=xs[:, m, :], in0=xs[:, m, :], scalar=col("dskip", m), in1=obank[:, :], op0=ALU.mult, op1=ALU.add), t)
        banks.release(bo, t1)
        yz_tok[m] = dve(lambda e, m=m: e.tensor_tensor(zs[:, m, :], zs[:, m, :], xs[:, m, :], ALU.mult),
                        t1, z_tok[m])
        if m % 2 == 1:
            tr = inv_rms([(zs[:, m - 1, :], (yz_tok[m - 1],)), (zs[:, m, :], (yz_tok[m],))], 1.0 / 256)
            for mm_ in (m - 1, m):
                ja, ya, fa = tmp.take()
                t2 = dve(lambda e, mm_=mm_, ya=ya: e.scalar_tensor_tensor(
                    out=ya, in0=zs[:, mm_, :], scalar=col("ssdn", mm_), in1=rs[:, :], op0=ALU.mult, op1=ALU.mult),
                    tr, *fa)
                rs_free = [t2]
                mix_ready[4 + mm_] = split_x(4 + mm_, ya, t2, [x_free], True)
                tmp.release(ja, *mix_ready[4 + mm_])
    fence = lasts()
    ssd.close()
    mixer.close()

    new = {}

    def evac_add(m, bank, tok):
        new[m] = (dve(lambda e: e.tensor_tensor(hT[:, m, :], hT[:, m, :], bank[:, :], ALU.add), tok, *htoks[m]),)
        return list(new[m])

    x_free = linear(8, [mix_ready[c] for c in range(8)], evac_add)
    htoks = [new[m] for m in range(8)]

    ready = norm(hT, htoks, "ffn", 0, [x_free])
    peer = ExitStack()
    iT = sb("iT", [128, 3, T], scope=peer)
    gl = sb("gl", [128, 4, T], scope=peer)
    top = ExitStack()
    qb = sb("qb", [128, 2, T], scope=top)
    kb = sb("kb", [128, 2, 128], scope=top)
    sS = sb("sS", [128, 3, T], scope=top)
    sR = sb("sR", [128, 4, 128], scope=top)
    tv = sb("tv", [128, 4, 16, 16], scope=top)
    ti = sb("ti", [128, 4, 16, 16], U32, scope=top)
    tif = sb("tif", [128, 2, 16, 16], scope=top)
    cand = sb("cand", [128, 2, 256], scope=top)
    cand2 = sb("cand2", [128, 2, 256], scope=top)
    bs_ = sb("bs_", [128, 4, 8, 16], scope=top)
    bp = sb("bp", [128, 4, 8, 16], U32, scope=top)
    bab = sb("bab", [128, 2, 128], U32, scope=top)
    baf = sb("baf", [128, 2, 128], scope=top)
    oh16 = sb("oh16", [128, 2, 2048], scope=top)
    slot = sb("slot", [128, 2, 3, 128], scope=top)
    den = sb("den", [128, 8], scope=top)

    qbr = Ring([qb[:, i, :] for i in range(2)])
    kbr = Ring([kb[:, i, :] for i in range(2)])
    ssr = Ring([sS[:, i, :] for i in range(3)])
    srr = Ring([sR[:, i, :] for i in range(4)])
    s_kb = [sem("s_kb0"), sem("s_kb1")]
    top_tok = {}

    pend = []

    def evac_q_late(m, bank, tok):
        i, qq, qf = qbr.take()
        t = act(lambda e: e.activation(qq, bank[:, :], ACT.Copy), tok, *qf, *fence)
        pend.append((m, i, qq, t))
        if len(pend) > 1:
            scores(*pend.pop(0))
        return [t]

    def scores(m, i, qq, t):
        jk, kk, kf = kbr.take()
        tk = dma(kk, A["keysT"][m, :, :], s_kb[jk], *kf, *fence)
        b2, bank2, f2 = banks.take()
        t2 = pe([lambda e, tc=tc: e.matmul(bank2[:, tc * 128:(tc + 1) * 128], qq[:, tc * 128:(tc + 1) * 128], kk,
                                           start=True, stop=True) for tc in range(4)], t, tk, *f2)
        qbr.release(i, t2)
        kbr.release(jk, t2)
        js, ss, sf = ssr.take()
        t3 = act(lambda e: e.activation(ss, bank2[:, :], ACT.Copy), t2, *sf)
        banks.release(b2, t3)
        for tc in range(4):
            src = ss[:, tc * 128:(tc + 1) * 128]
            a8, b8 = tv[:, tc, m, 0:8], tv[:, tc, m, 8:16]
            ta = dve(lambda e, a8=a8, src=src: e.max(a8, src), t3, *fence)
            dve(lambda e, a8=a8, src=src, tc=tc: e.max_index(ti[:, tc, m, 0:8], a8, src), ta)
            jr, rr, rf = srr.take()
            tb = dve(lambda e, a8=a8, src=src, rr=rr: e.match_replace(rr, a8, src, NEG), ta, *rf)
            tc2 = dve(lambda e, b8=b8, rr=rr: e.max(b8, rr), tb)
            td = dve(lambda e, b8=b8, rr=rr, tc=tc: e.max_index(ti[:, tc, m, 8:16], b8, rr), tc2)
            srr.release(jr, td)
            top_tok[m, tc] = td
        ssr.release(js, td)

    linear(16, ready, evac_q_late)
    scores(*pend.pop(0))

    it_tok = {}
    tfr = {}

    def second_dve(tc):
        k2 = tc % 2
        prev = tfr.get(tc - 2, [])
        t_if = dve(lambda e: e.tensor_copy(tif[:, k2, :, :], ti[:, tc, :, :]), top_tok[15, tc], *prev)
        for h in range(8):
            c3 = cand[:, h % 2, :].rearrange("p (a b) -> p a b", b=16)
            cf, c2 = cand[:, h % 2, :], cand2[:, h % 2, :]
            a8, b8 = bs_[:, tc, h, 0:8], bs_[:, tc, h, 8:16]
            t = dve(lambda e, c3=c3, h=h: e.tensor_tensor(
                c3, tv[:, tc, 2 * h, :].unsqueeze(2).to_broadcast([128, 16, 16]),
                tv[:, tc, 2 * h + 1, :].unsqueeze(1).to_broadcast([128, 16, 16]), ALU.add), top_tok[15, tc])
            ta = dve(lambda e, a8=a8, cf=cf: e.max(a8, cf), t)
            dve(lambda e, a8=a8, cf=cf, h=h: e.max_index(bp[:, tc, h, 0:8], a8, cf), ta)
            tb = dve(lambda e, a8=a8, cf=cf, c2=c2: e.match_replace(c2, a8, cf, NEG), ta)
            tb = dve(lambda e, b8=b8, c2=c2: e.max(b8, c2), tb)
            tb = dve(lambda e, b8=b8, c2=c2, h=h: e.max_index(bp[:, tc, h, 8:16], b8, c2), tb)
        bflat = bp[:, tc, :, :].rearrange("p h k -> p (h k)")
        t1 = dve(lambda e: e.tensor_scalar(bab[:, 0, :], bflat, 4, None, ALU.logical_shift_right), tb)
        t2 = dve(lambda e: e.tensor_scalar(bab[:, 1, :], bflat, 15, None, ALU.bitwise_and), tb)
        t3 = dve(lambda e: e.tensor_copy(baf[:, :, :], bab[:, :, :]), t1, t2)
        for w in range(2):
            o4 = oh16[:, w, :].rearrange("p (h k a) -> p h k a", k=16, a=16)
            o3 = oh16[:, w, :].rearrange("p (s a) -> p s a", a=16)
            ta = dve(lambda e, o3=o3, w=w: e.tensor_tensor(
                o3, baf[:, w, :].unsqueeze(2).to_broadcast([128, 128, 16]),
                iota[:, 0:16].unsqueeze(1).to_broadcast([128, 128, 16]), ALU.is_equal), t3, c_iota)
            last = None
            tg = dve(lambda e, o4=o4, w=w: e.tensor_tensor(
                o4, o4, tif[:, k2, w:16:2, :].unsqueeze(2).to_broadcast([128, 8, 16, 16]), ALU.mult), ta, t_if)
            last = dve(lambda e, o3=o3, w=w: e.tensor_reduce(slot[:, k2, w, :], o3, AX.X, ALU.add), tg)
        b3 = bs_[:, tc, :, :]
        t = dve(lambda e: e.tensor_tensor(slot[:, k2, 2, :].rearrange("p (h k) -> p h k", k=16), b3,
                                          b3[:, :, 0:1].to_broadcast([128, 8, 16]), ALU.subtract), tb, *prev)
        tfr[tc] = [last]
        return t, last

    def second_exp(tc, t, last):
        k2 = tc % 2
        g = slot[:, k2, 2, :]
        g3 = g.rearrange("p (h k) -> p h k", k=16)
        t = act(lambda e: e.activation(g, g, ACT.Exp), t)
        t = dve(lambda e: e.tensor_reduce(den[:, :], g3, AX.X, ALU.add), t)
        t = dve(lambda e: e.reciprocal(den[:, :], den[:, :]), t)
        t = dve(lambda e: e.tensor_tensor(g3, g3, den[:, :].unsqueeze(2).to_broadcast([128, 8, 16]), ALU.mult), t)
        return t, last

    def second_transpose(tc, t, last):
        k2 = tc % 2
        b, bank, free = banks.take()
        t = pe([lambda e, w=w: e.transpose(bank[:, w * 128:(w + 1) * 128], slot[:, k2, w, :], ident[:, :])
                for w in range(3)], t, last, *free)
        t = act(lambda e: e.activation(iT[:, :, tc * 128:(tc + 1) * 128],
                                       bank[:, 0:384].rearrange("p (w t) -> p w t", w=3), ACT.Copy), t)
        banks.release(b, t)
        tfr[tc] = [t]
        it_tok[tc] = t

    gsc = {}

    def gate_setup():
        top_fence = lasts()
        top.close()
        gsc["s"] = ExitStack()
        gsc["gb"] = sb("gbuf", [128, 128, 128], scope=gsc["s"])
        oh = sb("oh", [128, 4, 2, 128], scope=gsc["s"])
        gsc["oh"] = Ring([oh[:, i, :, :] for i in range(4)])
        gsc["fence"] = top_fence
        gsc["store"] = []
        gsc["sem"] = sem("s_g")

    def gate_four(t0):
        gb, ohr = gsc["gb"], gsc["oh"]
        tc, tl = t0 // 128, t0 % 128
        b, bank, free = banks.take()
        for k in range(4):
            j, o, of = ohr.take()
            tt = t0 + k
            ta = dve(lambda e, o=o, tt=tt: e.tensor_scalar(o[:, 0, :], iota[:, :], iT[:, 0, tt:tt + 1],
                                                           iT[:, 2, tt:tt + 1], ALU.is_equal, ALU.mult),
                     it_tok[tc], *of, *gsc["fence"])
            tb = dve(lambda e, o=o, tt=tt: e.tensor_scalar(o[:, 1, :], iota[:, :], iT[:, 1, tt:tt + 1], None,
                                                           ALU.is_equal), it_tok[tc], *of)
            t = pe(lambda e, o=o, k=k: e.matmul(bank[:, k * 128:(k + 1) * 128], o[:, 0, :], o[:, 1, :],
                                                start=True, stop=True), ta, tb, *free)
            ohr.release(j, t)
        t = act(lambda e: e.activation(gb[:, :, tl:tl + 4].rearrange("p i t -> p t i"),
                                       bank[:, :].rearrange("p (t i) -> p t i", t=4), ACT.Copy),
                t, *gsc["store"], *gsc["fence"])
        banks.release(b, t)
        return t

    s_ga = [sem(f"s_ga{i}") for i in range(4)]
    glr = Ring([gl[:, i, :] for i in range(4)])
    ga_store = {}
    gelu_pend = []

    def evac_u(m, bank, tok):
        i, g, gf = glr.take()
        t = act(lambda e: e.activation(g, bank[:, :], ACT.Gelu), tok, *gf, *fence)
        gelu_pend.append((m, i, g, t))
        if len(gelu_pend) > 1:
            store_u()
        return [t]

    def store_u():
        m, i, g, t = gelu_pend.pop(0)
        ga_store[m] = dma(gA[m, :, :], g, s_ga[i], t)
        glr.release(i, ga_store[m])

    plan = {}
    hold = {}
    for tc in range(4):
        plan.setdefault(2 + 5 * tc, []).append(("exp", tc))
        plan.setdefault(8 + 5 * tc, []).append(("tr", tc))
    for tc in range(4):
        for k in range(16):
            plan.setdefault(25 + 23 * tc + k, []).append(("gate", tc * 128 + k * 8))
        plan.setdefault(25 + 23 * tc + 16, []).append(("store", tc))
    for tc in range(4):
        hold[tc] = None
    gate_last = {}

    def side(m):
        for what, x in plan.get(m, ()):
            if what == "exp":
                hold[x] = second_exp(x, *second_dve(x))
            elif what == "tr":
                second_transpose(x, *hold[x])
                if x == 3:
                    gate_setup()
            elif what == "gate":
                gate_four(x)
                gate_last["t"] = gate_four(x + 4)
            else:
                gv = gG.rearrange("b a t -> a b t")[:, :, x * 128:(x + 1) * 128]
                gsc["store"] = [dma(gv, gsc["gb"][:, :, :], gsc["sem"], gate_last["t"])]

    x_free = linear(128, ready, evac_u, side=side)
    while gelu_pend:
        store_u()
    fence = lasts() + gsc["store"] + [ga_store[m] for m in range(124, 128)]
    gsc["s"].close()
    peer.close()

    pv = ExitStack()
    la = sb("la", [128, 4, T], scope=pv)
    lg = sb("lg", [128, 4, T], scope=pv)
    Hh = sb("Hh", [128, 3, T], F32R, scope=pv)
    Hl = sb("Hl", [128, 3, T], F32R, scope=pv)
    s_la = [sem(f"s_la{i}") for i in range(4)]
    h_used, h_ready, l_free, l_ready = {}, {}, {}, {}

    def load_h(m):
        i = m % 4
        dma(la[:, i, :], gA[m, :, :], s_la[i], *l_free.get(m - 4, ()), *fence)
        l_ready[m] = dma(lg[:, i, :], gG[m, :, :], s_la[i])

    def make_h(m):
        i, j = m % 4, m % 3
        t = dve(lambda e: e.tensor_tensor(la[:, i, :], la[:, i, :], lg[:, i, :], ALU.mult), l_ready[m])
        free = h_used.get(m - 3, ())
        th = act(lambda e: e.activation(Hh[:, j, :], la[:, i, :], ACT.Copy), t, *free, *fence)
        tl = dve(lambda e: e.tensor_tensor(Hl[:, j, :], la[:, i, :], Hh[:, j, :].bitcast(F32), ALU.subtract), th)
        h_ready[m] = (th, tl)
        l_free[m] = (th, tl)

    acc = [banks.take() for _ in range(8)]
    for m in range(4):
        load_h(m)
    for m in range(3):
        make_h(m)
        load_h(m + 4)
    for m in range(128):
        n, s, wtok = next_tile()
        j = m % 3
        for dc in range(8):
            cs = slice(dc * 128, dc * 128 + 128)
            t = pe(three(acc[dc][1][:, :], wh[:, s, cs], wl[:, s, cs], Hh[:, j, :], Hl[:, j, :], m == 0, m == 127),
                   *wtok, *h_ready[m], *acc[dc][2])
        h_used[m] = (t,)
        tile_used(n, t)
        if m + 3 < 128:
            make_h(m + 3)
            if m + 7 < 128:
                load_h(m + 7)
    for dc in range(8):
        new[dc] = (dve(lambda e, dc=dc: e.tensor_tensor(hT[:, dc, :], hT[:, dc, :], acc[dc][1][:, :], ALU.add),
                       t, *htoks[dc]),)
        banks.release(acc[dc][0], *new[dc])
    htoks = [new[m] for m in range(8)]
    fence = lasts()
    pv.close()

    tr = inv_rms([(hT[:, c, :], htoks[c]) for c in range(8)], 1.0 / 1024)
    for c in range(8):
        t = dve(lambda e, c=c: e.scalar_tensor_tensor(out=hT[:, c, :], in0=hT[:, c, :], scalar=col("fin", c),
                                                      in1=rs[:, :], op0=ALU.mult, op1=ALU.mult), tr)
        new[c] = (t,)
    rs_free = [t]
    htoks = [new[c] for c in range(8)]

    ready = norm(hT, htoks, "g2", 0, [x_free])
    ga = ExitStack()
    uT = sb("uTs", [128, 8, T], scope=ga)
    vn = sb("vn", [128, 4, 1024], scope=ga)
    mo = sb("mo", [128, 8, T], scope=ga)
    lngb = sb("lngb", [128, 3, 1024], scope=ga)
    wsT = sb("wsT", [128, 8, 128], scope=ga)
    st = sb("st", [128, 4, 2, 6], scope=ga)
    ag = sb("ag", [128, 4, 2], scope=ga)
    s_a = sem("s_a")
    dma(lngb[:, :, :], A["rows"], s_a, *fence)
    d_a = dma(wsT[:, :, :], A["wsT"], s_a, *fence)
    t_ws = pool_part(lambda e: e.memset(wsT[64:128, :, 0:64], 0.0), d_a)
    v_toks, u_tok = {}, {}

    def evac_vn(half, tc, bank, tok):
        t = act(lambda e: e.activation(vn[:, tc, half * 512:(half + 1) * 512], bank[:, :], ACT.Gelu_apprx_tanh),
                tok, *fence)
        v_toks[tc, half] = dve(lambda e: e.bn_stats(st[:, tc, half, :], vn[:, tc, half * 512:(half + 1) * 512]),
                               t, *fence)
        return [t]

    linear_tok(8, ready, evac_vn)

    def evac_u2(m, bank, tok):
        u_tok[m] = act(lambda e: e.activation(uT[:, m, :], bank[:, :], ACT.Gelu_apprx_tanh), tok)
        return [u_tok[m]]

    x_free = linear(8, ready, evac_u2)
    leps = sb("leps", [128, 1], scope=ga)
    c_leps = pool(lambda e: e.memset(leps[:, :], LN_EPS), *fence)
    vtok = {}
    for tc in range(4):
        t = dve(lambda e, tc=tc: e.bn_aggr(ag[:, tc, :], st[:, tc, :, :].rearrange("p a b -> p (a b)")),
                v_toks[tc, 0], v_toks[tc, 1])
        t = act(lambda e, tc=tc: e.activation(ag[:, tc, 1:2], ag[:, tc, 1:2], ACT.Sqrt, bias=leps[:, 0:1]), t, c_leps)
        t = dve(lambda e, tc=tc: e.reciprocal(ag[:, tc, 1:2], ag[:, tc, 1:2]), t)
        t = dve(lambda e, tc=tc: e.tensor_scalar(vn[:, tc, :], vn[:, tc, :], ag[:, tc, 0:1], ag[:, tc, 1:2],
                                                 ALU.subtract, ALU.mult), t)
        t = dve(lambda e, tc=tc: e.tensor_tensor(vn[:, tc, :], vn[:, tc, :], lngb[:, 0, :], ALU.mult), t, d_a)
        vtok[tc] = dve(lambda e, tc=tc: e.tensor_tensor(vn[:, tc, :], vn[:, tc, :], lngb[:, 1, :], ALU.add), t)
    ready = []
    for g in range(8):
        b, bank, free = banks.take()
        t = pe([lambda e, g=g, n=n, bank=bank: e.matmul(bank[:, n * 128:(n + 1) * 128],
                                                        vn[:, n, g * 128:(g + 1) * 128], wsT[:, g, :],
                                                        start=True, stop=True) for n in range(4)],
               *vtok.values(), t_ws, *free)
        ja, ya, fa = tmp.take()
        t = dve(lambda e, g=g, bank=bank, ya=ya: e.tensor_tensor(
            ya.rearrange("p (n i) -> p n i", i=128), bank[:, :].rearrange("p (n i) -> p n i", i=128),
            lngb[:, 2, g * 128:(g + 1) * 128].unsqueeze(1).to_broadcast([128, 4, 128]), ALU.add), t, d_a, *fa)
        banks.release(b, t)
        t = dve(lambda e, g=g, ya=ya: e.tensor_tensor(ya, ya, uT[:, g, :], ALU.mult), t, u_tok[g])
        r = split_x(g, ya, t, [x_free], g % 2 == 0)
        tmp.release(ja, *r)
        ready.append(r)
    mo_tok = {}

    def evac_mo(m, bank, tok):
        mo_tok[m] = (act(lambda e: e.activation(mo[:, m, :], bank[:, :], ACT.Copy), tok, *fence),)
        return list(mo_tok[m])

    x_free = linear(8, ready, evac_mo)
    htoks = add_norm(mo, mo_tok, "g2", 8, htoks)
    fence = lasts()
    ga.close()

    def ffn(layer, htoks, fence, x_free):
        ready = norm(hT, htoks, "g2", 32 * layer + 16, [x_free])
        sc = ExitStack()
        Fh = sb(f"Fh{layer}", [128, 16, T], F32R, scope=sc)
        Fl = sb(f"Fl{layer}", [128, 16, T], F32R, scope=sc)
        fo = sb(f"fo{layer}", [128, 8, T], scope=sc)
        f_free, toks = [], {}
        for half in range(2):
            fr = {}

            def evac_up(m, bank, tok):
                j, b, free = tmp.take()
                t = act(lambda e: e.activation(b, bank[:, :], ACT.Relu), tok, *free)
                t2 = dve(lambda e: e.tensor_tensor(b, b, b, ALU.mult), t)
                th = dve(lambda e: e.tensor_copy(Fh[:, m, :], b), t2, *fence, *f_free)
                tl = dve(lambda e: e.tensor_tensor(Fl[:, m, :], b, Fh[:, m, :].bitcast(F32), ALU.subtract), th)
                tmp.release(j, tl)
                fr[m] = (th, tl)
                return [t]

            x_free = linear(16, ready, evac_up)

            def evac_dn(m, bank, tok):
                if half == 0:
                    toks[m] = (act(lambda e: e.activation(fo[:, m, :], bank[:, :], ACT.Copy), tok, *fence),)
                else:
                    toks[m] = (dve(lambda e: e.tensor_tensor(fo[:, m, :], fo[:, m, :], bank[:, :], ALU.add),
                                   tok, *toks[m]),)
                return list(toks[m])

            f_free = [linear(8, [fr[m] for m in range(16)], evac_dn, tiles_each=2, xh=Fh, xl=Fl, kcs=16)]
        htoks = add_norm(fo, toks, "g2", 32 * layer + 24, htoks)
        fence = lasts()
        sc.close()
        return htoks, fence, x_free

    htoks, fence, x_free = ffn(0, htoks, fence, x_free)

    at = ExitStack()
    kTs = sb("kTs", [128, 8, T], scope=at)
    qTs = sb("qTs", [128, 8, T], scope=at)
    vs = sb("vs", [128, 4, 1024], scope=at)
    bias = sb("bias", [128, 2, T], scope=at)
    sc_ = sb("sc_", [128, 2, 1280], scope=at)
    pt = sb("pt", [128, 2, 1280], scope=at)
    mx = sb("mx", [128, 2, 3, 4], scope=at)

    tr = inv_rms([(hT[:, c, :], htoks[c]) for c in range(8)], 1.0 / 1024)
    ready = norm_split(hT, htoks, "kv", 0, tr, [x_free])
    kt, qt, vtk = {}, {}, {}

    def evac_k(m, bank, tok):
        kt[m] = act(lambda e: e.activation(kTs[:, m, :], bank[:, :], ACT.Copy), tok, *fence)
        return [kt[m]]

    linear(8, ready, evac_k)

    def evac_v2(half, tc, bank, tok):
        vtk[tc, half] = dve(lambda e: e.tensor_copy(vs[:, tc, half * 512:(half + 1) * 512], bank[:, :]), tok, *fence)
        return [vtk[tc, half]]

    x_free = linear_tok(8, ready, evac_v2)
    ready = norm_split(hT, htoks, "g2", 32, tr, [x_free])

    def evac_q2(m, bank, tok):
        qt[m] = act(lambda e: e.activation(qTs[:, m, :], bank[:, :], ACT.Copy, scale=0.125), tok, *fence)
        return [qt[m]]

    x_free = linear(8, ready, evac_q2)

    s_b = [sem("s_b0"), sem("s_b1")]
    OFF = [0, 128, 384, 768]
    JOF = [0, 512, 896, 1152]
    bias_free = {}
    bias_tok = {}

    def load_bias(h):
        i = h % 2
        t = dma(bias[:, i, :], A["relb"][h, :, :], s_b[i], *bias_free.get(h - 2, ()), *fence)
        bias_tok[h] = pool_part(lambda e: e.memset(bias[0:64, i, 448:512], -1e30), t)

    load_bias(0)
    load_bias(1)
    p_tok, pt_used, obk, ready = {}, {}, {}, [None] * 8

    def att_scores(h):
        i, m, r = h % 2, h // 2, 64 * (h % 2)
        b1, k1, f1 = banks.take()
        b2, k2, f2 = banks.take()
        b3, k3, f3 = banks.take()
        where = [(k1, 0), (k1, 128), (k2, 0), (k3, 0)]
        fns = []
        for I in range(4):
            bank, o = where[I]
            n = 128 * (I + 1)
            fns.append(lambda e, bank=bank, o=o, n=n, I=I: e.matmul(
                bank[:, o:o + n], qTs[r:r + 64, m, I * 128:(I + 1) * 128], kTs[r:r + 64, m, 0:n],
                start=True, stop=True))
        t = pe(fns, qt[m], kt[m], *f1, *f2, *f3)
        for I in range(4):
            bank, o = where[I]
            n = 128 * (I + 1)
            tt = dve(lambda e, bank=bank, o=o, n=n, I=I: e.tensor_tensor_reduce(
                out=sc_[:, i, OFF[I]:OFF[I] + n], in0=bank[:, o:o + n], in1=bias[:, i, 512 - n:512], scale=1.0,
                scalar=NEG, op0=ALU.add, op1=ALU.max, accum_out=mx[:, i, 0, I:I + 1]),
                t, bias_tok[h], *pt_used.get(h - 2, ()))
        banks.release(b1, tt)
        banks.release(b2, tt)
        banks.release(b3, tt)
        bias_free[h] = (tt,)
        if h + 2 < 16:
            load_bias(h + 2)
        tn = dve(lambda e: e.tensor_scalar(mx[:, i, 1, :], mx[:, i, 0, :], -1.0, None, ALU.mult), tt)
        for I in range(4):
            n = 128 * (I + 1)
            te = act(lambda e, n=n, I=I: e.activation(sc_[:, i, OFF[I]:OFF[I] + n], sc_[:, i, OFF[I]:OFF[I] + n],
                                                      ACT.Exp, bias=mx[:, i, 1, I:I + 1],
                                                      accum_out=mx[:, i, 2, I:I + 1]), tn)
        tr_ = dve(lambda e: e.reciprocal(mx[:, i, 2, :], mx[:, i, 2, :]), te)
        for I in range(4):
            n = 128 * (I + 1)
            tt = dve(lambda e, n=n, I=I: e.tensor_scalar(sc_[:, i, OFF[I]:OFF[I] + n], sc_[:, i, OFF[I]:OFF[I] + n],
                                                         mx[:, i, 2, I:I + 1], None, ALU.mult), tr_)
        p_tok[h] = tt

    def att_out(h):
        i, m, r = h % 2, h // 2, 64 * (h % 2)
        b1, k1, f1 = banks.take()
        b2, k2, f2 = banks.take()
        b3, k3, f3 = banks.take()
        where = [(k1, 0), (k2, 0), (k3, 0), (k2, 384)]
        fns = []
        for J in range(4):
            bank, o = where[J]
            for I in range(J, 4):
                fns.append(lambda e, bank=bank, o=o, I=I, J=J: e.transpose(
                    bank[:, o + (I - J) * 128:o + (I - J + 1) * 128],
                    sc_[:, i, OFF[I] + J * 128:OFF[I] + (J + 1) * 128], ident[:, :]))
        t = pe(fns, p_tok[h], *f1, *f2, *f3)
        pt_used[h] = (t,)
        te = []
        free = h_free.get(h - 2, ())
        te.append(act(lambda e: e.activation(pt[:, i, 0:512], k1[:, :], ACT.Copy), t, *free, *fence))
        te.append(dve(lambda e: e.tensor_copy(pt[:, i, 512:896], k2[:, 0:384]), t, *free, *fence))
        te.append(act(lambda e: e.activation(pt[:, i, 896:1152], k3[:, 0:256], ACT.Copy), t))
        te.append(dve(lambda e: e.tensor_copy(pt[:, i, 1152:1280], k2[:, 384:512]), t))
        banks.release(b1, te[0])
        banks.release(b2, te[3])
        banks.release(b3, te[2])
        if h % 2 == 0:
            obk[m] = banks.take()
        bo, ob, of = obk[m]
        t = pe([lambda e, J=J: e.matmul(ob[r:r + 64, J * 128:512], vs[:, J, h * 64:(h + 1) * 64],
                                        pt[:, i, JOF[J]:JOF[J] + 512 - 128 * J], start=(J == 0), stop=(J == 3))
                for J in range(4)], *te, *vtk.values(), *of)
        h_free[h] = (t,)
        if h % 2 == 1:
            ja, ya, fa = tmp.take()
            tc = dve(lambda e: e.tensor_copy(ya, ob[:, :]), t, *fa)
            banks.release(bo, tc)
            ready[m] = split_x(m, ya, tc, [x_free], True)
            tmp.release(ja, *ready[m])

    h_free = {}
    att_scores(0)
    for h in range(16):
        if h + 1 < 16:
            att_scores(h + 1)
        att_out(h)
    mo_tok = {}
    after_att = lasts()

    def evac_mo2(m, bank, tok):
        mo_tok[m] = (act(lambda e: e.activation(qTs[:, m, :], bank[:, :], ACT.Copy), tok, *after_att),)
        return list(mo_tok[m])

    x_free = linear(8, ready, evac_mo2)
    htoks = add_norm(qTs, mo_tok, "g2", 40, htoks)
    fence = lasts()
    at.close()

    htoks, fence, x_free = ffn(1, htoks, fence, x_free)

    s_out = sem("s_out")
    ov = out.rearrange("(c p) t -> p c t", p=128)
    d_out = dma(ov, hT[:, :, :], s_out, *[t for c in range(8) for t in htoks[c]])
    sp_l.items.append(([None], (d_out,), None, 0))

    block = ctx.enter_context(nc.Block())
    for reg, lane in ((block.sync, sp_l), (block.gpsimd, pool_l), (block.scalar, act_l), (block.vector, dve_l),
                      (block.tensor, pe_l)):
        def body(eng, lane=lane):
            lane.emit(eng)
        reg(body)
    ctx.close()


def _tiles(w):
    k, m = w.shape
    return np.ascontiguousarray(w.reshape(k // 128, 128, m // 128, 128).transpose(2, 1, 0, 3)).reshape(
        -1, 128, k)


def _tiles_tok(w):
    k, m = w.shape
    return np.ascontiguousarray(w.reshape(4, 2, 128, m // 512, 512).transpose(3, 0, 2, 1, 4)).reshape(-1, 128, 1024)


def _up_down(up, down):
    u = _tiles(up).reshape(2, 16, 128, 1024)
    d = [_tiles(down[i * 2048:(i + 1) * 2048]).reshape(8, 128, 2, 1024).transpose(0, 2, 1, 3).reshape(16, 128, 1024)
         for i in range(2)]
    return u, d


def _layout(v):
    a = {}
    a["xT"] = np.ascontiguousarray(v["x"][0].T)
    w = v["w_in"][0]
    at = np.cumsum([0, 256, 256, 512, 16, 512, 512, 768, 8])
    q, k, vv, gl, go, z, xbc, dt = (w[:, at[i]:at[i + 1]] for i in range(8))
    misc = np.zeros((1024, 128), np.float32)
    misc[:, 0:8] = dt
    misc[:, 32:48] = gl
    a["w_in"] = np.concatenate([_tiles(np.concatenate([misc, xbc, z, q, k, go], 1)), _tiles_tok(vv)], 0)
    a["w_out"] = _tiles(v["w_out"][0])
    a["w_q"] = _tiles(v["peer_w_query"][0])
    a["uT"] = np.ascontiguousarray(v["peer_u"][0].reshape(128, 128, 8, 128).transpose(1, 3, 2, 0)).reshape(
        128, 128, 1024)
    a["v"] = v["peer_v"][0]
    a["keysT"] = np.ascontiguousarray(v["peer_sub_keys"][0].reshape(16, 128, 128).transpose(0, 2, 1))
    a["w_gate2"] = v["gla_w_gate2"][0]
    wi = v["a_w_in_2"][0]
    a["a_in"] = np.concatenate([_tiles_tok(wi[:, 1024:]), _tiles(wi[:, :1024])], 0)
    a["a_out"] = _tiles(v["a_w_out_2"][0])
    for i in range(2):
        u, d = _up_down(v["w_up_2"][i], v["w_down_2"][i])
        a[f"up{i}"] = np.concatenate([u[0], d[0], u[1], d[1]], 0)
    a["w_k"] = _tiles(v["w_k_2"])
    a["w_v2"] = _tiles_tok(v["w_v_2"])
    a["w_q2"] = _tiles(v["b_w_q_2"][0])
    a["w_o2"] = _tiles(v["b_w_o_2"][0])
    a["wsT"] = np.ascontiguousarray(v["a_w_s_2"][0].transpose(2, 0, 1))
    rows = np.stack([v["a_ln_g_2"][0], v["a_ln_b_2"][0], v["a_b_s_2"][0].reshape(1024)], 0)
    a["rows"] = np.ascontiguousarray(np.broadcast_to(rows[None], (128, 3, 1024)))
    idx = np.clip(384 + np.arange(128)[:, None] - np.arange(512)[None, :], -256, 256) + 256
    a["relb"] = np.ascontiguousarray(v["b_rel_bias_2"][0][:, idx])

    def cols(x):
        return x.reshape(-1, 128).T

    pad = np.zeros((128, 2), np.float32)
    pad[0:8, 0] = v["ssd_dt_bias"][0]
    pad[0:8, 1] = v["ssd_a_log"][0]
    a["vec"] = np.ascontiguousarray(np.concatenate([
        cols(v["norm_mix_w"][0]), cols(v["norm_ffn_w"][0]), cols(v["norm_final_w"]), cols(v["norm_g_2"]),
        cols(v["kv_norm_g_2"]), cols(v["gla_b_gate"][0]), cols(v["gla_norm_w"][0]), cols(v["ssd_conv_w"][0]),
        cols(v["ssd_conv_b"][0]), cols(np.repeat(v["ssd_d"][0], 64)), cols(v["ssd_norm_w"][0]), pad], 1))
    return a


def kernel(**inputs):
    import concourse.bacc as _bacc
    from concourse.bass_utils import run_bass_kernel_spmd as _run

    nc = _bacc.Bacc("TRN2", target_bir_lowering=False, num_devices=1)
    laid = {k: v for k, v in _layout({k: np.asarray(v) for k, v in inputs.items()}).items() if v.size}
    arrays, aps = {}, {}
    for name, a in laid.items():
        arrays[f"in_{name}"] = a
        aps[name] = nc.dram_tensor(f"in_{name}", a.shape, F32, kind="ExternalInput").ap()
    out = nc.dram_tensor("out_T", (1024, T), F32, kind="ExternalOutput").ap()
    build_program(nc, aps, out)
    r = _run(nc, [arrays], core_ids=[0])
    return np.ascontiguousarray(r.results[0]["out_T"].T)[None]
```

```python
import numpy as np
import concourse.bass as bass
from concourse import mybir
from contextlib import ExitStack

F32 = mybir.dt.float32
F32R = mybir.dt.float32r
I32 = mybir.dt.int32
U32 = mybir.dt.uint32
ALU = mybir.AluOpType
ACT = mybir.ActivationFunctionType
AX = mybir.AxisListType

T = 512
WR = 4
EPS = 1e-6
LN_EPS = 1e-5
NEG = -3.0e38

COLS = {}
_n = 0
for _name, _k in (("mix", 8), ("ffn", 8), ("fin", 8), ("g2", 64), ("kv", 8), ("glab", 2), ("glan", 1),
                  ("cw", 24), ("cb", 6), ("dskip", 4), ("ssdn", 4), ("dtb", 1), ("alog", 1)):
    COLS[_name] = _n
    _n += _k
NVEC = _n


class Lane:

    def __init__(self, sem):
        self.sem, self.count, self.items = sem, 0, []

    def put(self, fns, after, sem=None, by=1):
        if sem is None:
            self.count += 1
            token = (self.sem, self.count)
        else:
            token = None
        self.items.append((fns, after, sem or self.sem, by))
        return token

    def emit(self, eng):
        seen = {}
        for fns, after, sem, by in self.items:
            for s, v in after:
                if seen.get(s.name, 0) < v:
                    seen[s.name] = v
                    eng.wait_ge(s, v)
            for fn in fns[:-1]:
                fn(eng)
            last = fns[-1]
            if last is not None:
                last(eng).then_inc(sem, by)


class Ring:

    def __init__(self, bufs):
        self.bufs, self.free, self.at = bufs, [[] for _ in bufs], 0

    def take(self):
        i = self.at % len(self.bufs)
        self.at += 1
        return i, self.bufs[i], list(self.free[i])

    def release(self, i, *tokens):
        self.free[i] = list(tokens)


def build_program(nc, A, out):
    ctx = ExitStack()

    def sb(name, shape, dt=F32, scope=None):
        return (scope or ctx).enter_context(nc.sbuf_tensor(name, shape, dt))

    def sem(name):
        return ctx.enter_context(nc.semaphore(name))

    pe_l, act_l, dve_l, pool_l, sp_l = (Lane(sem(n)) for n in ("s_pe", "s_act", "s_dve", "s_pool", "s_sp"))

    def pe(fns, *after):
        return pe_l.put(fns if isinstance(fns, list) else [fns], after)

    def act(fn, *after):
        return act_l.put([fn], after)

    def dve(fn, *after):
        return dve_l.put([fn], after)

    after_part = []

    def pool(fn, *after):
        t = pool_l.put([fn], (*after, *after_part))
        after_part.clear()
        return t

    def pool_part(fn, *after):
        t = pool(fn, *after, (pool_l.sem, pool_l.count))
        after_part.append(t)
        return t

    dma_counts = {}

    def dma(dst, src, s, *after, lane=None):
        (lane or sp_l).put([lambda e: e.dma_start(dst, src)], after, sem=s, by=16)
        dma_counts[s.name] = dma_counts.get(s.name, 0) + 16
        return s, dma_counts[s.name]

    def lasts():
        return [(l.sem, l.count) for l in (pe_l, act_l, dve_l, pool_l) if l.count]

    gA = nc.dram_tensor("gA_scratch", (128, 128, T), F32, kind="Internal").ap()
    gG = nc.dram_tensor("gG_scratch", (128, 128, T), F32, kind="Internal").ap()

    hT = sb("hT", [128, 8, T])
    Xh = sb("Xh", [128, 8, T], F32R)
    Xl = sb("Xl", [128, 8, T], F32R)
    wraw = sb("wraw", [128, 4, 1024])
    wh = sb("wh", [128, WR, 1024], F32R)
    wl = sb("wl", [128, WR, 1024], F32R)
    tmpb = sb("tmpb", [128, 4, T])
    sqb = sb("sqb", [128, 2, T])
    sqacc = sb("sqacc", [128, T])
    rsb = sb("rsb", [128, 3, T])
    rst4 = sb("rst4", [128, 3, 4])
    stdb = sb("stdb", [128, T])
    ident = sb("ident", [128, 128])
    ones = sb("ones", [128, 128])
    iota = sb("iota", [128, 128])
    vec = sb("vec", [128, NVEC])
    ps = [ctx.enter_context(nc.psum_tensor(f"ps{i}", [128, T], F32)) for i in range(8)]

    def col(name, i=0, lo=0, hi=128):
        c = COLS[name] + i
        return vec[lo:hi, c:c + 1]

    tmp = Ring([tmpb[:, i, :] for i in range(4)])
    sq = Ring([sqb[:, i, :] for i in range(2)])
    banks = Ring(ps)

    s_in = sem("s_in")
    d_vec = dma(vec[:, :], A["vec"], s_in)
    c0 = pool(lambda e: e.memset(ident[:, :], 0.0))
    c_ident = pool(lambda e: e.affine_select(out=ident[:, :], in_=ident[:, :], compare_op=ALU.not_equal, fill=1.0,
                                             base=0, pattern=[[-1, 128]], channel_multiplier=1), c0)
    c_ones = pool(lambda e: e.memset(ones[:, :], 1.0))
    c_iota = pool(lambda e: e.iota(iota[:, :], [[1, 128]], base=0, channel_multiplier=0,
                                   allow_small_or_imprecise_dtypes=True))
    xt = A["xT"].rearrange("(c p) t -> p c t", p=128)
    htoks = []
    for i in range(4):
        htoks += [(dma(hT[:, 2 * i:2 * i + 2, :], xt[:, 2 * i:2 * i + 2, :], sem(f"s_x{i}")),)] * 2

    wsem = [sem(f"s_w{i}") for i in range(4)]
    tiles = []
    for name in ("w_in", "w_out", "w_q", "uT"):
        tiles += [A[name][i, :, :] for i in range(A[name].shape[0])]
    v3 = A["v"].rearrange("(a b) d -> a b d", b=128)
    tiles += [v3[:, i, :] for i in range(128)]
    for name in ("a_in", "a_out", "up0", "w_k", "w_v2", "w_q2", "w_o2", "up1"):
        tiles += [A[name][i, :, :] for i in range(A[name].shape[0])]
    raw_ready, w_ready, w_used = {}, {}, {}
    state = {"dma": 0, "split": 0, "use": 0}

    def load_tile():
        n = state["dma"]
        if n < len(tiles):
            after = w_ready.get(n - 4, ())
            raw_ready[n] = dma(wraw[:, n % 4, :], tiles[n], wsem[n % 4], *after)
            state["dma"] += 1

    def split_tile():
        n = state["split"]
        if n >= len(tiles):
            return
        r, s = n % 4, n % WR
        free = w_used.get(n - WR, ())
        th = act(lambda e: e.activation(wh[:, s, :], wraw[:, r, :], ACT.Copy), raw_ready[n], *free)
        tl = pool(lambda e: e.tensor_tensor(wl[:, s, :], wraw[:, r, :], wh[:, s, :].bitcast(F32), ALU.subtract),
                  raw_ready[n], th, *free)
        w_ready[n] = (th, tl)
        state["split"] += 1
        load_tile()

    def next_tile():
        n = state["use"]
        state["use"] += 1
        return n, n % WR, w_ready[n]

    def tile_used(n, token):
        w_used[n] = (token,)
        split_tile()


    def three(o, ah, al, bh, bl, start, stop):
        return [lambda e: e.matmul(o, ah, bh, start=start, stop=False),
                lambda e: e.matmul(o, ah, bl, start=False, stop=False),
                lambda e: e.matmul(o, al, bh, start=False, stop=stop)]

    def linear(m_tiles, ready, evac, tiles_each=1, xh=None, xl=None, kcs=8, side=None, between=None, first=1, ring=None,
               late=None):
        xh, xl, ring = xh or Xh, xl or Xl, ring or banks
        m, last = 0, None
        while m < m_tiles:
            group = first if m == 0 else 1
            bs = [ring.take() for _ in range(group)]
            for q in range(tiles_each):
                ws = [next_tile() for _ in range(group)]
                per = kcs // tiles_each
                for k in range(per):
                    kc = q * per + k
                    for (b, bank, free), (n, s, wtok) in zip(bs, ws):
                        last = pe(three(bank[:, :], wh[:, s, k * 128:(k + 1) * 128], wl[:, s, k * 128:(k + 1) * 128],
                                        xh[:, kc, :], xl[:, kc, :], kc == 0, kc == kcs - 1),
                                  *wtok, *free, *ready[kc])
                        if k == per - 1:
                            tile_used(n, last)
                    if between is not None:
                        between()
            if m == 0 and late is not None:
                late()
            for i, (b, bank, free) in enumerate(bs):
                ring.release(b, *evac(m + i, bank, last))
                if side is not None:
                    side(m + i)
            m += group
        return last

    def linear_tok(ntiles, ready, evac, late=None):
        last = None
        for half in range(ntiles // 4):
            bs = [banks.take() for _ in range(4)]
            for q in range(4):
                n, s, wtok = next_tile()
                for k in range(2):
                    kc = 2 * q + k
                    for tc in range(4):
                        mm = three(bs[tc][1][:, :], Xh[:, kc, tc * 128:(tc + 1) * 128],
                                   Xl[:, kc, tc * 128:(tc + 1) * 128], wh[:, s, k * 512:(k + 1) * 512],
                                   wl[:, s, k * 512:(k + 1) * 512], kc == 0, kc == 7)
                        last = pe(mm, *wtok, *bs[tc][2], *ready[kc])
                tile_used(n, last)
            if half == 0 and late is not None:
                late()
            for tc in range(4):
                banks.release(bs[tc][0], *evac(half, tc, bs[tc][1], last))
        return last

    def split_x(c, src, tok, after, use_pool):
        th = act(lambda e: e.activation(Xh[:, c, :], src, ACT.Copy), tok, *after)
        eng = pool if use_pool else dve
        tl = eng(lambda e: e.tensor_tensor(Xl[:, c, :], src, Xh[:, c, :].bitcast(F32), ALU.subtract), th, tok, *after)
        return th, tl

    acc_free = []
    rs_used = [[], []]
    rs_count = [0]

    def sum_add(st, src, *toks):
        if not st:
            t = act(lambda e: e.activation(sqacc[:, :], src, ACT.Square), *toks, *acc_free)
            st.append(t)
            return t
        j, buf, free = sq.take()
        ts = act(lambda e: e.activation(buf, src, ACT.Square), *toks, *free)
        t = dve(lambda e: e.tensor_tensor(sqacc[:, :], sqacc[:, :], buf, ALU.add), ts, st[-1])
        sq.release(j, t)
        st.append(t)
        return ts

    def sum_done(st, scale, fixed=False, tokens=False):
        nonlocal acc_free
        i = 2 if fixed else rs_count[0] % 2
        used = [] if fixed else rs_used[i]
        rs = rsb[:, i, :]
        b, bank, free = banks.take()
        tm = pe(lambda e: e.matmul(bank[:, :], ones[:, :], sqacc[:, :], start=True, stop=True), st[-1], c_ones, *free)
        acc_free = [tm]
        tq = act(lambda e: e.activation(rs, bank[:, :], ACT.Sqrt, bias=epsc[:, 0:1], scale=scale), tm, c_eps, *used)
        banks.release(b, tq)
        tr = dve(lambda e: e.reciprocal(rs, rs), tq)
        tt = None
        if tokens:
            b, bank2, free = banks.take()
            tm = pe([lambda e, c=c: e.matmul(bank2[:, c:c + 1], sqacc[:, c * 128:(c + 1) * 128], ones[:, 0:1],
                                             start=True, stop=True) for c in range(4)], st[-1], *free)
            acc_free = [tm]
            tq = act(lambda e: e.activation(rst4[:, i, :], bank2[:, 0:4], ACT.Sqrt, bias=epsc[:, 0:1], scale=scale),
                     tm, *used)
            banks.release(b, tq)
            tt = dve(lambda e: e.reciprocal(rst4[:, i, :], rst4[:, i, :]), tq)
        if not fixed:
            rs_used[1 - i] = lasts()
            rs_count[0] += 1
        return rs, tr, rst4[:, i, :], tt

    RS, RS4, norm_tok = rsb[:, 2, :], rst4[:, 2, :], {}

    def stage_norm(st, tokens=False):
        def late():
            _, norm_tok["t"], _, norm_tok["t4"] = sum_done(st, 1.0 / 1024, fixed=True, tokens=tokens)
        return late

    epsc = sb("epsc", [128, 1])
    c_eps = pool(lambda e: e.memset(epsc[:, :], EPS))

    def fold(c, src, toks, w, i0, after):
        j, buf, free = tmp.take()
        t = dve(lambda e: e.tensor_scalar(buf, src[:, c, :], col(w, i0 + c), None, ALU.mult), d_vec, *toks, *free)
        r = split_x(c, buf, t, after, c > 0)
        tmp.release(j, *r)
        return r

    def norm_split(src, toks, w, i0, rs, tr, after):
        ready = []
        for c in range(8):
            j, buf, free = tmp.take()
            t = dve(lambda e, b=buf, c=c: e.scalar_tensor_tensor(out=b, in0=src[:, c, :], scalar=col(w, i0 + c),
                                                                 in1=rs, op0=ALU.mult, op1=ALU.mult),
                    tr, d_vec, *toks[c], *free)
            r = split_x(c, buf, t, after, c % 2 == 0)
            tmp.release(j, *r)
            ready.append(r)
        return ready

    def add_norm_fold(m, st, w, i0, htoks, after, w2=None, i2=0, tokens=False):
        rs, tr, _, _ = sum_done(st, 1.0 / 1024)
        new, ready = [], []
        for c in range(8):
            t = dve(lambda e, c=c: e.scalar_tensor_tensor(out=m[:, c, :], in0=m[:, c, :], scalar=col(w, i0 + c),
                                                          in1=rs, op0=ALU.mult, op1=ALU.mult), tr)
            t2 = dve(lambda e, c=c: e.tensor_tensor(hT[:, c, :], hT[:, c, :], m[:, c, :], ALU.add), t, *htoks[c])
            new.append((t2,))
            if w2 is not None:
                ready.append(fold(c, hT, new[c], w2, i2, after))
        st = []
        if w2 is not None:
            for c in range(8):
                sum_add(st, hT[:, c, :], *new[c])
        return new, ready, st

    for _ in range(4):
        load_tile()
    ready, st = [], []
    for c in range(8):
        ready.append(fold(c, hT, htoks[c], "mix", 0, []))
        if c % 2 == 0 and c < 4:
            split_tile()
    for _ in range(2):
        split_tile()
    for c in range(8):
        sum_add(st, hT[:, c, :], *htoks[c])

    s_c = sem("s_c")
    mixer = ExitStack()
    xs = sb("xs", [128, 6, T], scope=mixer)
    zs = sb("zs", [128, 4, T], scope=mixer)
    misc = sb("misc", [128, T], scope=mixer)
    gs = sb("gs", [128, 4, T], scope=mixer)
    gla = ExitStack()
    xp = sb("xp", [128, 2, T + 4], scope=gla)
    cacc = sb("cacc", [128, 2, T], scope=gla)
    qT = sb("qT", [128, 2, T], scope=gla)
    kT = sb("kT", [128, 2, T], scope=gla)
    vt = sb("vt", [128, 4, T], scope=gla)
    w2 = sb("w2", [128, 256], scope=gla)
    d_w2 = dma(w2[32:48, :], A["w_gate2"], s_c)
    xpr = Ring([xp[:, i, :] for i in range(2)])
    car = Ring([cacc[:, i, :] for i in range(2)])
    t_xp0 = dve(lambda e: e.memset(xp[:, :, 0:4], 0.0))

    xs_tok, z_tok, q_tok, k_tok, g_tok, v_tok = {}, {}, {}, {}, {}, {}
    misc_tok = []

    def scaled(dst, bank, tok, *after):
        return dve(lambda e: e.tensor_tensor(dst, bank[:, :], RS, ALU.mult), tok, norm_tok["t"], *after)

    def silu(dst, bank, tok):
        j, buf, free = tmp.take()
        t = scaled(buf, bank, tok, *free)
        t2 = act(lambda e: e.activation(dst, buf, ACT.Silu), t)
        tmp.release(j, t2)
        return t2, t

    def evac_in(m, bank, tok):
        if m == 0:
            misc_tok.append(scaled(misc[:, :], bank, tok))
            return misc_tok
        if m < 3:
            q_tok[m - 1] = scaled(qT[:, m - 1, :], bank, tok)
            return [q_tok[m - 1]]
        k_tok[m - 3] = scaled(kT[:, m - 3, :], bank, tok)
        return [k_tok[m - 3]]

    def evac_rest(m, bank, tok):
        if m < 6:
            c = m
            i, buf, free = xpr.take()
            t = scaled(buf[:, 3:3 + T], bank, tok, t_xp0, *free)
            j, acc, free2 = car.take()
            t1 = dve(lambda e: e.tensor_scalar(acc, buf[:, 0:T], col("cw", c), None, ALU.mult), t, d_vec, *free2)
            for k in range(1, 4):
                t1 = dve(lambda e, k=k: e.scalar_tensor_tensor(out=acc, in0=buf[:, k:k + T],
                                                               scalar=col("cw", 6 * k + c), in1=acc,
                                                               op0=ALU.mult, op1=ALU.add), t1)
            xpr.release(i, t1)
            xs_tok[c] = act(lambda e: e.activation(xs[:, c, :], acc, ACT.Silu, bias=col("cb", c)), t1, d_vec)
            car.release(j, xs_tok[c])
            return [t]
        if m < 10:
            g_tok[m - 6], t = silu(gs[:, m - 6, :], bank, tok)
            return [t]
        z_tok[m - 10], t = silu(zs[:, m - 10, :], bank, tok)
        return [t]

    linear(5, ready, evac_in, first=2, late=stage_norm(st, True))

    def evac_v(half, tc, bank, tok):
        v_tok[tc] = dve(lambda e: e.tensor_scalar(vt[:, tc, :], bank[:, :], RS4[:, tc:tc + 1], None, ALU.mult),
                        tok, norm_tok["t4"])
        return [v_tok[tc]]

    linear_tok(4, ready, evac_v)

    Gc = sb("Gc", [128, 2, T], scope=gla)
    eG = sb("eG", [128, 2, T], scope=gla)
    kin = sb("kin", [128, 2, T], scope=gla)
    kend = sb("kend", [128, 2, T], scope=gla)
    kendt = sb("kendt", [128, 4, 256], scope=gla)
    Sg = sb("Sg", [128, 2, 8, 128], scope=gla)
    rst = sb("rst", [128, T], scope=gla)
    gmask = sb("gmask", [128, 128], I32, scope=gla)
    gmf = kendt[:, 3, 0:128]

    m0 = pool(lambda e: e.memset(gmf, 1.0))
    m1 = pool(lambda e: e.affine_select(out=gmf, in_=gmf, compare_op=ALU.is_ge, fill=0.0, base=0,
                                        pattern=[[1, 128]], channel_multiplier=-1), m0)
    m2 = pool_part(lambda e: e.memset(kendt[0:64, 3, 64:128], 0.0), m1)
    t_gm = pool(lambda e: e.tensor_copy(gmask[:, :], gmf), m2)
    m3 = pool(lambda e: e.memset(rst[:, :], 1.0))
    t_rst = pool(lambda e: e.memset(rst[:, :].rearrange("p (c i) -> p c i", i=64)[:, :, 0:1], 0.0), m3)
    t_S0 = pool(lambda e: e.memset(Sg[:, :, 0, :], 0.0))

    qin_tok, kin_tok, kend_tok, dec_tok, kt_tok, s_tok, go_tok = {}, {}, {}, {}, {}, {}, {}

    def gla_steps():
        for m in range(2):
            b, bank, free = banks.take()
            t = pe(lambda e, m=m, bank=bank: e.matmul(bank[:, :], w2[32:48, m * 128:(m + 1) * 128], misc[32:48, :],
                                                      start=True, stop=True), d_w2, misc_tok[0], *free)
            ja, ya, fa = tmp.take()
            t = act(lambda e, bank=bank, ya=ya, m=m: e.activation(ya, bank[:, :], ACT.Identity, bias=col("glab", m)),
                    t, d_vec, *fa)
            banks.release(b, t)
            jb, yb, fb = tmp.take()
            t2 = act(lambda e, ya=ya, yb=yb: e.activation(yb, ya, ACT.Abs), t, *fb)
            t2 = act(lambda e, yb=yb: e.activation(yb, yb, ACT.Exp, scale=-1.0), t2)
            t2 = act(lambda e, yb=yb: e.activation(yb, yb, ACT.Ln, bias=1.0), t2)
            t3 = dve(lambda e, ya=ya, yb=yb: e.scalar_tensor_tensor(out=ya, in0=ya, scalar=0.0, in1=yb, op0=ALU.min,
                                                                    op1=ALU.subtract), t2)
            t4 = dve(lambda e, ya=ya, m=m: e.tensor_tensor_scan(Gc[:, m, :], rst[:, :], ya, 0.0, ALU.mult, ALU.add),
                     t3, t_rst)
            tmp.release(ja, t4)
            tmp.release(jb, t3)
            g3 = Gc[:, m, :].rearrange("p (c i) -> p c i", i=64)
            t5 = act(lambda e, m=m: e.activation(eG[:, m, :], Gc[:, m, :], ACT.Exp, scale=1.0 / 16), t4)
            dec_tok[m] = t5
            qin_tok[m] = dve(lambda e, m=m: e.scalar_tensor_tensor(out=qT[:, m, :], in0=qT[:, m, :], scalar=0.125,
                                                                   in1=eG[:, m, :], op0=ALU.mult, op1=ALU.mult),
                             t5, q_tok[m])
            t6 = act(lambda e, m=m: e.activation(kin[:, m, :], Gc[:, m, :], ACT.Exp, scale=-1.0 / 16), t4)
            kin_tok[m] = dve(lambda e, m=m: e.tensor_tensor(kin[:, m, :], kin[:, m, :], kT[:, m, :], ALU.mult),
                             t6, k_tok[m])
            ke3 = kend[:, m, :].rearrange("p (c i) -> p c i", i=64)
            t7 = dve(lambda e, ke3=ke3, g3=g3: e.tensor_tensor(ke3, g3[:, :, 63:64].to_broadcast([128, 8, 64]), g3,
                                                               ALU.subtract), t4)
            t7 = act(lambda e, m=m: e.activation(kend[:, m, :], kend[:, m, :], ACT.Exp, scale=1.0 / 16), t7)
            kend_tok[m] = dve(lambda e, m=m: e.tensor_tensor(kend[:, m, :], kend[:, m, :], kT[:, m, :], ALU.mult),
                              t7, k_tok[m])
        yield
        yield
        yield
        for tc in range(4):
            b, bank, free = banks.take()
            t = pe([lambda e, m=m, tc=tc, bank=bank: e.transpose(bank[:, m * 128:(m + 1) * 128],
                                                                 kend[:, m, tc * 128:(tc + 1) * 128], ident[:, :])
                    for m in range(2)], kend_tok[0], kend_tok[1], c_ident, *free)
            kt_tok[tc] = act(lambda e, tc=tc, bank=bank: e.activation(kendt[:, tc, :], bank[:, 0:256], ACT.Copy), t, t_gm)
            banks.release(b, kt_tok[tc])
        yield
        s_tok.update({(m, 0): t_S0 for m in range(2)})
        for c in range(7):
            tc, r = c // 2, 64 * (c % 2)
            if c == 4:
                yield
            for m in range(2):
                b, bank, free = banks.take()
                t = pe(lambda e, tc=tc, r=r, m=m, bank=bank: e.matmul(
                    bank[:, 0:256], kendt[r:r + 64, tc, m * 128:(m + 1) * 128], vt[r:r + 64, tc, m * 256:(m + 1) * 256],
                    start=True, stop=True), kt_tok[tc], v_tok[tc], *free)
                for p in range(2):
                    q = dve(lambda e, p=p, m=m, c=c, bank=bank: e.scalar_tensor_tensor(
                        out=Sg[64 * p:64 * p + 64, m, c + 1, :], in0=Sg[64 * p:64 * p + 64, m, c, :],
                        scalar=eG[64 * p:64 * p + 64, m, 64 * c + 63:64 * c + 64],
                        in1=bank[64 * p:64 * p + 64, 128 * p:128 * p + 128], op0=ALU.mult, op1=ALU.add),
                        t, s_tok[m, c], dec_tok[m])
                s_tok[m, c + 1] = q
                banks.release(b, q)

        yield
        t_att0 = pool(lambda e: e.memset(Gc[:, :, :], 0.0), kend_tok[0], kend_tok[1], *dec_tok.values(),
                      *kin_tok.values())
        attr = Ring([Gc[:, i, :] for i in range(2)])
        made = {}

        def att_make(h):
            m, r = h // 2, 64 * (h % 2)
            b, bank, free = banks.take()
            t = pe([lambda e, c=c: e.matmul(bank[:, c * 128:(c + 1) * 128], kin[r:r + 64, m, c * 128:(c + 1) * 128],
                                            qT[r:r + 64, m, c * 128:(c + 1) * 128], start=True, stop=True)
                    for c in range(4)], kin_tok[m], qin_tok[m], *free)
            j, ab, af = attr.take()
            for c in range(4):
                cs = slice(c * 128, c * 128 + 128)
                t2 = dve(lambda e, cs=cs: e.copy_predicated(ab[:, cs], gmask[:, :], bank[:, cs]), t, t_gm, t_att0, *af)
            banks.release(b, t2)
            made[h] = (j, ab, t2)

        def att_use(h):
            m, r = h // 2, 64 * (h % 2)
            j, ab, t = made[h]
            b, bank, free = banks.take()
            fns = []
            for tc in range(4):
                fns.append(lambda e, tc=tc: e.matmul(bank[:, tc * 128:(tc + 1) * 128], vt[:, tc, h * 128:(h + 1) * 128],
                                                     ab[:, tc * 128:(tc + 1) * 128], start=True, stop=False))
                for i in range(2):
                    c = 2 * tc + i
                    cc = slice(c * 64, c * 64 + 64)
                    fns.append(lambda e, c=c, cc=cc, i=i: e.matmul(
                        bank[:, cc], Sg[r:r + 64, m, c, :], qT[r:r + 64, m, cc], start=False, stop=(i == 1)))
            t = pe(fns, t, *v_tok.values(), s_tok[m, 7], *free)
            attr.release(j, t)
            st = []
            sum_add(st, bank[:, :], t)
            rs, tr, _, _ = sum_done(st, 1.0 / 128)
            ja, ya, fa = tmp.take()
            t1 = dve(lambda e: e.scalar_tensor_tensor(out=ya, in0=bank[:, :], scalar=col("glan"), in1=rs,
                                                      op0=ALU.mult, op1=ALU.mult), tr, d_vec, *fa)
            banks.release(b, t1)
            go_tok[h] = dve(lambda e: e.tensor_tensor(gs[:, h, :], ya, gs[:, h, :], ALU.mult), t1, g_tok[h])
            tmp.release(ja, go_tok[h])

        att_make(0)
        yield
        for h in range(4):
            if h < 3:
                att_make(h + 1)
            att_use(h)
            yield

    steps = gla_steps()
    next(steps)
    x_free = linear(14, ready, evac_rest, side=lambda m: next(steps, None))
    for _ in steps:
        pass
    mix_ready = {}
    for h in range(4):
        mix_ready[h] = split_x(h, gs[:, h, :], go_tok[h], [x_free], True)
    fence = lasts()
    gla.close()

    ssd = ExitStack()
    acB = sb("acB", [128, 8, T], scope=ssd)
    ead = sb("ead", [128, 4, 8], scope=ssd)
    sel = sb("sel", [8, 8, 128], scope=ssd)
    acT_ = sb("acT", [8, T], scope=ssd)
    rs8 = sb("rs8", [8, T], scope=ssd)
    ea1 = sb("ea1", [8, 1], scope=ssd)
    dtt = sb("dtt", [128, 4, 8], scope=ssd)
    act_ = sb("actok", [128, 4, 8], scope=ssd)
    dte = sb("dte", [128, 4, 8], scope=ssd)
    Bt = sb("Bt", [128, 4, 128], scope=ssd)
    Xd = sb("Xd", [128, 4, T], scope=ssd)
    Xw = sb("Xw", [128, 3, T], scope=ssd)
    Ss = sb("Ss", [128, 4, 256], scope=ssd)
    scm = sb("scm", [128, 2, T], scope=ssd)
    tri = sb("tri", [128, 128], scope=ssd)
    LT = sb("LT", [128, 2, T], scope=ssd)
    CE = sb("CE", [128, 2, T], scope=ssd)

    p0 = pool_part(lambda e: e.memset(sel[:, :, :], 0.0), *fence)
    t_sel = pool_part(lambda e: e.affine_select(out=sel[:, :, :], in_=sel[:, :, :], compare_op=ALU.not_equal, fill=1.0,
                                           base=0, pattern=[[-1, 8], [0, 128]], channel_multiplier=1), p0)
    p1 = pool(lambda e: e.memset(tri[:, :], 1.0))
    t_tri = pool(lambda e: e.affine_select(out=tri[:, :], in_=tri[:, :], compare_op=ALU.is_ge, fill=0.0, base=0,
                                           pattern=[[1, 128]], channel_multiplier=-1), p1)
    p2 = pool_part(lambda e: e.memset(rs8[:, :], 1.0))
    t_rs8 = pool_part(lambda e: e.memset(rs8[:, :].rearrange("p (c i) -> p c i", i=128)[:, :, 0:1], 0.0), p2)

    scratch = [tmp.take() for _ in range(3)]
    y, acT = misc[0:8, :], acT_[:, :]
    z, lnz, u1 = (x[1][0:8, :] for x in scratch)
    t = dve(lambda e: e.tensor_scalar(y, misc[0:8, :], col("dtb", 0, 0, 8), None, ALU.add),
            misc_tok[0], d_vec, *fence, *[x for q in scratch for x in q[2]])
    t1 = act(lambda e: e.activation(z, y, ACT.Abs), t)
    t1 = act(lambda e: e.activation(z, z, ACT.Exp, scale=-1.0), t1, *fence)
    t2 = dve(lambda e: e.tensor_scalar(u1, z, 1.0, None, ALU.add), t1)
    t3 = act(lambda e: e.activation(lnz, u1, ACT.Ln), t2)
    t3b = act(lambda e: e.activation(ea1[:, :], col("alog", 0, 0, 8), ACT.Exp), d_vec)
    t4 = dve(lambda e: e.scalar_tensor_tensor(out=z, in0=u1, scalar=-1.0, in1=z, op0=ALU.add, op1=ALU.subtract), t2)
    t5 = dve(lambda e: e.reciprocal(u1, u1), t4, t3)
    t5 = dve(lambda e: e.tensor_tensor(z, z, u1, ALU.mult), t5)
    t5 = dve(lambda e: e.tensor_tensor(lnz, lnz, z, ALU.subtract), t5, t3)
    t_dt = dve(lambda e: e.scalar_tensor_tensor(out=y, in0=y, scalar=0.0, in1=lnz, op0=ALU.max, op1=ALU.add), t5)
    t6 = dve(lambda e: e.tensor_scalar(z, y, ea1[:, 0:1], -1.0, ALU.mult, ALU.mult), t_dt, t3b)
    t_ac = dve(lambda e: e.tensor_tensor_scan(acT, rs8[:, :], z, 0.0, ALU.mult, ALU.add), t6, t_rs8)
    for x in scratch:
        tmp.release(x[0], t_ac)
    b, bank, free = banks.take()
    fns = []
    for tc in range(4):
        for k, src in ((0, y), (1, acT)):
            fns.append(lambda e, tc=tc, k=k, src=src, bank=bank: e.transpose(
                bank[:, (tc * 2 + k) * 8:(tc * 2 + k) * 8 + 8], src[:, tc * 128:(tc + 1) * 128], ident[0:8, 0:8]))
    t = pe(fns, t_ac, c_ident, *free)
    bv = bank[:, 0:64].rearrange("p (c k h) -> p c k h", k=2, h=8)
    t_dtt = dve(lambda e: e.tensor_copy(dtt[:, :, :], bv[:, :, 0, :]), t)
    t_act = dve(lambda e: e.tensor_copy(act_[:, :, :], bv[:, :, 1, :]), t)
    banks.release(b, t_act)
    acB_tok = {}
    for h in range(8):
        b, bank, free = banks.take()
        t = pe(lambda e, h=h, bank=bank: e.matmul(bank[:, :], sel[:, h, :], acT, start=True, stop=True),
               t_ac, t_sel, *free)
        acB_tok[h] = dve(lambda e, h=h, bank=bank: e.tensor_copy(acB[:, h, :], bank[:, :]), t)
        banks.release(b, acB_tok[h])
    acl = acB[:, :, :].rearrange("p h (c i) -> p c h i", i=128)[:, :, :, 127]
    t_ead = act(lambda e: e.activation(ead[:, :, :], acl, ACT.Exp), acB_tok[7])
    t = dve(lambda e: e.tensor_tensor(dte[:, :, :], acl, act_[:, :, :], ALU.subtract), acB_tok[7], t_act)
    t_dte = act(lambda e: e.activation(dte[:, :, :], dte[:, :, :], ACT.Exp), t)
    xd_tok, xw_tok, bt_tok = {}, {}, {}
    for tc in range(4):
        cols = slice(tc * 128, tc * 128 + 128)
        b, bank, free = banks.take()
        t = pe([lambda e, m=m, cols=cols, bank=bank: e.transpose(bank[:, m * 128:(m + 1) * 128], xs[:, m, cols],
                                                                 ident[:, :]) for m in range(4)],
               *[xs_tok[m] for m in range(4)], *free)
        xd_tok[tc] = dve(lambda e, tc=tc, bank=bank: e.tensor_tensor(
            Xd[:, tc, :].rearrange("p (h d) -> p h d", d=64), bank[:, :].rearrange("p (h d) -> p h d", d=64),
            dtt[:, tc, :].unsqueeze(2).to_broadcast([128, 8, 64]), ALU.mult), t, t_dtt)
        banks.release(b, xd_tok[tc])
        if tc == 3:
            continue
        xw_tok[tc] = dve(lambda e, tc=tc: e.tensor_tensor(
            Xw[:, tc, :].rearrange("p (h d) -> p h d", d=64), Xd[:, tc, :].rearrange("p (h d) -> p h d", d=64),
            dte[:, tc, :].unsqueeze(2).to_broadcast([128, 8, 64]), ALU.mult), xd_tok[tc], t_dte)
        b, bank, free = banks.take()
        t = pe(lambda e, cols=cols, bank=bank: e.transpose(bank[:, 0:128], xs[:, 4, cols], ident[:, :]),
               xs_tok[4], *free)
        bt_tok[tc] = act(lambda e, tc=tc, bank=bank: e.activation(Bt[:, tc, :], bank[:, 0:128], ACT.Copy), t)
        banks.release(b, bt_tok[tc])
    ss_tok = {}
    for c in range(3):
        b, bank, free = banks.take()
        t = pe(lambda e, c=c, bank=bank: e.matmul(bank[:, :], Bt[:, c, :], Xw[:, c, :], start=True, stop=True),
               bt_tok[c], xw_tok[c], *free)
        for g in range(2):
            p = slice(64 * g, 64 * g + 64)
            if c == 0:
                q = dve(lambda e, g=g, p=p, bank=bank: e.tensor_copy(Ss[p, 1, :], bank[p, g * 256:(g + 1) * 256]), t)
                continue
            for j in range(4):
                hh = 4 * g + j
                q = dve(lambda e, g=g, p=p, j=j, hh=hh, c=c, bank=bank: e.scalar_tensor_tensor(
                    out=Ss[p, c + 1, j * 64:(j + 1) * 64], in0=Ss[p, c, j * 64:(j + 1) * 64],
                    scalar=ead[p, c, hh:hh + 1],
                    in1=bank[p, g * 256 + j * 64:g * 256 + (j + 1) * 64], op0=ALU.mult, op1=ALU.add),
                    t, ss_tok[c], t_ead)
        ss_tok[c + 1] = q
        banks.release(b, q)
    scm_tok = {}
    for g in range(2):
        p = slice(64 * g, 64 * g + 64)
        b, bank, free = banks.take()
        t = pe([lambda e, p=p, c=c, bank=bank: e.matmul(bank[:, c * 128:(c + 1) * 128], xs[p, 4, c * 128:(c + 1) * 128],
                                                        xs[p, 5, c * 128:(c + 1) * 128], start=True, stop=True)
                for c in range(4)], xs_tok[4], xs_tok[5], *free)
        scm_tok[g] = dve(lambda e, g=g, bank=bank: e.tensor_tensor(
            scm[:, g, :].rearrange("p (c i) -> p c i", i=128), bank[:, :].rearrange("p (c i) -> p c i", i=128),
            tri[:, :].unsqueeze(1).to_broadcast([128, 4, 128]), ALU.mult), t, t_tri)
        banks.release(b, scm_tok[g])
    ltr = Ring([LT[:, i, :] for i in range(2)])
    cer = Ring([CE[:, i, :] for i in range(2)])
    yz_tok = {}
    for m in range(4):
        bo, obank, ofree = banks.take()
        for hp in range(2):
            h = 2 * m + hp
            g = h // 4
            j = h % 4
            p = slice(64 * g, 64 * g + 64)
            op = slice(64 * hp, 64 * hp + 64)
            jl, lt, lf = ltr.take()
            t = None
            for c in range(4):
                cols = slice(c * 128, c * 128 + 128)
                t = dve(lambda e, lt=lt, cols=cols, h=h, c=c: e.tensor_scalar(
                    lt[:, cols], acB[:, h, cols], act_[:, c, h:h + 1], 0.0, ALU.subtract, ALU.min),
                    acB_tok[h], t_act, *lf)
            t = act(lambda e, lt=lt: e.activation(lt, lt, ACT.Exp), t)
            t_m = dve(lambda e, lt=lt, g=g: e.tensor_tensor(lt, lt, scm[:, g, :], ALU.mult), t, scm_tok[g])
            jc, ce, cf = cer.take()
            t_c = act(lambda e, ce=ce, p=p, h=h: e.activation(ce[p, :], acB[p, h, :], ACT.Exp), acB_tok[h], *cf)
            t_c = dve(lambda e, ce=ce, p=p: e.tensor_tensor(ce[p, :], ce[p, :], xs[p, 5, :], ALU.mult),
                      t_c, xs_tok[5])
            fns = []
            for c in range(4):
                cols = slice(c * 128, c * 128 + 128)
                fns.append(lambda e, c=c, cols=cols, h=h, op=op, lt=lt, obank=obank: e.matmul(
                    obank[op, cols], Xd[:, c, h * 64:(h + 1) * 64], lt[:, cols], start=True, stop=(c == 0)))
                if c:
                    fns.append(lambda e, c=c, cols=cols, j=j, op=op, p=p, ce=ce, obank=obank: e.matmul(
                        obank[op, cols], Ss[p, c, j * 64:(j + 1) * 64], ce[p, cols], start=False, stop=True))
            t = pe(fns, t_m, t_c, ss_tok[3], *xd_tok.values(), *ofree)
            ltr.release(jl, t)
            cer.release(jc, t)
        t1 = dve(lambda e, m=m, obank=obank: e.scalar_tensor_tensor(
            out=xs[:, m, :], in0=xs[:, m, :], scalar=col("dskip", m), in1=obank[:, :], op0=ALU.mult, op1=ALU.add), t)
        banks.release(bo, t1)
        yz_tok[m] = dve(lambda e, m=m: e.tensor_tensor(zs[:, m, :], zs[:, m, :], xs[:, m, :], ALU.mult),
                        t1, z_tok[m])
        if m % 2 == 1:
            st = []
            sum_add(st, zs[:, m - 1, :], yz_tok[m - 1])
            sum_add(st, zs[:, m, :], yz_tok[m])
            rs, tr, _, _ = sum_done(st, 1.0 / 256)
            for mm_ in (m - 1, m):
                ja, ya, fa = tmp.take()
                t2 = dve(lambda e, mm_=mm_, ya=ya, rs=rs: e.scalar_tensor_tensor(
                    out=ya, in0=zs[:, mm_, :], scalar=col("ssdn", mm_), in1=rs, op0=ALU.mult, op1=ALU.mult),
                    tr, *fa)
                mix_ready[4 + mm_] = split_x(4 + mm_, ya, t2, [x_free], True)
                tmp.release(ja, *mix_ready[4 + mm_])
    fence = lasts()
    ssd.close()
    mixer.close()

    new = {}

    st = []

    def evac_add(m, bank, tok):
        new[m] = (dve(lambda e: e.tensor_tensor(hT[:, m, :], hT[:, m, :], bank[:, :], ALU.add), tok, *htoks[m]),)
        sum_add(st, hT[:, m, :], *new[m])
        return list(new[m])

    x_free = linear(8, [mix_ready[c] for c in range(8)], evac_add, first=2)
    htoks = [new[m] for m in range(8)]

    rs, tr, _, _ = sum_done(st, 1.0 / 1024)
    ready = norm_split(hT, htoks, "ffn", 0, rs, tr, [x_free])
    peer = ExitStack()
    iT = sb("iT", [128, 3, T], scope=peer)
    gl = sb("gl", [128, 4, T], scope=peer)
    top = ExitStack()
    qb = sb("qb", [128, 2, T], scope=top)
    kb = sb("kb", [128, 16, 128], scope=top)
    sS = sb("sS", [128, 3, T], scope=top)
    sR = sb("sR", [128, 4, 128], scope=top)
    tv = sb("tv", [128, 4, 16, 16], scope=top)
    ti = sb("ti", [128, 4, 16, 16], U32, scope=top)
    tif = sb("tif", [128, 2, 16, 16], scope=top)
    cand = sb("cand", [128, 2, 256], scope=top)
    cand2 = sb("cand2", [128, 2, 256], scope=top)
    bs_ = sb("bs_", [128, 4, 8, 16], scope=top)
    bp = sb("bp", [128, 4, 8, 16], U32, scope=top)
    bab = sb("bab", [128, 2, 128], U32, scope=top)
    baf = sb("baf", [128, 2, 128], scope=top)
    oh16 = sb("oh16", [128, 2, 2048], scope=top)
    slot = sb("slot", [128, 2, 3, 128], scope=top)
    den = sb("den", [128, 8], scope=top)

    qbr = Ring([qb[:, i, :] for i in range(2)])
    ssr = Ring([sS[:, i, :] for i in range(3)])
    srr = Ring([sR[:, i, :] for i in range(4)])
    t_kb = dma(kb[:, :, :], A["keysT"].rearrange("m p k -> p m k"), sem("s_kb"), *fence)
    top_tok = {}

    pend = []

    def evac_q_late(m, bank, tok):
        i, qq, qf = qbr.take()
        t = act(lambda e: e.activation(qq, bank[:, :], ACT.Copy), tok, *qf, *fence)
        pend.append((m, i, qq, t))
        if len(pend) > 1:
            scores(*pend.pop(0))
        return [t]

    def scores(m, i, qq, t):
        b2, bank2, f2 = banks.take()
        t2 = pe([lambda e, tc=tc: e.matmul(bank2[:, tc * 128:(tc + 1) * 128], qq[:, tc * 128:(tc + 1) * 128], kb[:, m, :],
                                           start=True, stop=True) for tc in range(4)], t, t_kb, *f2)
        qbr.release(i, t2)
        js, ss, sf = ssr.take()
        t3 = act(lambda e: e.activation(ss, bank2[:, :], ACT.Copy), t2, *sf)
        banks.release(b2, t3)
        for tc in range(4):
            src = ss[:, tc * 128:(tc + 1) * 128]
            a8, b8 = tv[:, tc, m, 0:8], tv[:, tc, m, 8:16]
            ta = dve(lambda e, a8=a8, src=src: e.max(a8, src), t3, *fence)
            dve(lambda e, a8=a8, src=src, tc=tc: e.max_index(ti[:, tc, m, 0:8], a8, src), ta)
            jr, rr, rf = srr.take()
            tb = dve(lambda e, a8=a8, src=src, rr=rr: e.match_replace(rr, a8, src, NEG), ta, *rf)
            tc2 = dve(lambda e, b8=b8, rr=rr: e.max(b8, rr), tb)
            td = dve(lambda e, b8=b8, rr=rr, tc=tc: e.max_index(ti[:, tc, m, 8:16], b8, rr), tc2)
            srr.release(jr, td)
            top_tok[m, tc] = td
        ssr.release(js, td)

    linear(16, ready, evac_q_late, first=2)
    scores(*pend.pop(0))

    it_tok = {}
    tfr = {}

    def second_dve(tc):
        k2 = tc % 2
        prev = tfr.get(tc - 2, [])
        t_if = dve(lambda e: e.tensor_copy(tif[:, k2, :, :], ti[:, tc, :, :]), top_tok[15, tc], *prev)
        for h in range(8):
            c3 = cand[:, h % 2, :].rearrange("p (a b) -> p a b", b=16)
            cf, c2 = cand[:, h % 2, :], cand2[:, h % 2, :]
            a8, b8 = bs_[:, tc, h, 0:8], bs_[:, tc, h, 8:16]
            t = dve(lambda e, c3=c3, h=h: e.tensor_tensor(
                c3, tv[:, tc, 2 * h, :].unsqueeze(2).to_broadcast([128, 16, 16]),
                tv[:, tc, 2 * h + 1, :].unsqueeze(1).to_broadcast([128, 16, 16]), ALU.add), top_tok[15, tc])
            ta = dve(lambda e, a8=a8, cf=cf: e.max(a8, cf), t)
            dve(lambda e, a8=a8, cf=cf, h=h: e.max_index(bp[:, tc, h, 0:8], a8, cf), ta)
            tb = dve(lambda e, a8=a8, cf=cf, c2=c2: e.match_replace(c2, a8, cf, NEG), ta)
            tb = dve(lambda e, b8=b8, c2=c2: e.max(b8, c2), tb)
            tb = dve(lambda e, b8=b8, c2=c2, h=h: e.max_index(bp[:, tc, h, 8:16], b8, c2), tb)
        bflat = bp[:, tc, :, :].rearrange("p h k -> p (h k)")
        t1 = dve(lambda e: e.tensor_scalar(bab[:, 0, :], bflat, 4, None, ALU.logical_shift_right), tb)
        t2 = dve(lambda e: e.tensor_scalar(bab[:, 1, :], bflat, 15, None, ALU.bitwise_and), tb)
        t3 = dve(lambda e: e.tensor_copy(baf[:, :, :], bab[:, :, :]), t1, t2)
        for w in range(2):
            o4 = oh16[:, w, :].rearrange("p (h k a) -> p h k a", k=16, a=16)
            o3 = oh16[:, w, :].rearrange("p (s a) -> p s a", a=16)
            ta = dve(lambda e, o3=o3, w=w: e.tensor_tensor(
                o3, baf[:, w, :].unsqueeze(2).to_broadcast([128, 128, 16]),
                iota[:, 0:16].unsqueeze(1).to_broadcast([128, 128, 16]), ALU.is_equal), t3, c_iota)
            last = None
            tg = dve(lambda e, o4=o4, w=w: e.tensor_tensor(
                o4, o4, tif[:, k2, w:16:2, :].unsqueeze(2).to_broadcast([128, 8, 16, 16]), ALU.mult), ta, t_if)
            last = dve(lambda e, o3=o3, w=w: e.tensor_reduce(slot[:, k2, w, :], o3, AX.X, ALU.add), tg)
        b3 = bs_[:, tc, :, :]
        t = dve(lambda e: e.tensor_tensor(slot[:, k2, 2, :].rearrange("p (h k) -> p h k", k=16), b3,
                                          b3[:, :, 0:1].to_broadcast([128, 8, 16]), ALU.subtract), tb, *prev)
        tfr[tc] = [last]
        return t, last

    def second_exp(tc, t, last):
        k2 = tc % 2
        g = slot[:, k2, 2, :]
        g3 = g.rearrange("p (h k) -> p h k", k=16)
        t = act(lambda e: e.activation(g, g, ACT.Exp), t)
        t = dve(lambda e: e.tensor_reduce(den[:, :], g3, AX.X, ALU.add), t)
        t = dve(lambda e: e.reciprocal(den[:, :], den[:, :]), t)
        t = dve(lambda e: e.tensor_tensor(g3, g3, den[:, :].unsqueeze(2).to_broadcast([128, 8, 16]), ALU.mult), t)
        return t, last

    def second_transpose(tc, t, last):
        k2 = tc % 2
        b, bank, free = banks.take()
        t = pe([lambda e, w=w: e.transpose(bank[:, w * 128:(w + 1) * 128], slot[:, k2, w, :], ident[:, :])
                for w in range(3)], t, last, *free)
        t = act(lambda e: e.activation(iT[:, :, tc * 128:(tc + 1) * 128],
                                       bank[:, 0:384].rearrange("p (w t) -> p w t", w=3), ACT.Copy), t)
        banks.release(b, t)
        tfr[tc] = [t]
        it_tok[tc] = t

    gsc = {}

    def gate_setup():
        top_fence = lasts()
        top.close()
        gsc["s"] = ExitStack()
        gsc["gb"] = sb("gbuf", [128, 128, 128], scope=gsc["s"])
        oh = sb("oh", [128, 8, 2, 128], scope=gsc["s"])
        gsc["oh"] = Ring([oh[:, i, :, :] for i in range(8)])
        gsc["fence"] = top_fence
        gsc["store"] = []
        gsc["made"] = []
        gsc["sem"] = sem("s_g")

    def gate_make(tt):
        j, o, of = gsc["oh"].take()
        tc = tt // 128
        ta = dve(lambda e: e.tensor_scalar(o[:, 0, :], iota[:, :], iT[:, 0, tt:tt + 1], iT[:, 2, tt:tt + 1],
                                           ALU.is_equal, ALU.mult), it_tok[tc], *of, *gsc["fence"])
        tb = dve(lambda e: e.tensor_scalar(o[:, 1, :], iota[:, :], iT[:, 1, tt:tt + 1], None, ALU.is_equal),
                 it_tok[tc], *of)
        gsc["made"].append((tt, j, o, ta, tb))

    def gate_use():
        tt, j, o, ta, tb = gsc["made"].pop(0)
        gb, k, tl = gsc["gb"], tt % 4, tt % 128 - tt % 4
        if k == 0:
            gsc["bank"] = banks.take()
        b, bank, free = gsc["bank"]
        t = pe(lambda e: e.matmul(bank[:, k * 128:(k + 1) * 128], o[:, 0, :], o[:, 1, :], start=True, stop=True),
               ta, tb, *free)
        gsc["oh"].release(j, t)
        if k == 3:
            t = act(lambda e: e.activation(gb[:, :, tl:tl + 4].rearrange("p i t -> p t i"),
                                           bank[:, :].rearrange("p (t i) -> p t i", t=4), ACT.Copy),
                    t, *gsc["store"], *gsc["fence"])
            banks.release(b, t)
            gate_last["t"] = t

    s_ga = [sem(f"s_ga{i}") for i in range(4)]
    glr = Ring([gl[:, i, :] for i in range(4)])
    ga_store = {}
    gelu_pend = []

    def evac_u(m, bank, tok):
        i, g, gf = glr.take()
        t = act(lambda e: e.activation(g, bank[:, :], ACT.Gelu), tok, *gf, *fence)
        gelu_pend.append((m, i, g, t))
        if len(gelu_pend) > 1:
            store_u()
        return [t]

    def store_u():
        m, i, g, t = gelu_pend.pop(0)
        ga_store[m] = dma(gA[m, :, :], g, s_ga[i], t)
        glr.release(i, ga_store[m])

    plan = {}
    hold = {}
    for tc in range(4):
        plan.setdefault(6 + 7 * tc, []).append(("exp", tc))
        plan.setdefault(10 + 7 * tc, []).append(("tr", tc))
    for tc in range(4):
        for k in range(16):
            plan.setdefault(33 + 22 * tc + k, []).append(("gate", tc * 128 + k * 8))
        plan.setdefault(33 + 22 * tc + 16, []).append(("store", tc))
    for tc in range(4):
        hold[tc] = None
    gate_last = {}

    def side(m):
        for what, x in plan.get(m, ()):
            if what == "exp":
                hold[x] = second_exp(x, *second_dve(x))
            elif what == "tr":
                second_transpose(x, *hold[x])
                if x == 3:
                    gate_setup()
            elif what == "gate":
                for k in range(8):
                    gate_make(x + k)
            else:
                gv = gG.rearrange("b a t -> a b t")[:, :, x * 128:(x + 1) * 128]
                gsc["store"] = [dma(gv, gsc["gb"][:, :, :], gsc["sem"], gate_last["t"])]
        if m == 122:
            turn()

    s_la = [sem(f"s_la{i}") for i in range(4)]
    h_used, h_ready, l_free, l_ready, vst = {}, {}, {}, {}, {}

    def turn():
        vst["fence"] = lasts() + gsc["store"]
        gsc["s"].close()
        vst["scope"] = ExitStack()
        for name, n, dt in (("la", 4, F32), ("lg", 4, F32), ("Hh", 3, F32R), ("Hl", 3, F32R)):
            vst[name] = sb(name, [128, n, T], dt, scope=vst["scope"])
        for m in range(4):
            load_h(m)
        for m in range(3):
            make_h(m)
            load_h(m + 4)

    def load_h(m):
        i, la, lg = m % 4, vst["la"], vst["lg"]
        dma(la[:, i, :], gA[m, :, :], s_la[i], *l_free.get(m - 4, ()), *vst["fence"], ga_store[m])
        l_ready[m] = dma(lg[:, i, :], gG[m, :, :], s_la[i])

    def make_h(m):
        i, j = m % 4, m % 3
        la, lg, Hh, Hl = vst["la"], vst["lg"], vst["Hh"], vst["Hl"]
        t = dve(lambda e: e.tensor_tensor(la[:, i, :], la[:, i, :], lg[:, i, :], ALU.mult), l_ready[m])
        free = h_used.get(m - 3, ())
        th = act(lambda e: e.activation(Hh[:, j, :], la[:, i, :], ACT.Copy), t, *free)
        tl = dve(lambda e: e.tensor_tensor(Hl[:, j, :], la[:, i, :], Hh[:, j, :].bitcast(F32), ALU.subtract), th)
        h_ready[m] = (th, tl)
        l_free[m] = (th, tl)

    def between():
        if gsc.get("made"):
            gate_use()

    x_free = linear(128, ready, evac_u, side=side, between=between)
    while gelu_pend:
        store_u()

    acc = [banks.take() for _ in range(8)]
    Hh, Hl = vst["Hh"], vst["Hl"]

    def second(m, s, wtok, dc):
        cs = slice(dc * 128, dc * 128 + 128)
        return pe(three(acc[dc][1][:, :], wh[:, s, cs], wl[:, s, cs], Hh[:, m % 3, :], Hl[:, m % 3, :],
                        m == 0, m == 127), *wtok, *h_ready[m], *acc[dc][2])

    for m in range(125):
        n, s, wtok = next_tile()
        for dc in range(8):
            t = second(m, s, wtok, dc)
        h_used[m] = (t,)
        tile_used(n, t)
        make_h(m + 3)
        if m + 7 < 128:
            load_h(m + 7)
    ws = [next_tile() for _ in range(3)]
    st = []
    for dc in range(8):
        for m, (n, s, wtok) in zip(range(125, 128), ws):
            t = second(m, s, wtok, dc)
            if dc == 7:
                tile_used(n, t)
        new[dc] = (dve(lambda e, dc=dc: e.tensor_tensor(hT[:, dc, :], hT[:, dc, :], acc[dc][1][:, :], ALU.add),
                       t, *htoks[dc]),)
        banks.release(acc[dc][0], *new[dc])
        sum_add(st, hT[:, dc, :], *new[dc])
    htoks = [new[m] for m in range(8)]
    fence = lasts()
    vst["scope"].close()
    peer.close()

    rs, tr, _, _ = sum_done(st, 1.0 / 1024)
    ready, st = [], []
    for c in range(8):
        t = dve(lambda e, c=c, rs=rs: e.scalar_tensor_tensor(out=hT[:, c, :], in0=hT[:, c, :], scalar=col("fin", c),
                                                             in1=rs, op0=ALU.mult, op1=ALU.mult), tr)
        new[c] = (t,)
        ready.append(fold(c, hT, new[c], "g2", 0, []))
    htoks = [new[c] for c in range(8)]
    for c in range(8):
        sum_add(st, hT[:, c, :], *new[c])

    ga = ExitStack()
    uT = sb("uTs", [128, 8, T], scope=ga)
    vn = sb("vn", [128, 4, 1024], scope=ga)
    mo = sb("mo", [128, 8, T], scope=ga)
    lngb = sb("lngb", [128, 3, 1024], scope=ga)
    wsT = sb("wsT", [128, 8, 128], scope=ga)
    lnst = sb("lnst", [128, 4, 2, 6], scope=ga)
    ag = sb("ag", [128, 4, 2], scope=ga)
    s_a = sem("s_a")
    dma(lngb[:, :, :], A["rows"], s_a, *fence)
    d_a = dma(wsT[:, :, :], A["wsT"], s_a, *fence)
    t_ws = pool_part(lambda e: e.memset(wsT[64:128, :, 0:64], 0.0), d_a)
    v_toks, u_tok = {}, {}

    def evac_vn(half, tc, bank, tok):
        t = act(lambda e: e.activation(vn[:, tc, half * 512:(half + 1) * 512], bank[:, :], ACT.Gelu_apprx_tanh,
                                       scale=RS4[:, tc:tc + 1]), tok, norm_tok["t4"], *fence)
        v_toks[tc, half] = dve(lambda e: e.bn_stats(lnst[:, tc, half, :], vn[:, tc, half * 512:(half + 1) * 512]),
                               t, *fence)
        return [t]

    linear_tok(8, ready, evac_vn, late=stage_norm(st, True))

    leps = sb("leps", [128, 1], scope=ga)
    c_leps = pool(lambda e: e.memset(leps[:, :], LN_EPS), *fence)
    vtok = {}
    for tc in range(4):
        t = dve(lambda e, tc=tc: e.bn_aggr(ag[:, tc, :], lnst[:, tc, :, :].rearrange("p a b -> p (a b)")),
                v_toks[tc, 0], v_toks[tc, 1])
        t = act(lambda e, tc=tc: e.activation(ag[:, tc, 1:2], ag[:, tc, 1:2], ACT.Sqrt, bias=leps[:, 0:1]), t, c_leps)
        t = dve(lambda e, tc=tc: e.reciprocal(ag[:, tc, 1:2], ag[:, tc, 1:2]), t)
        t = dve(lambda e, tc=tc: e.tensor_scalar(vn[:, tc, :], vn[:, tc, :], ag[:, tc, 0:1], ag[:, tc, 1:2],
                                                 ALU.subtract, ALU.mult), t)
        t = dve(lambda e, tc=tc: e.tensor_tensor(vn[:, tc, :], vn[:, tc, :], lngb[:, 0, :], ALU.mult), t, d_a)
        vtok[tc] = dve(lambda e, tc=tc: e.tensor_tensor(vn[:, tc, :], vn[:, tc, :], lngb[:, 1, :], ALU.add), t)
    gate_tok = {}

    def evac_u2(m, bank, tok):
        j, buf, free = tmp.take()
        t = dve(lambda e: e.tensor_tensor(buf, bank[:, :], RS, ALU.mult), tok, norm_tok["t"], *free)
        u_tok[m] = act(lambda e: e.activation(uT[:, m, :], buf, ACT.Gelu_apprx_tanh), t)
        tmp.release(j, u_tok[m])
        return [t]

    def gating(g):
        b, bank, free = banks.take()
        t = pe([lambda e, n=n: e.matmul(bank[:, n * 128:(n + 1) * 128], vn[:, n, g * 128:(g + 1) * 128],
                                        wsT[:, g, :], start=True, stop=True) for n in range(4)],
               *vtok.values(), t_ws, *free)
        t = dve(lambda e: e.tensor_tensor(
            mo[:, g, :].rearrange("p (n i) -> p n i", i=128), bank[:, :].rearrange("p (n i) -> p n i", i=128),
            lngb[:, 2, g * 128:(g + 1) * 128].unsqueeze(1).to_broadcast([128, 4, 128]), ALU.add), t, d_a)
        banks.release(b, t)
        gate_tok[g] = dve(lambda e: e.tensor_tensor(mo[:, g, :], mo[:, g, :], uT[:, g, :], ALU.mult), t, u_tok[g])

    def side_a(m):
        if m >= 2:
            gating(m - 2)
            if m == 7:
                gating(6)

    x_free = linear(8, ready, evac_u2, side=side_a)
    gating(7)
    ready = [split_x(g, mo[:, g, :], gate_tok[g], [x_free], g % 2 == 0) for g in range(8)]
    st = []

    def evac_mo(m, bank, tok):
        t = act(lambda e: e.activation(uT[:, m, :], bank[:, :], ACT.Copy), tok, gate_tok[m])
        return [t, sum_add(st, uT[:, m, :], t)]

    x_free = linear(8, ready, evac_mo, first=2)
    htoks, ready, st = add_norm_fold(uT, st, "g2", 8, htoks, [x_free], "g2", 16)
    fence = lasts()
    ga.close()

    def ffn(layer, htoks, ready, st, fence, nxt, n0):
        late = stage_norm(st)
        sc = ExitStack()
        Fh = sb(f"Fh{layer}", [128, 16, T], F32R, scope=sc)
        Fl = sb(f"Fl{layer}", [128, 16, T], F32R, scope=sc)
        fo = sb(f"fo{layer}", [128, 8, T], scope=sc)
        f_free, toks, st = [], {}, []
        for half in range(2):
            fr = {}

            def evac_up(m, bank, tok):
                j, b, free = tmp.take()
                t = act(lambda e: e.activation(b, bank[:, :], ACT.Relu), tok, *free)
                t2 = dve(lambda e: e.tensor_tensor(b, b, RS, ALU.mult), t, norm_tok["t"])
                t2 = dve(lambda e: e.tensor_tensor(b, b, b, ALU.mult), t2)
                th = dve(lambda e: e.tensor_copy(Fh[:, m, :], b), t2, *fence, *f_free)
                tl = dve(lambda e: e.tensor_tensor(Fl[:, m, :], b, Fh[:, m, :].bitcast(F32), ALU.subtract), th)
                tmp.release(j, tl)
                fr[m] = (th, tl)
                return [t]

            x_free = linear(16, ready, evac_up, first=2 - half, late=late if half == 0 else None)

            def evac_dn(m, bank, tok):
                if half == 0:
                    toks[m] = (act(lambda e: e.activation(fo[:, m, :], bank[:, :], ACT.Copy), tok, *fence),)
                else:
                    toks[m] = (dve(lambda e: e.tensor_tensor(fo[:, m, :], fo[:, m, :], bank[:, :], ALU.add),
                                   tok, *toks[m]),)
                    sum_add(st, fo[:, m, :], *toks[m])
                return list(toks[m])

            f_free = [linear(8, [fr[m] for m in range(16)], evac_dn, tiles_each=2, xh=Fh, xl=Fl, kcs=16)]
        htoks, ready, st = add_norm_fold(fo, st, "g2", 32 * layer + 24, htoks, [x_free], nxt, n0)
        fence = lasts()
        sc.close()
        return htoks, ready, st, fence

    htoks, ready, st, fence = ffn(0, htoks, ready, st, fence, "kv", 0)

    at = ExitStack()
    kTs = sb("kTs", [128, 8, T], scope=at)
    qTs = sb("qTs", [128, 8, T], scope=at)
    vs = sb("vs", [128, 4, 1024], scope=at)
    bias = sb("bias", [128, 2, T], scope=at)
    sc_ = sb("sc_", [128, 3, 1280], scope=at)
    pt = sb("pt", [128, 2, 1280], scope=at)
    mx = sb("mx", [128, 3, 3, 4], scope=at)

    kt, qt, vtk = {}, {}, {}

    def evac_k(m, bank, tok):
        kt[m] = dve(lambda e: e.tensor_tensor(kTs[:, m, :], bank[:, :], RS, ALU.mult), tok, norm_tok["t"], *fence)
        return [kt[m]]

    linear(8, ready, evac_k, first=2, late=stage_norm(st, True))

    def evac_v2(half, tc, bank, tok):
        vtk[tc, half] = act(lambda e: e.activation(vs[:, tc, half * 512:(half + 1) * 512], bank[:, :], ACT.Copy,
                                                   scale=RS4[:, tc:tc + 1]), tok, norm_tok["t4"], *fence)
        return [vtk[tc, half]]

    x_free = linear_tok(8, ready, evac_v2)
    ready = [fold(c, hT, htoks[c], "g2", 32, [x_free]) for c in range(8)]

    def evac_q2(m, bank, tok):
        qt[m] = dve(lambda e: e.scalar_tensor_tensor(out=qTs[:, m, :], in0=bank[:, :], scalar=0.125, in1=RS,
                                                     op0=ALU.mult, op1=ALU.mult), tok, *fence)
        return [qt[m]]

    def part(*which):
        r = Ring([ps[i] for i in which])
        r.free = [banks.free[i] for i in which]
        return r

    sc_banks, tr_banks, o_banks, q_banks = part(0, 1, 2), part(3, 4), part(5), part(6, 7)

    s_b = [sem("s_b0"), sem("s_b1")]
    OFF = [0, 128, 384, 768]
    JOF = [0, 512, 896, 1152]
    bias_free = {}
    bias_tok = {}

    def load_bias(h):
        i = h % 2
        t = dma(bias[:, i, :], A["relb"][h, :, :], s_b[i], *bias_free.get(h - 2, ()), *fence)
        bias_tok[h] = pool_part(lambda e: e.memset(bias[0:64, i, 448:512], -1e30), t)

    load_bias(0)
    load_bias(1)
    p_tok, pt_used, obk, at_tok, sc_used, h_free = {}, {}, {}, {}, {}, {}

    def att_scores(h):
        i, ib, m, r = h % 3, h % 2, h // 2, 64 * (h % 2)
        b1, k1, f1 = sc_banks.take()
        b2, k2, f2 = sc_banks.take()
        b3, k3, f3 = sc_banks.take()
        where = [(k1, 0), (k1, 128), (k2, 0), (k3, 0)]
        fns = []
        for I in range(4):
            bank, o = where[I]
            n = 128 * (I + 1)
            fns.append(lambda e, bank=bank, o=o, n=n, I=I: e.matmul(
                bank[:, o:o + n], qTs[r:r + 64, m, I * 128:(I + 1) * 128], kTs[r:r + 64, m, 0:n],
                start=True, stop=True))
        t = pe(fns, qt[m], kt[m], *f1, *f2, *f3)
        sc_used[h] = t
        for I in range(4):
            bank, o = where[I]
            n = 128 * (I + 1)
            tt = dve(lambda e, bank=bank, o=o, n=n, I=I: e.tensor_tensor_reduce(
                out=sc_[:, i, OFF[I]:OFF[I] + n], in0=bank[:, o:o + n], in1=bias[:, ib, 512 - n:512], scale=1.0,
                scalar=NEG, op0=ALU.add, op1=ALU.max, accum_out=mx[:, i, 0, I:I + 1]),
                t, bias_tok[h], *pt_used.get(h - 3, ()))
        for b in (b1, b2, b3):
            sc_banks.release(b, tt)
        bias_free[h] = (tt,)
        if h + 2 < 16:
            load_bias(h + 2)
        tn = dve(lambda e: e.tensor_scalar(mx[:, i, 1, :], mx[:, i, 0, :], -1.0, None, ALU.mult), tt)
        for I in range(4):
            n = 128 * (I + 1)
            te = act(lambda e, n=n, I=I: e.activation(sc_[:, i, OFF[I]:OFF[I] + n], sc_[:, i, OFF[I]:OFF[I] + n],
                                                      ACT.Exp, bias=mx[:, i, 1, I:I + 1],
                                                      accum_out=mx[:, i, 2, I:I + 1]), tn)
        p_tok[h] = te

    def att_weights(h):
        i = h % 3
        tt = dve(lambda e: e.reciprocal(mx[:, i, 2, :], mx[:, i, 2, :]), p_tok[h])
        for I in range(4):
            n = 128 * (I + 1)
            p_tok[h] = dve(lambda e, n=n, I=I: e.tensor_scalar(
                sc_[:, i, OFF[I]:OFF[I] + n], sc_[:, i, OFF[I]:OFF[I] + n], mx[:, i, 2, I:I + 1], None, ALU.mult), tt)

    def att_step(h):
        i, ip, m, r = h % 3, h % 2, h // 2, 64 * (h % 2)
        free = h_free.get(h - 2, ())

        def trs(bank, o, J):
            return [lambda e, I=I: e.transpose(bank[:, o + (I - J) * 128:o + (I - J + 1) * 128],
                                               sc_[:, i, OFF[I] + J * 128:OFF[I] + (J + 1) * 128], ident[:, :])
                    for I in range(J, 4)]

        b1, k1, f1 = tr_banks.take()
        t = pe(trs(k1, 0, 0), p_tok[h], *f1)
        e0 = act(lambda e: e.activation(pt[:, ip, 0:512], k1[:, :], ACT.Copy), t, *free, *fence)
        tr_banks.release(b1, e0)
        b2, k2, f2 = tr_banks.take()
        t = pe(trs(k2, 0, 1) + trs(k2, 384, 3), *f2)
        e1 = dve(lambda e: e.tensor_copy(pt[:, ip, 512:896], k2[:, 0:384]), t, *free, *fence)
        e3 = dve(lambda e: e.tensor_copy(pt[:, ip, 1152:1280], k2[:, 384:512]), t)
        tr_banks.release(b2, e3)
        if h + 2 < 16:
            att_scores(h + 2)
        b3, k3, f3 = tr_banks.take()
        t = pe(trs(k3, 0, 2), *f3)
        e2 = act(lambda e: e.activation(pt[:, ip, 896:1152], k3[:, 0:256], ACT.Copy), t)
        tr_banks.release(b3, e2)
        pt_used[h] = (t,)
        if h % 2 == 0:
            obk[m] = o_banks.take()
        bo, ob, of = obk[m]
        t = pe([lambda e, J=J: e.matmul(ob[r:r + 64, J * 128:512], vs[:, J, h * 64:(h + 1) * 64],
                                        pt[:, ip, JOF[J]:JOF[J] + 512 - 128 * J], start=(J == 0), stop=(J == 3))
                for J in range(4)], e0, e1, e2, e3, *vtk.values(), *of)
        h_free[h] = (t,)
        if h % 2 == 1:
            at_tok[m] = act(lambda e: e.activation(qTs[:, m, :], ob[:, :], ACT.Copy), t, sc_used[h])
            o_banks.release(bo, at_tok[m])
        if h + 1 < 16:
            att_weights(h + 1)

    def side_q(m):
        if m == 0:
            att_scores(0)
            att_scores(1)
            att_weights(0)
        else:
            att_step(2 * m - 2)
            att_step(2 * m - 1)

    x_free = linear(8, ready, evac_q2, side=side_q, ring=q_banks)
    ready = [split_x(c, qTs[:, c, :], at_tok[c], [x_free], True) for c in range(7)]
    att_step(14)
    att_step(15)
    ready.append(split_x(7, qTs[:, 7, :], at_tok[7], [x_free], False))
    for r_, which in ((sc_banks, (0, 1, 2)), (tr_banks, (3, 4)), (o_banks, (5,)), (q_banks, (6, 7))):
        for k, i in enumerate(which):
            banks.free[i] = r_.free[k]
    after_att = lasts()
    st = []

    def evac_mo2(m, bank, tok):
        t = act(lambda e: e.activation(kTs[:, m, :], bank[:, :], ACT.Copy), tok, *after_att)
        return [t, sum_add(st, kTs[:, m, :], t)]

    x_free = linear(8, ready, evac_mo2, first=2)
    htoks, ready, st = add_norm_fold(kTs, st, "g2", 40, htoks, [x_free], "g2", 48)
    fence = lasts()
    at.close()

    htoks, ready, st, fence = ffn(1, htoks, ready, st, fence, None, 0)

    s_out = sem("s_out")
    ov = out.rearrange("(c p) t -> p c t", p=128)
    for c in range(8):
        d_out = dma(ov[:, c, :], hT[:, c, :], s_out, *htoks[c])
    sp_l.items.append(([None], (d_out,), None, 0))

    block = ctx.enter_context(nc.Block())
    for reg, lane in ((block.sync, sp_l), (block.gpsimd, pool_l), (block.scalar, act_l), (block.vector, dve_l),
                      (block.tensor, pe_l)):
        def body(eng, lane=lane):
            lane.emit(eng)
        reg(body)
    ctx.close()


def _tiles(w):
    k, m = w.shape
    return np.ascontiguousarray(w.reshape(k // 128, 128, m // 128, 128).transpose(2, 1, 0, 3)).reshape(
        -1, 128, k)


def _tiles_tok(w):
    k, m = w.shape
    return np.ascontiguousarray(w.reshape(4, 2, 128, m // 512, 512).transpose(3, 0, 2, 1, 4)).reshape(-1, 128, 1024)


def _up_down(up, down):
    u = _tiles(up).reshape(2, 16, 128, 1024)
    d = [_tiles(down[i * 2048:(i + 1) * 2048]).reshape(8, 128, 2, 1024).transpose(0, 2, 1, 3).reshape(16, 128, 1024)
         for i in range(2)]
    return u, d


def _layout(v):
    a = {}
    a["xT"] = np.ascontiguousarray(v["x"][0].T)
    w = v["w_in"][0]
    at = np.cumsum([0, 256, 256, 512, 16, 512, 512, 768, 8])
    q, k, vv, gl, go, z, xbc, dt = (w[:, at[i]:at[i + 1]] for i in range(8))
    misc = np.zeros((1024, 128), np.float32)
    misc[:, 0:8] = dt
    misc[:, 32:48] = gl
    a["w_in"] = np.concatenate([_tiles(np.concatenate([misc, q, k], 1)), _tiles_tok(vv),
                                _tiles(np.concatenate([xbc, go, z], 1))], 0)
    a["w_out"] = _tiles(v["w_out"][0])
    a["w_q"] = _tiles(v["peer_w_query"][0])
    a["uT"] = np.ascontiguousarray(v["peer_u"][0].reshape(128, 128, 8, 128).transpose(1, 3, 2, 0)).reshape(
        128, 128, 1024)
    a["v"] = v["peer_v"][0]
    a["keysT"] = np.ascontiguousarray(v["peer_sub_keys"][0].reshape(16, 128, 128).transpose(0, 2, 1))
    a["w_gate2"] = v["gla_w_gate2"][0]
    wi = v["a_w_in_2"][0]
    a["a_in"] = np.concatenate([_tiles_tok(wi[:, 1024:]), _tiles(wi[:, :1024])], 0)
    a["a_out"] = _tiles(v["a_w_out_2"][0])
    for i in range(2):
        u, d = _up_down(v["w_up_2"][i], v["w_down_2"][i])
        a[f"up{i}"] = np.concatenate([u[0], d[0], u[1], d[1]], 0)
    a["w_k"] = _tiles(v["w_k_2"])
    a["w_v2"] = _tiles_tok(v["w_v_2"])
    a["w_q2"] = _tiles(v["b_w_q_2"][0])
    a["w_o2"] = _tiles(v["b_w_o_2"][0])
    a["wsT"] = np.ascontiguousarray(v["a_w_s_2"][0].transpose(2, 0, 1))
    rows = np.stack([v["a_ln_g_2"][0], v["a_ln_b_2"][0], v["a_b_s_2"][0].reshape(1024)], 0)
    a["rows"] = np.ascontiguousarray(np.broadcast_to(rows[None], (128, 3, 1024)))
    idx = np.clip(384 + np.arange(128)[:, None] - np.arange(512)[None, :], -256, 256) + 256
    a["relb"] = np.ascontiguousarray(v["b_rel_bias_2"][0][:, idx])

    def cols(x):
        return x.reshape(-1, 128).T

    pad = np.zeros((128, 2), np.float32)
    pad[0:8, 0] = v["ssd_dt_bias"][0]
    pad[0:8, 1] = v["ssd_a_log"][0]
    a["vec"] = np.ascontiguousarray(np.concatenate([
        cols(v["norm_mix_w"][0]), cols(v["norm_ffn_w"][0]), cols(v["norm_final_w"]), cols(v["norm_g_2"]),
        cols(v["kv_norm_g_2"]), cols(v["gla_b_gate"][0]), cols(v["gla_norm_w"][0]), cols(v["ssd_conv_w"][0]),
        cols(v["ssd_conv_b"][0]), cols(np.repeat(v["ssd_d"][0], 64)), cols(v["ssd_norm_w"][0]), pad], 1))
    return a


def kernel(**inputs):
    import concourse.bacc as _bacc
    from concourse.bass_utils import run_bass_kernel_spmd as _run

    nc = _bacc.Bacc("TRN2", target_bir_lowering=False, num_devices=1)
    laid = {k: v for k, v in _layout({k: np.asarray(v) for k, v in inputs.items()}).items() if v.size}
    arrays, aps = {}, {}
    for name, a in laid.items():
        arrays[f"in_{name}"] = a
        aps[name] = nc.dram_tensor(f"in_{name}", a.shape, F32, kind="ExternalInput").ap()
    out = nc.dram_tensor("out_T", (1024, T), F32, kind="ExternalOutput").ap()
    build_program(nc, aps, out)
    r = _run(nc, [arrays], core_ids=[0])
    return np.ascontiguousarray(r.results[0]["out_T"].T)[None]
```

```python
import numpy as np
import concourse.bass as bass
from concourse import mybir
from contextlib import ExitStack

F32 = mybir.dt.float32
F32R = mybir.dt.float32r
I32 = mybir.dt.int32
U32 = mybir.dt.uint32
ALU = mybir.AluOpType
ACT = mybir.ActivationFunctionType
AX = mybir.AxisListType

T = 512
WR = 4
SP = 64
ND = T - SP
EPS = 1e-6
LN_EPS = 1e-5
NEG = -3.0e38

COLS = {}
_n = 0
for _name, _k in (("mix", 8), ("ffn", 8), ("fin", 8), ("g2", 64), ("kv", 8), ("glab", 2), ("glan", 1),
                  ("cw", 24), ("cb", 6), ("dskip", 4), ("ssdn", 4), ("dtb", 1), ("alog", 1)):
    COLS[_name] = _n
    _n += _k
NVEC = _n


class Lane:

    def __init__(self, sem):
        self.sem, self.count, self.items = sem, 0, []

    def put(self, fns, after, sem=None, by=1):
        if sem is None:
            self.count += 1
            token = (self.sem, self.count)
        else:
            token = None
        self.items.append((fns, after, sem or self.sem, by))
        return token

    def emit(self, eng):
        seen = {}
        for fns, after, sem, by in self.items:
            for s, v in after:
                if seen.get(s.name, 0) < v:
                    seen[s.name] = v
                    eng.wait_ge(s, v)
            for fn in fns[:-1]:
                fn(eng)
            last = fns[-1]
            if last is not None:
                last(eng).then_inc(sem, by)


class Ring:

    def __init__(self, bufs):
        self.bufs, self.free, self.at = bufs, [[] for _ in bufs], 0

    def take(self):
        i = self.at % len(self.bufs)
        self.at += 1
        return i, self.bufs[i], list(self.free[i])

    def release(self, i, *tokens):
        self.free[i] = list(tokens)


def build_program(nc, A, out):
    ctx = ExitStack()

    def sb(name, shape, dt=F32, scope=None):
        return (scope or ctx).enter_context(nc.sbuf_tensor(name, shape, dt))

    def sem(name):
        return ctx.enter_context(nc.semaphore(name))

    pe_l, act_l, dve_l, pool_l, sp_l = (Lane(sem(n)) for n in ("s_pe", "s_act", "s_dve", "s_pool", "s_sp"))

    def pe(fns, *after):
        return pe_l.put(fns if isinstance(fns, list) else [fns], after)

    def act(fn, *after):
        return act_l.put([fn], after)

    def dve(fn, *after):
        return dve_l.put([fn], after)

    after_part = []

    def pool(fn, *after):
        t = pool_l.put([fn], (*after, *after_part))
        after_part.clear()
        return t

    def pool_part(fn, *after):
        t = pool(fn, *after, (pool_l.sem, pool_l.count))
        after_part.append(t)
        return t

    dma_counts = {}

    def dma(dst, src, s, *after, lane=None):
        (lane or sp_l).put([lambda e: e.dma_start(dst, src)], after, sem=s, by=16)
        dma_counts[s.name] = dma_counts.get(s.name, 0) + 16
        return s, dma_counts[s.name]

    def lasts():
        return [(l.sem, l.count) for l in (pe_l, act_l, dve_l, pool_l) if l.count]

    gA = nc.dram_tensor("gA_scratch", (128, 128, ND), F32, kind="Internal").ap()
    gG = nc.dram_tensor("gG_scratch", (128, 128, ND), F32, kind="Internal").ap()

    hT = sb("hT", [128, 8, T])
    Xh = sb("Xh", [128, 8, T], F32R)
    Xl = sb("Xl", [128, 8, T], F32R)
    wraw = sb("wraw", [128, 4, 1024])
    wh = sb("wh", [128, WR, 1024], F32R)
    wl = sb("wl", [128, WR, 1024], F32R)
    tmpb = sb("tmpb", [128, 4, T])
    sqb = sb("sqb", [128, 2, T])
    sqacc = sb("sqacc", [128, T])
    rsb = sb("rsb", [128, 3, T])
    rst4 = sb("rst4", [128, 3, 4])
    stdb = sb("stdb", [128, T])
    ident = sb("ident", [128, 128])
    ones = sb("ones", [128, 128])
    iota = sb("iota", [128, 128])
    vec = sb("vec", [128, NVEC])
    ps = [ctx.enter_context(nc.psum_tensor(f"ps{i}", [128, T], F32)) for i in range(8)]

    def col(name, i=0, lo=0, hi=128):
        c = COLS[name] + i
        return vec[lo:hi, c:c + 1]

    tmp = Ring([tmpb[:, i, :] for i in range(4)])
    sq = Ring([sqb[:, i, :] for i in range(2)])
    banks = Ring(ps)

    s_in = sem("s_in")
    d_vec = dma(vec[:, :], A["vec"], s_in)
    c0 = pool(lambda e: e.memset(ident[:, :], 0.0))
    c_ident = pool(lambda e: e.affine_select(out=ident[:, :], in_=ident[:, :], compare_op=ALU.not_equal, fill=1.0,
                                             base=0, pattern=[[-1, 128]], channel_multiplier=1), c0)
    c_ones = pool(lambda e: e.memset(ones[:, :], 1.0))
    c_iota = pool(lambda e: e.iota(iota[:, :], [[1, 128]], base=0, channel_multiplier=0,
                                   allow_small_or_imprecise_dtypes=True))
    wsem = [sem(f"s_w{i}") for i in range(4)]
    tiles = []
    for name in ("w_in", "w_out", "w_q", "uT"):
        tiles += [A[name][i, :, :] for i in range(A[name].shape[0])]
    v3 = A["v"].rearrange("(a b) d -> a b d", b=128)
    tiles += [v3[:, i, :] for i in range(128)]
    for name in ("a_in", "a_out", "up0", "w_k", "w_v2", "w_q2", "w_o2", "up1"):
        tiles += [A[name][i, :, :] for i in range(A[name].shape[0])]
    raw_ready, w_ready, w_used = {}, {}, {}
    state = {"dma": 0, "split": 0, "use": 0}

    def load_tile():
        n = state["dma"]
        if n < len(tiles):
            after = w_ready.get(n - 4, ())
            raw_ready[n] = dma(wraw[:, n % 4, :], tiles[n], wsem[n % 4], *after)
            state["dma"] += 1

    def split_tile():
        n = state["split"]
        if n >= len(tiles):
            return
        r, s = n % 4, n % WR
        free = w_used.get(n - WR, ())
        th = act(lambda e: e.activation(wh[:, s, :], wraw[:, r, :], ACT.Copy), raw_ready[n], *free)
        tl = pool(lambda e: e.tensor_tensor(wl[:, s, :], wraw[:, r, :], wh[:, s, :].bitcast(F32), ALU.subtract),
                  raw_ready[n], th, *free)
        w_ready[n] = (th, tl)
        state["split"] += 1
        load_tile()

    def next_tile():
        n = state["use"]
        state["use"] += 1
        return n, n % WR, w_ready[n]

    def tile_used(n, token):
        w_used[n] = (token,)
        split_tile()


    xt = A["xT"].rearrange("(c p) t -> p c t", p=128)
    htoks = []
    for i in range(4):
        if i == 1:
            load_tile()
            load_tile()
        htoks += [(dma(hT[:, 2 * i:2 * i + 2, :], xt[:, 2 * i:2 * i + 2, :], sem(f"s_x{i}")),)] * 2

    def three(o, ah, al, bh, bl, start, stop):
        return [lambda e: e.matmul(o, ah, bh, start=start, stop=False),
                lambda e: e.matmul(o, ah, bl, start=False, stop=False),
                lambda e: e.matmul(o, al, bh, start=False, stop=stop)]

    def linear(m_tiles, ready, evac, tiles_each=1, xh=None, xl=None, kcs=8, side=None, between=None, first=1, ring=None,
               late=None, warm=False, t0=0):
        xh, xl, ring = xh or Xh, xl or Xl, ring or banks
        m, last, held = 0, None, []
        while m < m_tiles:
            group = first if m == 0 else 1
            if warm and m == m_tiles - 1:
                sqrt_next()
            bs = [ring.take() for _ in range(group)]
            for q in range(tiles_each):
                ws = [next_tile() for _ in range(group)]
                per = kcs // tiles_each
                for k in range(per):
                    kc = q * per + k
                    for (b, bank, free), (n, s, wtok) in zip(bs, ws):
                        last = pe(three(bank[:, t0:T], wh[:, s, k * 128:(k + 1) * 128],
                                        wl[:, s, k * 128:(k + 1) * 128], xh[:, kc, t0:T], xl[:, kc, t0:T],
                                        kc == 0, kc == kcs - 1),
                                  *wtok, *free, *ready[kc])
                        if k == per - 1:
                            tile_used(n, last)
                    if between is not None:
                        between()
            held += [(m + i, b, bank, last) for i, (b, bank, free) in enumerate(bs)]
            m += group
            if late is not None and m < 4:
                continue
            if late is not None:
                late()
                late = None
            for i, b, bank, tok in held:
                ring.release(b, *evac(i, bank, tok))
                if side is not None:
                    side(i)
            held = []
        return last

    def linear_tok(ntiles, ready, evac, late=None):
        last = None
        for half in range(ntiles // 4):
            bs = [banks.take() for _ in range(4)]
            for q in range(4):
                n, s, wtok = next_tile()
                for k in range(2):
                    kc = 2 * q + k
                    for tc in range(4):
                        mm = three(bs[tc][1][:, :], Xh[:, kc, tc * 128:(tc + 1) * 128],
                                   Xl[:, kc, tc * 128:(tc + 1) * 128], wh[:, s, k * 512:(k + 1) * 512],
                                   wl[:, s, k * 512:(k + 1) * 512], kc == 0, kc == 7)
                        last = pe(mm, *wtok, *bs[tc][2], *ready[kc])
                tile_used(n, last)
            if half == 0 and late is not None:
                late()
            for tc in range(4):
                banks.release(bs[tc][0], *evac(half, tc, bs[tc][1], last))
        return last

    def split_x(c, src, tok, after, use_pool):
        th = act(lambda e: e.activation(Xh[:, c, :], src, ACT.Copy), tok, *after)
        eng = pool if use_pool else dve
        tl = eng(lambda e: e.tensor_tensor(Xl[:, c, :], src, Xh[:, c, :].bitcast(F32), ALU.subtract), th, tok, *after)
        return th, tl

    acc_free = []
    rs_used = [[], []]
    rs_count = [0]

    def sum_add(st, src, *toks):
        if not st:
            t = act(lambda e: e.activation(sqacc[:, :], src, ACT.Square), *toks, *acc_free)
            st.append(t)
            return t
        j, buf, free = sq.take()
        ts = act(lambda e: e.activation(buf, src, ACT.Square), *toks, *free)
        t = dve(lambda e: e.tensor_tensor(sqacc[:, :], sqacc[:, :], buf, ALU.add), ts, st[-1])
        sq.release(j, t)
        st.append(t)
        return ts

    def sum_done_small(st, scale):
        nonlocal acc_free
        i = rs_count[0] % 2
        used, rs, r4 = rs_used[i], rsb[:, i, :], rst4[:, i, :]
        b, bank, free = banks.take()
        tm = pe([lambda e, c=c: e.matmul(bank[:, c:c + 1], sqacc[:, c * 128:(c + 1) * 128], ones[:, 0:1],
                                         start=True, stop=True) for c in range(4)], st[-1], c_ones, *free)
        acc_free = [tm]
        tq = act(lambda e: e.activation(r4, bank[:, 0:4], ACT.Sqrt, bias=epsc[:, 0:1], scale=scale), tm, c_eps, *used)
        banks.release(b, tq)
        tt = dve(lambda e: e.reciprocal(r4, r4), tq)
        j, dg, free = sq.take()
        td = dve(lambda e: e.tensor_tensor(
            dg.rearrange("p (c t) -> p c t", t=128), ident[:, :].unsqueeze(1).to_broadcast([128, 4, 128]),
            r4.unsqueeze(2).to_broadcast([128, 4, 128]), ALU.mult), tt, c_ident, *free)
        b, bank2, free = banks.take()
        tm = pe(lambda e: e.matmul(bank2[:, :], ones[:, :], dg, start=True, stop=True), td, *free)
        sq.release(j, tm)
        tr = act(lambda e: e.activation(rs, bank2[:, :], ACT.Copy), tm, *used)
        banks.release(b, tr)
        rs_used[1 - i] = lasts()
        rs_count[0] += 1
        return rs, tr, None, None

    def sum_done(st, scale, fixed=False, tokens=False):
        nonlocal acc_free
        i = 2 if fixed else rs_count[0] % 2
        used = [] if fixed else rs_used[i]
        rs = rsb[:, i, :]
        b, bank, free = banks.take()
        tm = pe(lambda e: e.matmul(bank[:, :], ones[:, :], sqacc[:, :], start=True, stop=True), st[-1], c_ones, *free)
        acc_free = [tm]
        tq = act(lambda e: e.activation(rs, bank[:, :], ACT.Sqrt, bias=epsc[:, 0:1], scale=scale), tm, c_eps, *used)
        banks.release(b, tq)
        tr = dve(lambda e: e.reciprocal(rs, rs), tq)
        tt = None
        if tokens:
            b, bank2, free = banks.take()
            tm = pe([lambda e, c=c: e.matmul(bank2[:, c:c + 1], sqacc[:, c * 128:(c + 1) * 128], ones[:, 0:1],
                                             start=True, stop=True) for c in range(4)], st[-1], *free)
            acc_free = [tm]
            tq = act(lambda e: e.activation(rst4[:, i, :], bank2[:, 0:4], ACT.Sqrt, bias=epsc[:, 0:1], scale=scale),
                     tm, *used)
            banks.release(b, tq)
            tt = dve(lambda e: e.reciprocal(rst4[:, i, :], rst4[:, i, :]), tq)
        if not fixed:
            rs_used[1 - i] = lasts()
            rs_count[0] += 1
        return rs, tr, rst4[:, i, :], tt

    RS, RS4, norm_tok = rsb[:, 2, :], rst4[:, 2, :], {}

    def stage_norm(st, tokens=False):
        def late():
            _, norm_tok["t"], _, norm_tok["t4"] = sum_done(st, 1.0 / 1024, fixed=True, tokens=tokens)
        return late

    def sqrt_next():
        act(lambda e: e.activation(warmb[:, :], epsc[:, :], ACT.Sqrt), c_eps)

    warmb = sb("warmb", [128, 1])
    epsc = sb("epsc", [128, 1])
    c_eps = pool(lambda e: e.memset(epsc[:, :], EPS))

    def fold(c, src, toks, w, i0, after):
        j, buf, free = tmp.take()
        t = act(lambda e: e.activation(buf, src[:, c, :], ACT.Identity, scale=col(w, i0 + c)), d_vec, *toks, *free)
        r = split_x(c, buf, t, after, True)
        tmp.release(j, *r)
        return r

    def norm_split(src, toks, w, i0, rs, tr, after):
        ready = []
        for c in range(8):
            j, buf, free = tmp.take()
            t = dve(lambda e, b=buf, c=c: e.scalar_tensor_tensor(out=b, in0=src[:, c, :], scalar=col(w, i0 + c),
                                                                 in1=rs, op0=ALU.mult, op1=ALU.mult),
                    tr, d_vec, *toks[c], *free)
            r = split_x(c, buf, t, after, c % 2 == 0)
            tmp.release(j, *r)
            ready.append(r)
        return ready

    def add_norm_fold(m, st, w, i0, htoks, after, w2=None, i2=0, tokens=False):
        rs, tr, _, _ = sum_done_small(st, 1.0 / 1024)
        new, ready = [], []
        for c in range(8):
            t = dve(lambda e, c=c: e.scalar_tensor_tensor(out=m[:, c, :], in0=m[:, c, :], scalar=col(w, i0 + c),
                                                          in1=rs, op0=ALU.mult, op1=ALU.mult), tr)
            eng = pool if w2 is None and c % 3 == 1 else dve
            t2 = eng(lambda e, c=c: e.tensor_tensor(hT[:, c, :], hT[:, c, :], m[:, c, :], ALU.add), t, *htoks[c])
            new.append((t2,))
            if w2 is not None:
                ready.append(fold(c, hT, new[c], w2, i2, after))
        st = []
        if w2 is not None:
            for c in range(8):
                sum_add(st, hT[:, c, :], *new[c])
        return new, ready, st

    for _ in range(2):
        load_tile()
    ready, st = [], []
    for c in range(8):
        ready.append(fold(c, hT, htoks[c], "mix", 0, []))
        if c % 2 == 0 and c < 4:
            split_tile()
    for _ in range(2):
        split_tile()
    for c in range(8):
        sum_add(st, hT[:, c, :], *htoks[c])

    s_c = sem("s_c")
    mixer = ExitStack()
    xs = sb("xs", [128, 6, T], scope=mixer)
    zs = sb("zs", [128, 4, T], scope=mixer)
    misc = sb("misc", [128, T], scope=mixer)
    gs = sb("gs", [128, 4, T], scope=mixer)
    acT_ = sb("acT", [8, T], scope=mixer)
    ea1 = sb("ea1", [8, 1], scope=mixer)
    tri = sb("tri", [128, 128], scope=mixer)
    p1 = pool(lambda e: e.memset(tri[:, :], 1.0))
    t_tri = pool(lambda e: e.affine_select(out=tri[:, :], in_=tri[:, :], compare_op=ALU.is_ge, fill=0.0, base=0,
                                           pattern=[[1, 128]], channel_multiplier=-1), p1)
    gla = ExitStack()
    xp = sb("xp", [128, 2, T + 4], scope=gla)
    cacc = sb("cacc", [128, 2, T], scope=gla)
    qT = sb("qT", [128, 2, T], scope=gla)
    kT = sb("kT", [128, 2, T], scope=gla)
    vt = sb("vt", [128, 4, T], scope=gla)
    w2 = sb("w2", [128, 256], scope=gla)
    d_w2 = dma(w2[32:48, :], A["w_gate2"], s_c)
    xpr = Ring([xp[:, i, :] for i in range(2)])
    car = Ring([cacc[:, i, :] for i in range(2)])
    t_xp0 = dve(lambda e: e.memset(xp[:, :, 0:4], 0.0))

    xs_tok, z_tok, q_tok, k_tok, g_tok, v_tok = {}, {}, {}, {}, {}, {}
    misc_tok = []

    def scaled(dst, bank, tok, *after):
        return dve(lambda e: e.tensor_tensor(dst, bank[:, :], RS, ALU.mult), tok, norm_tok["t"], *after)

    def silu(dst, bank, tok, ring=tmp):
        j, buf, free = ring.take()
        t = scaled(buf, bank, tok, *free)
        t2 = act(lambda e: e.activation(dst, buf, ACT.Silu), t)
        ring.release(j, t2)
        return t2, t

    def evac_in(m, bank, tok):
        if m == 0:
            misc_tok.append(scaled(misc[:, :], bank, tok))
            return misc_tok
        if m < 3:
            q_tok[m - 1] = scaled(qT[:, m - 1, :], bank, tok)
            return [q_tok[m - 1]]
        k_tok[m - 3] = scaled(kT[:, m - 3, :], bank, tok)
        return [k_tok[m - 3]]

    def evac_rest(m, bank, tok):
        if m < 4:
            g_tok[m], t = silu(gs[:, m, :], bank, tok)
            return [t]
        if m < 10:
            c = m - 4
            i, buf, free = xpr.take()
            t = scaled(buf[:, 3:3 + T], bank, tok, t_xp0, *free)
            j, acc, free2 = car.take()
            t1 = dve(lambda e: e.tensor_scalar(acc, buf[:, 0:T], col("cw", c), None, ALU.mult), t, d_vec, *free2)
            for k in range(1, 4):
                t1 = dve(lambda e, k=k: e.scalar_tensor_tensor(out=acc, in0=buf[:, k:k + T],
                                                               scalar=col("cw", 6 * k + c), in1=acc,
                                                               op0=ALU.mult, op1=ALU.add), t1)
            xpr.release(i, t1)
            xs_tok[c] = act(lambda e: e.activation(xs[:, c, :], acc, ACT.Silu, bias=col("cb", c)), t1, d_vec)
            car.release(j, xs_tok[c])
            return [t]
        z_tok[m - 10], t = silu(zs[:, m - 10, :], bank, tok, sq)
        return [t]

    linear(5, ready, evac_in, first=2, late=stage_norm(st, True))

    def evac_v(half, tc, bank, tok):
        v_tok[tc] = dve(lambda e: e.tensor_scalar(vt[:, tc, :], bank[:, :], RS4[:, tc:tc + 1], None, ALU.mult),
                        tok, norm_tok["t4"])
        return [v_tok[tc]]


    Gc = sb("Gc", [128, 2, T], scope=gla)
    eG = sb("eG", [128, 2, T], scope=gla)
    kin = sb("kin", [128, 2, T], scope=gla)
    kend = sb("kend", [128, 2, T], scope=gla)
    kendt = sb("kendt", [128, 4, 256], scope=gla)
    Sg = sb("Sg", [128, 2, 8, 128], scope=gla)
    gmask = sb("gmask", [128, 128], I32, scope=gla)
    gmf = kendt[:, 3, 0:128]

    m0 = pool(lambda e: e.memset(gmf, 1.0))
    m1 = pool(lambda e: e.affine_select(out=gmf, in_=gmf, compare_op=ALU.is_ge, fill=0.0, base=0,
                                        pattern=[[1, 128]], channel_multiplier=-1), m0)
    m2 = pool_part(lambda e: e.memset(kendt[0:64, 3, 64:128], 0.0), m1)
    t_gm = pool(lambda e: e.tensor_copy(gmask[:, :], gmf), m2)
    t_S0 = pool(lambda e: e.memset(Sg[:, :, 0, :], 0.0))

    qin_tok, kin_tok, kend_tok, dec_tok, kt_tok, s_tok, go_tok = {}, {}, {}, {}, {}, {}, {}

    y, acT = misc[0:8, :], acT_[:, :]
    z, lnz, u1 = cacc[0:8, 0, :], cacc[0:8, 1, :], kin[0:8, 0, :]
    scan_tok, ya, yb, fa, t1g = {}, {}, {}, {}, {}
    for m in range(2):
        b, bank, free = banks.take()
        t = pe(lambda e, m=m, bank=bank: e.matmul(bank[:, :], w2[32:48, m * 128:(m + 1) * 128], misc[32:48, :],
                                                  start=True, stop=True), d_w2, misc_tok[0], *free)
        ja, ya[m], fa = tmp.take()
        jb, yb[m], fb = tmp.take()
        t = act(lambda e, bank=bank, m=m: e.activation(ya[m], bank[:, :], ACT.Identity, bias=col("glab", m)),
                t, d_vec, *fa)
        banks.release(b, t)
        t1g[m] = (act(lambda e, m=m: e.activation(yb[m], ya[m], ACT.Abs), t, *fb), ja, jb)
    t = dve(lambda e: e.tensor_scalar(y, misc[0:8, :], col("dtb", 0, 0, 8), None, ALU.add), misc_tok[0], d_vec)
    t1 = act(lambda e: e.activation(z, y, ACT.Abs), t)
    t1 = act(lambda e: e.activation(z, z, ACT.Exp, scale=-1.0), t1)
    t3b = act(lambda e: e.activation(ea1[:, :], col("alog", 0, 0, 8), ACT.Exp), d_vec)
    for m in range(2):
        t2 = act(lambda e, m=m: e.activation(yb[m], yb[m], ACT.Exp, scale=-1.0), t1g[m][0])
        t1g[m] = (t2, *t1g[m][1:])
    t2 = dve(lambda e: e.tensor_scalar(u1, z, 1.0, None, ALU.add), t1)
    t3 = act(lambda e: e.activation(lnz, u1, ACT.Ln), t2)
    t4 = dve(lambda e: e.scalar_tensor_tensor(out=z, in0=u1, scalar=-1.0, in1=z, op0=ALU.add, op1=ALU.subtract), t2)
    t5 = dve(lambda e: e.reciprocal(u1, u1), t4, t3)
    t5 = dve(lambda e: e.tensor_tensor(z, z, u1, ALU.mult), t5)
    t5 = dve(lambda e: e.tensor_tensor(lnz, lnz, z, ALU.subtract), t5, t3)
    t_dt = dve(lambda e: e.scalar_tensor_tensor(out=y, in0=y, scalar=0.0, in1=lnz, op0=ALU.max, op1=ALU.add), t5)
    t6 = dve(lambda e: e.tensor_scalar(z, y, ea1[:, 0:1], -1.0, ALU.mult, ALU.mult), t_dt, t3b)
    for c in range(4):
        cs = slice(c * 128, c * 128 + 128)
        t_ac = dve(lambda e, cs=cs: e.tensor_tensor_scan(acT[:, cs], ones[0:8, :], z[:, cs], 0.0, ALU.mult, ALU.add),
                   t6, c_ones)
    for i in range(2):
        car.release(i, t_ac)
    for m in range(2):
        t2, ja, jb = t1g[m]
        t2 = act(lambda e, m=m: e.activation(yb[m], yb[m], ACT.Ln, bias=1.0), t2)
        t3 = dve(lambda e, m=m: e.scalar_tensor_tensor(out=ya[m], in0=ya[m], scalar=0.0, in1=yb[m], op0=ALU.min,
                                                       op1=ALU.subtract), t2)
        for c in range(8):
            cs = slice(c * 64, c * 64 + 64)
            t4 = dve(lambda e, m=m, cs=cs: e.tensor_tensor_scan(Gc[:, m, cs], ones[:, 0:64], ya[m][:, cs], 0.0,
                                                                ALU.mult, ALU.add), t3, c_ones)
        tmp.release(ja, t4)
        tmp.release(jb, t3)
        scan_tok[m] = t4
    linear_tok(4, ready, evac_v)

    def gla_steps():
        for m in range(2):
            t4 = scan_tok[m]
            g3 = Gc[:, m, :].rearrange("p (c i) -> p c i", i=64)
            t5 = act(lambda e, m=m: e.activation(eG[:, m, :], Gc[:, m, :], ACT.Exp, scale=1.0 / 16), t4)
            dec_tok[m] = t5
            qin_tok[m] = dve(lambda e, m=m: e.scalar_tensor_tensor(out=qT[:, m, :], in0=qT[:, m, :], scalar=0.125,
                                                                   in1=eG[:, m, :], op0=ALU.mult, op1=ALU.mult),
                             t5, q_tok[m])
            t6 = act(lambda e, m=m: e.activation(kin[:, m, :], Gc[:, m, :], ACT.Exp, scale=-1.0 / 16), t4)
            kin_tok[m] = dve(lambda e, m=m: e.tensor_tensor(kin[:, m, :], kin[:, m, :], kT[:, m, :], ALU.mult),
                             t6, k_tok[m])
            ke3 = kend[:, m, :].rearrange("p (c i) -> p c i", i=64)
            t7 = dve(lambda e, ke3=ke3, g3=g3: e.tensor_tensor(ke3, g3[:, :, 63:64].to_broadcast([128, 8, 64]), g3,
                                                               ALU.subtract), t4)
            t7 = act(lambda e, m=m: e.activation(kend[:, m, :], kend[:, m, :], ACT.Exp, scale=1.0 / 16), t7)
            kend_tok[m] = dve(lambda e, m=m: e.tensor_tensor(kend[:, m, :], kend[:, m, :], kT[:, m, :], ALU.mult),
                              t7, k_tok[m])
            yield
        yield
        for tc in range(4):
            b, bank, free = banks.take()
            t = pe([lambda e, m=m, tc=tc, bank=bank: e.transpose(bank[:, m * 128:(m + 1) * 128],
                                                                 kend[:, m, tc * 128:(tc + 1) * 128], ident[:, :])
                    for m in range(2)], kend_tok[0], kend_tok[1], c_ident, *free)
            kt_tok[tc] = act(lambda e, tc=tc, bank=bank: e.activation(kendt[:, tc, :], bank[:, 0:256], ACT.Copy), t, t_gm)
            banks.release(b, kt_tok[tc])
        yield
        s_tok.update({(m, 0): t_S0 for m in range(2)})
        for c in range(7):
            tc, r = c // 2, 64 * (c % 2)
            if c == 4:
                yield
            for m in range(2):
                b, bank, free = banks.take()
                t = pe(lambda e, tc=tc, r=r, m=m, bank=bank: e.matmul(
                    bank[:, 0:256], kendt[r:r + 64, tc, m * 128:(m + 1) * 128], vt[r:r + 64, tc, m * 256:(m + 1) * 256],
                    start=True, stop=True), kt_tok[tc], v_tok[tc], *free)
                for p in range(2):
                    q = dve(lambda e, p=p, m=m, c=c, bank=bank: e.scalar_tensor_tensor(
                        out=Sg[64 * p:64 * p + 64, m, c + 1, :], in0=Sg[64 * p:64 * p + 64, m, c, :],
                        scalar=eG[64 * p:64 * p + 64, m, 64 * c + 63:64 * c + 64],
                        in1=bank[64 * p:64 * p + 64, 128 * p:128 * p + 128], op0=ALU.mult, op1=ALU.add),
                        t, s_tok[m, c], dec_tok[m])
                s_tok[m, c + 1] = q
                banks.release(b, q)

        yield
        t_att0 = pool(lambda e: e.memset(Gc[:, :, :], 0.0), kend_tok[0], kend_tok[1], *dec_tok.values(),
                      *kin_tok.values())
        attr = Ring([Gc[:, i, :] for i in range(2)])
        made = {}

        def att_make(h):
            m, r = h // 2, 64 * (h % 2)
            b, bank, free = banks.take()
            t = pe([lambda e, c=c: e.matmul(bank[:, c * 128:(c + 1) * 128], kin[r:r + 64, m, c * 128:(c + 1) * 128],
                                            qT[r:r + 64, m, c * 128:(c + 1) * 128], start=True, stop=True)
                    for c in range(4)], kin_tok[m], qin_tok[m], *free)
            j, ab, af = attr.take()
            for c in range(4):
                cs = slice(c * 128, c * 128 + 128)
                t2 = dve(lambda e, cs=cs: e.copy_predicated(ab[:, cs], gmask[:, :], bank[:, cs]), t, t_gm, t_att0, *af)
            banks.release(b, t2)
            made[h] = (j, ab, t2)

        def att_use(h):
            m, r = h // 2, 64 * (h % 2)
            j, ab, t = made[h]
            b, bank, free = banks.take()
            fns = []
            for tc in range(4):
                fns.append(lambda e, tc=tc: e.matmul(bank[:, tc * 128:(tc + 1) * 128], vt[:, tc, h * 128:(h + 1) * 128],
                                                     ab[:, tc * 128:(tc + 1) * 128], start=True, stop=False))
                for i in range(2):
                    c = 2 * tc + i
                    cc = slice(c * 64, c * 64 + 64)
                    fns.append(lambda e, c=c, cc=cc, i=i: e.matmul(
                        bank[:, cc], Sg[r:r + 64, m, c, :], qT[r:r + 64, m, cc], start=False, stop=(i == 1)))
            t = pe(fns, t, *v_tok.values(), s_tok[m, 7], *free)
            attr.release(j, t)
            st = []
            sum_add(st, bank[:, :], t)
            rs, tr, _, _ = sum_done(st, 1.0 / 128)
            ja, ya, fa = tmp.take()
            t1 = dve(lambda e: e.scalar_tensor_tensor(out=ya, in0=bank[:, :], scalar=col("glan"), in1=rs,
                                                      op0=ALU.mult, op1=ALU.mult), tr, d_vec, *fa)
            banks.release(b, t1)
            go_tok[h] = dve(lambda e: e.tensor_tensor(gs[:, h, :], ya, gs[:, h, :], ALU.mult), t1, g_tok[h])
            tmp.release(ja, go_tok[h])

        att_make(0)
        yield
        for h in range(4):
            if h < 3:
                att_make(h + 1)
            att_use(h)
            yield

    steps = gla_steps()

    x_free = linear(12, ready, evac_rest, side=lambda m: next(steps, None))
    for _ in steps:
        pass
    fence = lasts()
    gla.close()

    ssd = ExitStack()
    acB = sb("acB", [128, 8, T], scope=ssd)
    ead = sb("ead", [128, 4, 8], scope=ssd)
    dtt = sb("dtt", [128, 4, 8], scope=ssd)
    act_ = sb("actok", [128, 4, 8], scope=ssd)
    dte = sb("dte", [128, 4, 8], scope=ssd)
    Bt = sb("Bt", [128, 4, 128], scope=ssd)
    Xd = sb("Xd", [128, 4, T], scope=ssd)
    Xw = sb("Xw", [128, 3, T], scope=ssd)
    Ss = sb("Ss", [128, 4, 256], scope=ssd)
    scm = sb("scm", [128, 2, T], scope=ssd)
    LT = sb("LT", [128, 4, T], scope=ssd)

    b, bank, free = banks.take()
    fns = []
    for tc in range(4):
        for k, src in ((0, y), (1, acT)):
            fns.append(lambda e, tc=tc, k=k, src=src, bank=bank: e.transpose(
                bank[:, (tc * 2 + k) * 8:(tc * 2 + k) * 8 + 8], src[:, tc * 128:(tc + 1) * 128], ident[0:8, 0:8]))
    t = pe(fns, t_ac, c_ident, *free)
    bv = bank[:, 0:64].rearrange("p (c k h) -> p c k h", k=2, h=8)
    t_dtt = dve(lambda e: e.tensor_copy(dtt[:, :, :], bv[:, :, 0, :]), t)
    t_act = dve(lambda e: e.tensor_copy(act_[:, :, :], bv[:, :, 1, :]), t)
    banks.release(b, t_act)
    acB_tok = {}
    for h in range(8):
        b, bank, free = banks.take()
        t = pe(lambda e, h=h, bank=bank: e.matmul(bank[:, :], ident[0:8, h:h + 1].to_broadcast([8, 128]), acT,
                                                  start=True, stop=True), t_ac, c_ident, *free)
        acB_tok[h] = act(lambda e, h=h, bank=bank: e.activation(acB[:, h, :], bank[:, :], ACT.Copy), t, *fence)
        banks.release(b, acB_tok[h])
    acl = acB[:, :, :].rearrange("p h (c i) -> p c h i", i=128)[:, :, :, 127]
    t_ead = act(lambda e: e.activation(ead[:, :, :], acl, ACT.Exp), acB_tok[7])
    t = dve(lambda e: e.tensor_tensor(dte[:, :, :], acl, act_[:, :, :], ALU.subtract), acB_tok[7], t_act)
    t_dte = act(lambda e: e.activation(dte[:, :, :], dte[:, :, :], ACT.Exp), t)
    xd_tok, xw_tok, bt_tok = {}, {}, {}
    for tc in range(4):
        cols = slice(tc * 128, tc * 128 + 128)
        b, bank, free = banks.take()
        t = pe([lambda e, m=m, cols=cols, bank=bank: e.transpose(bank[:, m * 128:(m + 1) * 128], xs[:, m, cols],
                                                                 ident[:, :]) for m in range(4)],
               *[xs_tok[m] for m in range(4)], *free)
        xd_tok[tc] = dve(lambda e, tc=tc, bank=bank: e.tensor_tensor(
            Xd[:, tc, :].rearrange("p (h d) -> p h d", d=64), bank[:, :].rearrange("p (h d) -> p h d", d=64),
            dtt[:, tc, :].unsqueeze(2).to_broadcast([128, 8, 64]), ALU.mult), t, t_dtt)
        banks.release(b, xd_tok[tc])
        if tc == 3:
            continue
        xw_tok[tc] = dve(lambda e, tc=tc: e.tensor_tensor(
            Xw[:, tc, :].rearrange("p (h d) -> p h d", d=64), Xd[:, tc, :].rearrange("p (h d) -> p h d", d=64),
            dte[:, tc, :].unsqueeze(2).to_broadcast([128, 8, 64]), ALU.mult), xd_tok[tc], t_dte)
        b, bank, free = banks.take()
        t = pe(lambda e, cols=cols, bank=bank: e.transpose(bank[:, 0:128], xs[:, 4, cols], ident[:, :]),
               xs_tok[4], *free)
        bt_tok[tc] = act(lambda e, tc=tc, bank=bank: e.activation(Bt[:, tc, :], bank[:, 0:128], ACT.Copy), t)
        banks.release(b, bt_tok[tc])
    ss_tok = {}
    for c in range(3):
        b, bank, free = banks.take()
        t = pe(lambda e, c=c, bank=bank: e.matmul(bank[:, :], Bt[:, c, :], Xw[:, c, :], start=True, stop=True),
               bt_tok[c], xw_tok[c], *free)
        for g in range(2):
            p = slice(64 * g, 64 * g + 64)
            if c == 0:
                q = dve(lambda e, g=g, p=p, bank=bank: e.tensor_copy(Ss[p, 1, :], bank[p, g * 256:(g + 1) * 256]), t)
                continue
            for j in range(4):
                hh = 4 * g + j
                q = dve(lambda e, g=g, p=p, j=j, hh=hh, c=c, bank=bank: e.scalar_tensor_tensor(
                    out=Ss[p, c + 1, j * 64:(j + 1) * 64], in0=Ss[p, c, j * 64:(j + 1) * 64],
                    scalar=ead[p, c, hh:hh + 1],
                    in1=bank[p, g * 256 + j * 64:g * 256 + (j + 1) * 64], op0=ALU.mult, op1=ALU.add),
                    t, ss_tok[c], t_ead)
        ss_tok[c + 1] = q
        banks.release(b, q)
    scm_tok = {}
    for g in range(2):
        p = slice(64 * g, 64 * g + 64)
        b, bank, free = banks.take()
        t = pe([lambda e, p=p, c=c, bank=bank: e.matmul(bank[:, c * 128:(c + 1) * 128], xs[p, 4, c * 128:(c + 1) * 128],
                                                        xs[p, 5, c * 128:(c + 1) * 128], start=True, stop=True)
                for c in range(4)], xs_tok[4], xs_tok[5], *free)
        scm_tok[g] = dve(lambda e, g=g, bank=bank: e.tensor_tensor(
            scm[:, g, :].rearrange("p (c i) -> p c i", i=128), bank[:, :].rearrange("p (c i) -> p c i", i=128),
            tri[:, :].unsqueeze(1).to_broadcast([128, 4, 128]), ALU.mult), t, t_tri)
        banks.release(b, scm_tok[g])
    ltr = Ring([LT[:, i, :] for i in range(4)])
    yz_tok, head, obs = {}, {}, {}

    def ssd_make(h):
        g = h // 4
        p = slice(64 * g, 64 * g + 64)
        jl, lt, lf = ltr.take()
        for c in range(4):
            cols = slice(c * 128, c * 128 + 128)
            t = dve(lambda e, cols=cols, c=c: e.tensor_scalar(
                lt[:, cols], acB[:, h, cols], act_[:, c, h:h + 1], 0.0, ALU.subtract, ALU.min),
                acB_tok[h], t_act, *lf)
        t = act(lambda e: e.activation(lt, lt, ACT.Exp), t)
        jc, ce, cf = tmp.take()
        t_c = act(lambda e: e.activation(ce[p, :], acB[p, h, :], ACT.Exp), acB_tok[h], *cf)
        head[h] = (jl, lt, t, jc, ce, t_c)

    def ssd_use(h):
        g, j, hp, m = h // 4, h % 4, h % 2, h // 2
        p, op = slice(64 * g, 64 * g + 64), slice(64 * hp, 64 * hp + 64)
        jl, lt, t, jc, ce, t_c = head[h]
        t_m = dve(lambda e: e.tensor_tensor(lt, lt, scm[:, g, :], ALU.mult), t, scm_tok[g])
        t_c = dve(lambda e: e.tensor_tensor(ce[p, :], ce[p, :], xs[p, 5, :], ALU.mult), t_c, xs_tok[5])
        if hp == 0:
            obs[m] = banks.take()
        obank = obs[m][1]
        fns = []
        for c in range(4):
            cols = slice(c * 128, c * 128 + 128)
            fns.append(lambda e, c=c, cols=cols: e.matmul(
                obank[op, cols], Xd[:, c, h * 64:(h + 1) * 64], lt[:, cols], start=True, stop=(c == 0)))
            if c:
                fns.append(lambda e, c=c, cols=cols: e.matmul(
                    obank[op, cols], Ss[p, c, j * 64:(j + 1) * 64], ce[p, cols], start=False, stop=True))
        t = pe(fns, t_m, t_c, ss_tok[3], *xd_tok.values(), *obs[m][2])
        ltr.release(jl, t)
        tmp.release(jc, t)
        return t

    def ssd_gate(m, t):
        obank = obs[m][1]
        t1 = dve(lambda e: e.scalar_tensor_tensor(out=xs[:, m, :], in0=xs[:, m, :], scalar=col("dskip", m),
                                                  in1=obank[:, :], op0=ALU.mult, op1=ALU.add), t)
        banks.release(obs[m][0], t1)
        yz_tok[m] = dve(lambda e: e.tensor_tensor(zs[:, m, :], zs[:, m, :], xs[:, m, :], ALU.mult), t1, z_tok[m])

    def ssd_norm(g):
        st = []
        for m in (2 * g, 2 * g + 1):
            sum_add(st, zs[:, m, :], yz_tok[m])
        rs, tr, _, _ = sum_done(st, 1.0 / 256)
        for m in (2 * g, 2 * g + 1):
            ja, ya, fa = tmp.take()
            t2 = dve(lambda e, m=m, ya=ya: e.scalar_tensor_tensor(
                out=ya, in0=zs[:, m, :], scalar=col("ssdn", m), in1=rs, op0=ALU.mult, op1=ALU.mult), tr, *fa)
            mix_ready[4 + m] = split_x(4 + m, ya, t2, [x_free], m % 2 == 0)
            tmp.release(ja, *mix_ready[4 + m])

    mix_ready = {}
    for h in range(3):
        ssd_make(h)
    for h in range(8):
        if h in (0, 2):
            x_free = linear(1, ready, lambda m, bank, tok, h=h: evac_rest(12 + h // 2, bank, tok))
        if h == 3:
            for i in range(4):
                mix_ready[i] = split_x(i, gs[:, i, :], go_tok[i], [x_free], True)
        t = ssd_use(h)
        if h + 3 < 8:
            ssd_make(h + 3)
        if h % 2 == 1:
            ssd_gate(h // 2, t)
        if h == 5:
            ssd_norm(0)
    ssd_norm(1)
    fence = lasts()
    ssd.close()
    mixer.close()

    new = {}

    st = []

    def evac_add(m, bank, tok):
        new[m] = (dve(lambda e: e.tensor_tensor(hT[:, m, :], hT[:, m, :], bank[:, :], ALU.add), tok, *htoks[m]),)
        sum_add(st, hT[:, m, :], *new[m])
        return list(new[m])

    x_free = linear(8, [mix_ready[c] for c in range(8)], evac_add, first=2, warm=True)
    htoks = [new[m] for m in range(8)]

    rs, tr, _, _ = sum_done_small(st, 1.0 / 1024)
    ready = norm_split(hT, htoks, "ffn", 0, rs, tr, [x_free])
    peer = ExitStack()
    iT = sb("iT", [128, 3, T], scope=peer)
    gl = sb("gl", [128, 4, ND], scope=peer)
    idx = sb("idx", [128, 64], U32, scope=peer)
    gsp = sb("gsp", [128, 64], scope=peer)
    hid = sb("hid", [128, 64], scope=peer)
    top = ExitStack()
    qb = sb("qb", [128, 2, T], scope=top)
    kb = sb("kb", [128, 16, 128], scope=top)
    sS = sb("sS", [128, 3, T], scope=top)
    sR = sb("sR", [128, 4, 128], scope=top)
    tv = sb("tv", [128, 4, 16, 16], scope=top)
    ti = sb("ti", [128, 4, 16, 16], U32, scope=top)
    tif = sb("tif", [128, 2, 16, 16], scope=top)
    cand = sb("cand", [128, 2, 256], scope=top)
    cand2 = sb("cand2", [128, 2, 256], scope=top)
    bs_ = sb("bs_", [128, 4, 8, 16], scope=top)
    bp = sb("bp", [128, 4, 8, 16], U32, scope=top)
    bab = sb("bab", [128, 2, 128], U32, scope=top)
    baf = sb("baf", [128, 2, 128], scope=top)
    oh16 = sb("oh16", [128, 2, 2048], scope=top)
    slot = sb("slot", [128, 2, 3, 128], scope=top)
    den = sb("den", [128, 8], scope=top)
    ef = sb("ef", [64, 128], scope=top)
    eu = sb("eu", [64, 128], U32, scope=top)

    qbr = Ring([qb[:, i, :] for i in range(2)])
    ssr = Ring([sS[:, i, :] for i in range(3)])
    srr = Ring([sR[:, i, :] for i in range(4)])
    t_kb = dma(kb[:, :, :], A["keysT"].rearrange("m p k -> p m k"), sem("s_kb"), *fence)
    top_tok = {}

    pend = []

    def evac_q_late(m, bank, tok):
        i, qq, qf = qbr.take()
        t = act(lambda e: e.activation(qq, bank[:, :], ACT.Copy), tok, *qf, *fence)
        pend.append((m, i, qq, t))
        if len(pend) > 1:
            scores(*pend.pop(0))
        return [t]

    def scores(m, i, qq, t):
        b2, bank2, f2 = banks.take()
        t2 = pe([lambda e, tc=tc: e.matmul(bank2[:, tc * 128:(tc + 1) * 128], qq[:, tc * 128:(tc + 1) * 128], kb[:, m, :],
                                           start=True, stop=True) for tc in range(4)], t, t_kb, *f2)
        qbr.release(i, t2)
        js, ss, sf = ssr.take()
        t3 = act(lambda e: e.activation(ss, bank2[:, :], ACT.Copy), t2, *sf)
        banks.release(b2, t3)
        for tc in range(4):
            src = ss[:, tc * 128:(tc + 1) * 128]
            a8, b8 = tv[:, tc, m, 0:8], tv[:, tc, m, 8:16]
            ta = dve(lambda e, a8=a8, src=src: e.max(a8, src), t3, *fence)
            dve(lambda e, a8=a8, src=src, tc=tc: e.max_index(ti[:, tc, m, 0:8], a8, src), ta)
            jr, rr, rf = srr.take()
            tb = dve(lambda e, a8=a8, src=src, rr=rr: e.match_replace(rr, a8, src, NEG), ta, *rf)
            tc2 = dve(lambda e, b8=b8, rr=rr: e.max(b8, rr), tb)
            td = dve(lambda e, b8=b8, rr=rr, tc=tc: e.max_index(ti[:, tc, m, 8:16], b8, rr), tc2)
            srr.release(jr, td)
            top_tok[m, tc] = td
        ssr.release(js, td)

    linear(16, ready, evac_q_late, first=2)
    scores(*pend.pop(0))

    it_tok = {}
    tfr = {}

    def second_dve(tc):
        k2 = tc % 2
        prev = tfr.get(tc - 2, [])
        t_if = dve(lambda e: e.tensor_copy(tif[:, k2, :, :], ti[:, tc, :, :]), top_tok[15, tc], *prev)
        for h in range(8):
            c3 = cand[:, h % 2, :].rearrange("p (a b) -> p a b", b=16)
            cf, c2 = cand[:, h % 2, :], cand2[:, h % 2, :]
            a8, b8 = bs_[:, tc, h, 0:8], bs_[:, tc, h, 8:16]
            t = dve(lambda e, c3=c3, h=h: e.tensor_tensor(
                c3, tv[:, tc, 2 * h, :].unsqueeze(2).to_broadcast([128, 16, 16]),
                tv[:, tc, 2 * h + 1, :].unsqueeze(1).to_broadcast([128, 16, 16]), ALU.add), top_tok[15, tc])
            ta = dve(lambda e, a8=a8, cf=cf: e.max(a8, cf), t)
            dve(lambda e, a8=a8, cf=cf, h=h: e.max_index(bp[:, tc, h, 0:8], a8, cf), ta)
            tb = dve(lambda e, a8=a8, cf=cf, c2=c2: e.match_replace(c2, a8, cf, NEG), ta)
            tb = dve(lambda e, b8=b8, c2=c2: e.max(b8, c2), tb)
            tb = dve(lambda e, b8=b8, c2=c2, h=h: e.max_index(bp[:, tc, h, 8:16], b8, c2), tb)
        bflat = bp[:, tc, :, :].rearrange("p h k -> p (h k)")
        t1 = dve(lambda e: e.tensor_scalar(bab[:, 0, :], bflat, 4, None, ALU.logical_shift_right), tb)
        t2 = dve(lambda e: e.tensor_scalar(bab[:, 1, :], bflat, 15, None, ALU.bitwise_and), tb)
        t3 = dve(lambda e: e.tensor_copy(baf[:, :, :], bab[:, :, :]), t1, t2)
        for w in range(2):
            o4 = oh16[:, w, :].rearrange("p (h k a) -> p h k a", k=16, a=16)
            o3 = oh16[:, w, :].rearrange("p (s a) -> p s a", a=16)
            ta = dve(lambda e, o3=o3, w=w: e.tensor_tensor(
                o3, baf[:, w, :].unsqueeze(2).to_broadcast([128, 128, 16]),
                iota[:, 0:16].unsqueeze(1).to_broadcast([128, 128, 16]), ALU.is_equal), t3, c_iota)
            last = None
            tg = dve(lambda e, o4=o4, w=w: e.tensor_tensor(
                o4, o4, tif[:, k2, w:16:2, :].unsqueeze(2).to_broadcast([128, 8, 16, 16]), ALU.mult), ta, t_if)
            last = dve(lambda e, o3=o3, w=w: e.tensor_reduce(slot[:, k2, w, :], o3, AX.X, ALU.add), tg)
        b3 = bs_[:, tc, :, :]
        t = dve(lambda e: e.tensor_tensor(slot[:, k2, 2, :].rearrange("p (h k) -> p h k", k=16), b3,
                                          b3[:, :, 0:1].to_broadcast([128, 8, 16]), ALU.subtract), tb, *prev)
        tfr[tc] = [last]
        return t, last

    def second_exp(tc, t, last):
        k2 = tc % 2
        g = slot[:, k2, 2, :]
        g3 = g.rearrange("p (h k) -> p h k", k=16)
        t = act(lambda e: e.activation(g, g, ACT.Exp), t)
        t = dve(lambda e: e.tensor_reduce(den[:, :], g3, AX.X, ALU.add), t)
        t = dve(lambda e: e.reciprocal(den[:, :], den[:, :]), t)
        t = dve(lambda e: e.tensor_tensor(g3, g3, den[:, :].unsqueeze(2).to_broadcast([128, 8, 16]), ALU.mult), t)
        return t, last

    sp_tok = {}

    def sparse_index(t, last):
        ta = dve(lambda e: e.scalar_tensor_tensor(out=ef[:, :], in0=slot[0:64, 0, 0, :], scalar=128.0,
                                                  in1=slot[0:64, 0, 1, :], op0=ALU.mult, op1=ALU.add), last)
        ta = dve(lambda e: e.tensor_copy(eu[:, :], ef[:, :]), ta)
        s_i = sem("s_idx")
        for s in range(2):
            rows, cs = slice(64 * s, 64 * s + 64), slice(64 * s, 64 * s + 64)
            dma(idx[rows, :], eu[:, cs], s_i, ta, *fence)
            sp_tok["idx"] = dma(gsp[rows, :], slot[0:64, 0, 2, cs], s_i, t, *fence)
        tfr[0] = [sp_tok["idx"]]

    def second_transpose(tc, t, last):
        k2 = tc % 2
        b, bank, free = banks.take()
        t = pe([lambda e, w=w: e.transpose(bank[:, w * 128:(w + 1) * 128], slot[:, k2, w, :], ident[:, :])
                for w in range(3)], t, last, *free)
        t = act(lambda e: e.activation(iT[:, :, tc * 128:(tc + 1) * 128],
                                       bank[:, 0:384].rearrange("p (w t) -> p w t", w=3), ACT.Copy), t)
        banks.release(b, t)
        tfr[tc] = [t, *(tfr[0] if tc == 0 else [])]
        it_tok[tc] = t

    gsc = {}

    def gate_setup():
        top_fence = lasts()
        top.close()
        gsc["s"] = ExitStack()
        gsc["gb"] = sb("gbuf", [128, 128, 128], scope=gsc["s"])
        oh = sb("oh", [128, 8, 2, 128], scope=gsc["s"])
        gsc["oh"] = Ring([oh[:, i, :, :] for i in range(8)])
        gsc["fence"] = top_fence
        gsc["store"] = []
        gsc["made"] = []
        gsc["sem"] = sem("s_g")

    def gate_make(tt):
        j, o, of = gsc["oh"].take()
        tc = tt // 128
        ta = dve(lambda e: e.tensor_scalar(o[:, 0, :], iota[:, :], iT[:, 0, tt:tt + 1], iT[:, 2, tt:tt + 1],
                                           ALU.is_equal, ALU.mult), it_tok[tc], *of, *gsc["fence"])
        tb = dve(lambda e: e.tensor_scalar(o[:, 1, :], iota[:, :], iT[:, 1, tt:tt + 1], None, ALU.is_equal),
                 it_tok[tc], *of)
        gsc["made"].append((tt, j, o, ta, tb))

    def gate_use():
        tt, j, o, ta, tb = gsc["made"].pop(0)
        gb, k, tl = gsc["gb"], tt % 4, tt % 128 - tt % 4
        if k == 0:
            gsc["bank"] = banks.take()
        b, bank, free = gsc["bank"]
        t = pe(lambda e: e.matmul(bank[:, k * 128:(k + 1) * 128], o[:, 0, :], o[:, 1, :], start=True, stop=True),
               ta, tb, *free)
        gsc["oh"].release(j, t)
        if k == 3:
            t = act(lambda e: e.activation(gb[:, :, tl:tl + 4].rearrange("p i t -> p t i"),
                                           bank[:, :].rearrange("p (t i) -> p t i", t=4), ACT.Copy),
                    t, *gsc["store"], *gsc["fence"])
            banks.release(b, t)
            gate_last["t"] = t

    s_ga = [sem(f"s_ga{i}") for i in range(4)]
    glr = Ring([gl[:, i, :] for i in range(4)])
    ga_store = {}
    gelu_pend = []

    def evac_u(m, bank, tok):
        i, g, gf = glr.take()
        t = act(lambda e: e.activation(g, bank[:, SP:T], ACT.Gelu), tok, *gf, *fence)
        gelu_pend.append((m, i, g, t))
        if len(gelu_pend) > 1:
            store_u()
        return [t]

    def store_u():
        m, i, g, t = gelu_pend.pop(0)
        ga_store[m] = dma(gA[m, :, :], g, s_ga[i], t)
        glr.release(i, ga_store[m])

    plan = {}
    hold = {}
    for tc in range(4):
        plan.setdefault(6 + 7 * tc, []).append(("exp", tc))
        plan.setdefault(10 + 7 * tc, []).append(("tr", tc))
    for tc in range(4):
        at0, toks = (32, 50, 74, 99)[tc], range(max(SP, tc * 128), tc * 128 + 128, 8)
        for k, x in enumerate(toks):
            plan.setdefault(at0 + k, []).append(("gate", x))
        for k in range(8):
            plan.setdefault(at0 + len(toks) + k, []).append(("store", (tc, k)))
    plan.setdefault(28, []).append(("rows", 0))
    plan.setdefault(30, []).append(("rows", 1))
    busy = {m for m, p in plan.items() if p[0][0] == "store"}
    dots = {m: k for k, m in enumerate([m for m in range(32, 128) if m not in busy][:64])}
    for tc in range(4):
        hold[tc] = None
    gate_last = {}

    xrow = sqb[:, :, :].rearrange("p a t -> p (a t)")
    fetch = [tmpb[:, 2 * i:2 * i + 2, :].rearrange("p a t -> p (a t)") for i in range(2)]
    s_f = [sem("s_f0"), sem("s_f1")]
    row, fetched = {}, {}

    def gather(dst, src, k, s, *after):
        col_k = idx[:, k:k + 1]
        pool_l.put([lambda e: e.indirect_dma_start(out=dst, out_offset=None, in_=src,
                                                   in_offset=bass.IndirectOffsetOnAxis(ap=col_k, axis=0))],
                   (sp_tok["idx"], *after), sem=s, by=16)
        dma_counts[s.name] = dma_counts.get(s.name, 0) + 16
        return s, dma_counts[s.name]

    def row_sums():
        row["tmp"] = [tmp.take() for _ in range(4)]
        row["sq"] = [sq.take() for _ in range(2)]
        free = [x for q in row["tmp"] + row["sq"] for x in q[2]]
        x3 = fetch[0].rearrange("p (c t) -> p c t", t=128)
        for s in range(2):
            row["sum"] = dve(lambda e, s=s: e.tensor_tensor(
                x3[:, :, 64 * s:64 * s + 64], Xh[:, :, 0:SP].bitcast(F32), Xl[:, :, 0:SP].bitcast(F32), ALU.add),
                *free, *[t for r in ready for t in r])

    def row_transposes():
        x3 = fetch[0].rearrange("p (c t) -> p c t", t=128)
        for half in range(2):
            b, bank, free = banks.take()
            t = pe([lambda e, c=c, h=half, bank=bank: e.transpose(bank[:, c * 128:(c + 1) * 128], x3[:, 4 * h + c, :],
                                                                  ident[:, :])
                    for c in range(4)], row["sum"], *free)
            row["x"] = act(lambda e, h=half, bank=bank: e.activation(xrow[:, h * 512:(h + 1) * 512], bank[:, :],
                                                                     ACT.Copy), t, row["sum"])
            banks.release(b, row["x"])
        row["t"] = t
        for k in range(2):
            fetched[k] = gather(fetch[k], A["un"], k, s_f[k], row["t"])

    def row_dot(k):
        g = fetch[k % 2]
        row[k] = dve(lambda e: e.tensor_tensor_reduce(out=g, in0=g, in1=xrow, scale=1.0, scalar=0.0, op0=ALU.mult,
                                                      op1=ALU.add, accum_out=hid[:, k:k + 1]), fetched[k], row["x"])
        if k > 0 and k + 1 < 64:
            fetched[k + 1] = gather(fetch[(k + 1) % 2], A["un"], k + 1, s_f[(k + 1) % 2], row[k - 1])
        if k == 63:
            for q in row["tmp"]:
                tmp.release(q[0], row[k], row[k - 1])
            for q in row["sq"]:
                sq.release(q[0], row[k])

    def side(m):
        for what, x in plan.get(m, ()):
            if what == "exp":
                hold[x] = second_exp(x, *second_dve(x))
                if x == 0:
                    sparse_index(*hold[x])
            elif what == "tr":
                second_transpose(x, *hold[x])
                if x == 3:
                    gate_setup()
            elif what == "gate":
                for k in range(8):
                    gate_make(x + k)
            elif what == "rows":
                (row_sums, row_transposes)[x]()
            else:
                tc, bs = x[0], slice(16 * x[1], 16 * x[1] + 16)
                lo = max(SP, tc * 128)
                gv = gG.rearrange("b a t -> a b t")[:, bs, lo - SP:(tc + 1) * 128 - SP]
                gsc["store"] = [dma(gv, gsc["gb"][:, bs, lo - tc * 128:128], gsc["sem"], gate_last["t"])]
        if m in dots:
            row_dot(dots[m])
        if m == 124:
            turn()

    s_la = [sem(f"s_la{i}") for i in range(4)]
    h_used, h_ready, l_free, l_ready, vst = {}, {}, {}, {}, {}

    def turn():
        vst["fence"] = lasts() + gsc["store"]
        gsc["s"].close()
        vst["scope"] = ExitStack()
        for name, n, dt in (("la", 4, F32), ("lg", 4, F32), ("Hh", 3, F32R), ("Hl", 3, F32R)):
            vst[name] = sb(name, [128, n, ND], dt, scope=vst["scope"])
        vst["vg"] = sb("vg", [128, 3, 1024], scope=vst["scope"])
        vst["va"] = sb("va", [128, 1024], scope=vst["scope"])
        vst["fold"] = sb("foldI", [128, 64], scope=vst["scope"])
        for m in range(4):
            load_h(m)
        for m in range(3):
            make_h(m)
            load_h(m + 4)

    def load_h(m):
        i, la, lg = m % 4, vst["la"], vst["lg"]
        dma(la[:, i, :], gA[m, :, :], s_la[i], *l_free.get(m - 4, ()), *vst["fence"], ga_store[m])
        l_ready[m] = dma(lg[:, i, :], gG[m, :, :], s_la[i])

    def make_h(m):
        i, j = m % 4, m % 3
        la, lg, Hh, Hl = vst["la"], vst["lg"], vst["Hh"], vst["Hl"]
        t = dve(lambda e: e.tensor_tensor(la[:, i, :], la[:, i, :], lg[:, i, :], ALU.mult), l_ready[m])
        free = h_used.get(m - 3, ())
        th = act(lambda e: e.activation(Hh[:, j, :], la[:, i, :], ACT.Copy), t, *free)
        tl = dve(lambda e: e.tensor_tensor(Hl[:, j, :], la[:, i, :], Hh[:, j, :].bitcast(F32), ALU.subtract), th)
        h_ready[m] = (th, tl)
        l_free[m] = (th, tl)

    def between():
        if gsc.get("made"):
            gate_use()

    x_free = linear(128, ready, evac_u, side=side, between=between, t0=SP)
    while gelu_pend:
        store_u()

    acc = [banks.take() for _ in range(8)]
    Hh, Hl = vst["Hh"], vst["Hl"]

    def second(m, s, wtok, dc):
        cs = slice(dc * 128, dc * 128 + 128)
        return pe(three(acc[dc][1][:, SP:T], wh[:, s, cs], wl[:, s, cs], Hh[:, m % 3, :], Hl[:, m % 3, :],
                        m == 0, m == 127), *wtok, *h_ready[m], *acc[dc][2])

    vg, va, foldI = vst["vg"], vst["va"], vst["fold"]
    s_vg = [sem(f"s_vg{i}") for i in range(3)]
    t = act(lambda e: e.activation(hid[:, :], hid[:, :], ACT.Gelu), row[63])
    t_hid = dve(lambda e: e.tensor_tensor(hid[:, :], hid[:, :], gsp[:, :], ALU.mult), t, sp_tok["idx"])
    t_fold = dve(lambda e: e.tensor_tensor(foldI[:, :], ident[:, 0:64], ident[:, 64:128], ALU.add),
                 c_ident, *vst["fence"])
    vsum, vgot = {}, {}

    def v_get(k):
        if k < 64:
            vgot[k] = gather(vg[:, k % 3, :], A["v"], k, s_vg[k % 3], *vst["fence"],
                             *([vsum[k - 3]] if k >= 3 else []))

    def v_add(k):
        if k == 0:
            vsum[k] = dve(lambda e: e.tensor_scalar(va[:, :], vg[:, 0, :], hid[:, 0:1], None, ALU.mult),
                          vgot[0], t_hid)
        else:
            vsum[k] = dve(lambda e: e.scalar_tensor_tensor(out=va[:, :], in0=vg[:, k % 3, :], scalar=hid[:, k:k + 1],
                                                           in1=va[:, :], op0=ALU.mult, op1=ALU.add),
                          vgot[k], vsum[k - 1])

    v_get(0)
    v_get(1)
    for m in range(125):
        if m % 3 != 2 and 6 <= m < 6 + 96:
            k = (m - 6) // 3 * 2 + (m - 6) % 3
            v_get(k + 2)
            v_add(k)
        n, s, wtok = next_tile()
        for dc in range(8):
            t = second(m, s, wtok, dc)
        h_used[m] = (t,)
        tile_used(n, t)
        make_h(m + 3)
        if m + 7 < 128:
            load_h(m + 7)
    sqrt_next()
    ws = [next_tile() for _ in range(3)]
    st = []
    for dc in range(8):
        for m, (n, s, wtok) in zip(range(125, 128), ws):
            t = second(m, s, wtok, dc)
            if dc == 7:
                tile_used(n, t)
        t = pe(lambda e, dc=dc: e.matmul(acc[dc][1][:, 0:SP], va[:, dc * 128:(dc + 1) * 128], foldI[:, :],
                                         start=True, stop=True), vsum[63], t_fold)
        new[dc] = (dve(lambda e, dc=dc: e.tensor_tensor(hT[:, dc, :], hT[:, dc, :], acc[dc][1][:, :], ALU.add),
                       t, *htoks[dc]),)
        banks.release(acc[dc][0], *new[dc])
        sum_add(st, hT[:, dc, :], *new[dc])
    htoks = [new[m] for m in range(8)]
    fence = lasts()
    vst["scope"].close()
    peer.close()

    rs, tr, _, _ = sum_done(st, 1.0 / 1024)
    ready, st = [], []
    for c in range(8):
        t = dve(lambda e, c=c, rs=rs: e.scalar_tensor_tensor(out=hT[:, c, :], in0=hT[:, c, :], scalar=col("fin", c),
                                                             in1=rs, op0=ALU.mult, op1=ALU.mult), tr)
        new[c] = (t,)
        ready.append(fold(c, hT, new[c], "g2", 0, []))
    htoks = [new[c] for c in range(8)]
    for c in range(8):
        sum_add(st, hT[:, c, :], *new[c])

    ga = ExitStack()
    uT = sb("uTs", [128, 8, T], scope=ga)
    vn = sb("vn", [128, 4, 1024], scope=ga)
    mo = sb("mo", [128, 8, T], scope=ga)
    lngb = sb("lngb", [128, 3, 1024], scope=ga)
    wsT = sb("wsT", [128, 8, 128], scope=ga)
    lnst = sb("lnst", [128, 4, 2, 6], scope=ga)
    ag = sb("ag", [128, 4, 2], scope=ga)
    s_a = sem("s_a")
    dma(lngb[:, :, :], A["rows"], s_a, *fence)
    d_a = dma(wsT[:, :, :], A["wsT"], s_a, *fence)
    t_ws = pool_part(lambda e: e.memset(wsT[64:128, :, 0:64], 0.0), d_a)
    v_toks, u_tok = {}, {}

    def evac_vn(half, tc, bank, tok):
        t = act(lambda e: e.activation(vn[:, tc, half * 512:(half + 1) * 512], bank[:, :], ACT.Gelu_apprx_tanh,
                                       scale=RS4[:, tc:tc + 1]), tok, norm_tok["t4"], *fence)
        v_toks[tc, half] = dve(lambda e: e.bn_stats(lnst[:, tc, half, :], vn[:, tc, half * 512:(half + 1) * 512]),
                               t, *fence)
        return [t]

    linear_tok(8, ready, evac_vn, late=stage_norm(st, True))

    leps = sb("leps", [128, 1], scope=ga)
    c_leps = pool(lambda e: e.memset(leps[:, :], LN_EPS), *fence)
    vtok = {}
    for tc in range(4):
        t = dve(lambda e, tc=tc: e.bn_aggr(ag[:, tc, :], lnst[:, tc, :, :].rearrange("p a b -> p (a b)")),
                v_toks[tc, 0], v_toks[tc, 1])
        t = act(lambda e, tc=tc: e.activation(ag[:, tc, 1:2], ag[:, tc, 1:2], ACT.Sqrt, bias=leps[:, 0:1]), t, c_leps)
        t = dve(lambda e, tc=tc: e.reciprocal(ag[:, tc, 1:2], ag[:, tc, 1:2]), t)
        t = dve(lambda e, tc=tc: e.tensor_scalar(vn[:, tc, :], vn[:, tc, :], ag[:, tc, 0:1], ag[:, tc, 1:2],
                                                 ALU.subtract, ALU.mult), t)
        t = dve(lambda e, tc=tc: e.tensor_tensor(vn[:, tc, :], vn[:, tc, :], lngb[:, 0, :], ALU.mult), t, d_a)
        vtok[tc] = dve(lambda e, tc=tc: e.tensor_tensor(vn[:, tc, :], vn[:, tc, :], lngb[:, 1, :], ALU.add), t)
    gate_tok = {}

    def evac_u2(m, bank, tok):
        j, buf, free = tmp.take()
        t = dve(lambda e: e.tensor_tensor(buf, bank[:, :], RS, ALU.mult), tok, norm_tok["t"], *free)
        u_tok[m] = act(lambda e: e.activation(uT[:, m, :], buf, ACT.Gelu_apprx_tanh), t)
        tmp.release(j, u_tok[m])
        return [t]

    def gating(g):
        b, bank, free = banks.take()
        t = pe([lambda e, n=n: e.matmul(bank[:, n * 128:(n + 1) * 128], vn[:, n, g * 128:(g + 1) * 128],
                                        wsT[:, g, :], start=True, stop=True) for n in range(4)],
               *vtok.values(), t_ws, *free)
        t = dve(lambda e: e.tensor_tensor(
            mo[:, g, :].rearrange("p (n i) -> p n i", i=128), bank[:, :].rearrange("p (n i) -> p n i", i=128),
            lngb[:, 2, g * 128:(g + 1) * 128].unsqueeze(1).to_broadcast([128, 4, 128]), ALU.add), t, d_a)
        banks.release(b, t)
        gate_tok[g] = dve(lambda e: e.tensor_tensor(mo[:, g, :], mo[:, g, :], uT[:, g, :], ALU.mult), t, u_tok[g])

    def side_a(m):
        if m >= 2:
            gating(m - 2)
            if m == 7:
                gating(6)

    x_free = linear(8, ready, evac_u2, side=side_a)
    gating(7)
    ready = [split_x(g, mo[:, g, :], gate_tok[g], [x_free], g % 2 == 0) for g in range(8)]
    st = []

    def evac_mo(m, bank, tok):
        t = act(lambda e: e.activation(uT[:, m, :], bank[:, :], ACT.Copy), tok, gate_tok[m])
        return [t, sum_add(st, uT[:, m, :], t)]

    x_free = linear(8, ready, evac_mo, first=2, warm=True)
    htoks, ready, st = add_norm_fold(uT, st, "g2", 8, htoks, [x_free], "g2", 16)
    fence = lasts()
    ga.close()

    def ffn(layer, htoks, ready, st, fence, nxt, n0):
        late = stage_norm(st)
        sc = ExitStack()
        Fh = sb(f"Fh{layer}", [128, 16, T], F32R, scope=sc)
        Fl = sb(f"Fl{layer}", [128, 16, T], F32R, scope=sc)
        fo = sb(f"fo{layer}", [128, 8, T], scope=sc)
        f_free, toks, st = [], {}, []
        for half in range(2):
            fr = {}

            def evac_up(m, bank, tok):
                j, b, free = tmp.take()
                t = act(lambda e: e.activation(b, bank[:, :], ACT.Relu), tok, *free)
                t2 = dve(lambda e: e.tensor_tensor(b, b, RS, ALU.mult), t, norm_tok["t"])
                t2 = dve(lambda e: e.tensor_tensor(b, b, b, ALU.mult), t2)
                th = dve(lambda e: e.tensor_copy(Fh[:, m, :], b), t2, *fence, *f_free)
                tl = dve(lambda e: e.tensor_tensor(Fl[:, m, :], b, Fh[:, m, :].bitcast(F32), ALU.subtract), th)
                tmp.release(j, tl)
                fr[m] = (th, tl)
                return [t]

            x_free = linear(16, ready, evac_up, first=2 - half, late=late if half == 0 else None)

            def evac_dn(m, bank, tok):
                if half == 0:
                    toks[m] = (act(lambda e: e.activation(fo[:, m, :], bank[:, :], ACT.Copy), tok, *fence),)
                else:
                    toks[m] = (dve(lambda e: e.tensor_tensor(fo[:, m, :], fo[:, m, :], bank[:, :], ALU.add),
                                   tok, *toks[m]),)
                    sum_add(st, fo[:, m, :], *toks[m])
                return list(toks[m])

            f_free = [linear(8, [fr[m] for m in range(16)], evac_dn, tiles_each=2, xh=Fh, xl=Fl, kcs=16,
                             warm=half == 1)]
        htoks, ready, st = add_norm_fold(fo, st, "g2", 32 * layer + 24, htoks, [x_free], nxt, n0)
        fence = lasts()
        sc.close()
        return htoks, ready, st, fence

    htoks, ready, st, fence = ffn(0, htoks, ready, st, fence, "kv", 0)

    at = ExitStack()
    kTs = sb("kTs", [128, 8, T], scope=at)
    qTs = sb("qTs", [128, 8, T], scope=at)
    vs = sb("vs", [128, 4, 1024], scope=at)
    bias = sb("bias", [128, 2, T], scope=at)
    sc_ = sb("sc_", [128, 3, 1280], scope=at)
    pt = sb("pt", [128, 2, 1280], scope=at)
    mx = sb("mx", [128, 3, 3, 4], scope=at)

    kt, qt, vtk = {}, {}, {}

    def evac_k(m, bank, tok):
        kt[m] = dve(lambda e: e.tensor_tensor(kTs[:, m, :], bank[:, :], RS, ALU.mult), tok, norm_tok["t"], *fence)
        return [kt[m]]

    linear(8, ready, evac_k, first=2, late=stage_norm(st, True))

    def evac_v2(half, tc, bank, tok):
        vtk[tc, half] = act(lambda e: e.activation(vs[:, tc, half * 512:(half + 1) * 512], bank[:, :], ACT.Copy,
                                                   scale=RS4[:, tc:tc + 1]), tok, norm_tok["t4"], *fence)
        return [vtk[tc, half]]

    x_free = linear_tok(8, ready, evac_v2)
    ready = [fold(c, hT, htoks[c], "g2", 32, [x_free]) for c in range(8)]

    def evac_q2(m, bank, tok):
        qt[m] = dve(lambda e: e.scalar_tensor_tensor(out=qTs[:, m, :], in0=bank[:, :], scalar=0.125, in1=RS,
                                                     op0=ALU.mult, op1=ALU.mult), tok, *fence)
        return [qt[m]]

    def part(*which):
        r = Ring([ps[i] for i in which])
        r.free = [banks.free[i] for i in which]
        return r

    sc_banks, tr_banks, o_banks, q_banks = part(0, 1, 2), part(3, 4), part(5), part(6, 7)

    s_b = [sem("s_b0"), sem("s_b1")]
    OFF = [0, 128, 384, 768]
    JOF = [0, 512, 896, 1152]
    bias_free = {}
    bias_tok = {}

    def load_bias(h):
        i = h % 2
        t = dma(bias[:, i, :], A["relb"][h, :, :], s_b[i], *bias_free.get(h - 2, ()), *fence)
        bias_tok[h] = pool_part(lambda e: e.memset(bias[0:64, i, 448:512], -1e30), t)

    load_bias(0)
    load_bias(1)
    p_tok, pt_used, obk, at_tok, sc_used, h_free = {}, {}, {}, {}, {}, {}

    def att_scores(h):
        i, ib, m, r = h % 3, h % 2, h // 2, 64 * (h % 2)
        b1, k1, f1 = sc_banks.take()
        b2, k2, f2 = sc_banks.take()
        b3, k3, f3 = sc_banks.take()
        where = [(k1, 0), (k1, 128), (k2, 0), (k3, 0)]
        fns = []
        for I in range(4):
            bank, o = where[I]
            n = 128 * (I + 1)
            fns.append(lambda e, bank=bank, o=o, n=n, I=I: e.matmul(
                bank[:, o:o + n], qTs[r:r + 64, m, I * 128:(I + 1) * 128], kTs[r:r + 64, m, 0:n],
                start=True, stop=True))
        t = pe(fns, qt[m], kt[m], *f1, *f2, *f3)
        sc_used[h] = t
        for I in range(4):
            bank, o = where[I]
            n = 128 * (I + 1)
            tt = dve(lambda e, bank=bank, o=o, n=n, I=I: e.tensor_tensor_reduce(
                out=sc_[:, i, OFF[I]:OFF[I] + n], in0=bank[:, o:o + n], in1=bias[:, ib, 512 - n:512], scale=1.0,
                scalar=NEG, op0=ALU.add, op1=ALU.max, accum_out=mx[:, i, 0, I:I + 1]),
                t, bias_tok[h], *pt_used.get(h - 3, ()))
        for b in (b1, b2, b3):
            sc_banks.release(b, tt)
        bias_free[h] = (tt,)
        if h + 2 < 16:
            load_bias(h + 2)
        tn = dve(lambda e: e.tensor_scalar(mx[:, i, 1, :], mx[:, i, 0, :], -1.0, None, ALU.mult), tt)
        p_tok[h] = tn

    def att_exp(h):
        i, tn = h % 3, p_tok[h]
        for I in range(4):
            n = 128 * (I + 1)
            te = act(lambda e, n=n, I=I: e.activation(sc_[:, i, OFF[I]:OFF[I] + n], sc_[:, i, OFF[I]:OFF[I] + n],
                                                      ACT.Exp, bias=mx[:, i, 1, I:I + 1],
                                                      accum_out=mx[:, i, 2, I:I + 1]), tn)
        p_tok[h] = te

    def att_weights(h):
        i = h % 3
        tt = dve(lambda e: e.reciprocal(mx[:, i, 2, :], mx[:, i, 2, :]), p_tok[h])
        for I in range(4):
            n = 128 * (I + 1)
            p_tok[h] = dve(lambda e, n=n, I=I: e.tensor_scalar(
                sc_[:, i, OFF[I]:OFF[I] + n], sc_[:, i, OFF[I]:OFF[I] + n], mx[:, i, 2, I:I + 1], None, ALU.mult), tt)

    def att_step(h):
        i, ip, m, r = h % 3, h % 2, h // 2, 64 * (h % 2)
        free = h_free.get(h - 2, ())

        def trs(bank, o, J):
            return [lambda e, I=I: e.transpose(bank[:, o + (I - J) * 128:o + (I - J + 1) * 128],
                                               sc_[:, i, OFF[I] + J * 128:OFF[I] + (J + 1) * 128], ident[:, :])
                    for I in range(J, 4)]

        b1, k1, f1 = tr_banks.take()
        t = pe(trs(k1, 0, 0), p_tok[h], *f1)
        e0 = act(lambda e: e.activation(pt[:, ip, 0:512], k1[:, :], ACT.Copy), t, *free, *fence)
        tr_banks.release(b1, e0)
        b2, k2, f2 = tr_banks.take()
        t = pe(trs(k2, 0, 1) + trs(k2, 384, 3), *f2)
        e1 = dve(lambda e: e.tensor_copy(pt[:, ip, 512:896], k2[:, 0:384]), t, *free, *fence)
        e3 = dve(lambda e: e.tensor_copy(pt[:, ip, 1152:1280], k2[:, 384:512]), t)
        tr_banks.release(b2, e3)
        if h + 2 < 16:
            att_scores(h + 2)
        b3, k3, f3 = tr_banks.take()
        t = pe(trs(k3, 0, 2), *f3)
        e2 = act(lambda e: e.activation(pt[:, ip, 896:1152], k3[:, 0:256], ACT.Copy), t)
        tr_banks.release(b3, e2)
        if h + 2 < 16:
            att_exp(h + 2)
        pt_used[h] = (t,)
        if h % 2 == 0:
            obk[m] = o_banks.take()
        bo, ob, of = obk[m]
        t = pe([lambda e, J=J: e.matmul(ob[r:r + 64, J * 128:512], vs[:, J, h * 64:(h + 1) * 64],
                                        pt[:, ip, JOF[J]:JOF[J] + 512 - 128 * J], start=(J == 0), stop=(J == 3))
                for J in range(4)], e0, e1, e2, e3, *vtk.values(), *of)
        h_free[h] = (t,)
        if h % 2 == 1:
            at_tok[m] = act(lambda e: e.activation(qTs[:, m, :], ob[:, :], ACT.Copy), t, sc_used[h])
            o_banks.release(bo, at_tok[m])
        if h + 1 < 16:
            att_weights(h + 1)

    def side_q(m):
        if m == 0:
            att_scores(0)
            att_exp(0)
            att_scores(1)
            att_exp(1)
            att_weights(0)
        else:
            att_step(2 * m - 2)
            att_step(2 * m - 1)

    x_free = linear(8, ready, evac_q2, side=side_q, ring=q_banks)
    ready = [split_x(c, qTs[:, c, :], at_tok[c], [x_free], True) for c in range(7)]
    att_step(14)
    att_step(15)
    ready.append(split_x(7, qTs[:, 7, :], at_tok[7], [x_free], False))
    for r_, which in ((sc_banks, (0, 1, 2)), (tr_banks, (3, 4)), (o_banks, (5,)), (q_banks, (6, 7))):
        for k, i in enumerate(which):
            banks.free[i] = r_.free[k]
    after_att = lasts()
    st = []

    def evac_mo2(m, bank, tok):
        t = act(lambda e: e.activation(kTs[:, m, :], bank[:, :], ACT.Copy), tok, *after_att)
        return [t, sum_add(st, kTs[:, m, :], t)]

    x_free = linear(8, ready, evac_mo2, first=2, warm=True)
    htoks, ready, st = add_norm_fold(kTs, st, "g2", 40, htoks, [x_free], "g2", 48)
    fence = lasts()
    at.close()

    htoks, ready, st, fence = ffn(1, htoks, ready, st, fence, None, 0)

    s_out = sem("s_out")
    ov = out.rearrange("(c p) t -> p c t", p=128)
    for c in range(8):
        d_out = dma(ov[:, c, :], hT[:, c, :], s_out, *htoks[c])
    sp_l.items.append(([None], (d_out,), None, 0))

    block = ctx.enter_context(nc.Block())
    for reg, lane in ((block.sync, sp_l), (block.gpsimd, pool_l), (block.scalar, act_l), (block.vector, dve_l),
                      (block.tensor, pe_l)):
        def body(eng, lane=lane):
            lane.emit(eng)
        reg(body)
    ctx.close()


def _tiles(w):
    k, m = w.shape
    return np.ascontiguousarray(w.reshape(k // 128, 128, m // 128, 128).transpose(2, 1, 0, 3)).reshape(
        -1, 128, k)


def _tiles_tok(w):
    k, m = w.shape
    return np.ascontiguousarray(w.reshape(4, 2, 128, m // 512, 512).transpose(3, 0, 2, 1, 4)).reshape(-1, 128, 1024)


def _up_down(up, down):
    u = _tiles(up).reshape(2, 16, 128, 1024)
    d = [_tiles(down[i * 2048:(i + 1) * 2048]).reshape(8, 128, 2, 1024).transpose(0, 2, 1, 3).reshape(16, 128, 1024)
         for i in range(2)]
    return u, d


def _layout(v):
    a = {}
    a["xT"] = np.ascontiguousarray(v["x"][0].T)
    w = v["w_in"][0]
    at = np.cumsum([0, 256, 256, 512, 16, 512, 512, 768, 8])
    q, k, vv, gl, go, z, xbc, dt = (w[:, at[i]:at[i + 1]] for i in range(8))
    misc = np.zeros((1024, 128), np.float32)
    misc[:, 0:8] = dt
    misc[:, 32:48] = gl
    a["w_in"] = np.concatenate([_tiles(np.concatenate([misc, q, k], 1)), _tiles_tok(vv),
                                _tiles(np.concatenate([go, xbc, z], 1))], 0)
    a["w_out"] = _tiles(v["w_out"][0])
    a["w_q"] = _tiles(v["peer_w_query"][0])
    a["uT"] = np.ascontiguousarray(v["peer_u"][0].reshape(128, 128, 8, 128).transpose(1, 3, 2, 0)).reshape(
        128, 128, 1024)
    a["v"] = v["peer_v"][0]
    a["un"] = v["peer_u"][0]
    a["keysT"] = np.ascontiguousarray(v["peer_sub_keys"][0].reshape(16, 128, 128).transpose(0, 2, 1))
    a["w_gate2"] = v["gla_w_gate2"][0]
    wi = v["a_w_in_2"][0]
    a["a_in"] = np.concatenate([_tiles_tok(wi[:, 1024:]), _tiles(wi[:, :1024])], 0)
    a["a_out"] = _tiles(v["a_w_out_2"][0])
    for i in range(2):
        u, d = _up_down(v["w_up_2"][i], v["w_down_2"][i])
        a[f"up{i}"] = np.concatenate([u[0], d[0], u[1], d[1]], 0)
    a["w_k"] = _tiles(v["w_k_2"])
    a["w_v2"] = _tiles_tok(v["w_v_2"])
    a["w_q2"] = _tiles(v["b_w_q_2"][0])
    a["w_o2"] = _tiles(v["b_w_o_2"][0])
    a["wsT"] = np.ascontiguousarray(v["a_w_s_2"][0].transpose(2, 0, 1))
    rows = np.stack([v["a_ln_g_2"][0], v["a_ln_b_2"][0], v["a_b_s_2"][0].reshape(1024)], 0)
    a["rows"] = np.ascontiguousarray(np.broadcast_to(rows[None], (128, 3, 1024)))
    idx = np.clip(384 + np.arange(128)[:, None] - np.arange(512)[None, :], -256, 256) + 256
    a["relb"] = np.ascontiguousarray(v["b_rel_bias_2"][0][:, idx])

    def cols(x):
        return x.reshape(-1, 128).T

    pad = np.zeros((128, 2), np.float32)
    pad[0:8, 0] = v["ssd_dt_bias"][0]
    pad[0:8, 1] = v["ssd_a_log"][0]
    a["vec"] = np.ascontiguousarray(np.concatenate([
        cols(v["norm_mix_w"][0]), cols(v["norm_ffn_w"][0]), cols(v["norm_final_w"]), cols(v["norm_g_2"]),
        cols(v["kv_norm_g_2"]), cols(v["gla_b_gate"][0]), cols(v["gla_norm_w"][0]), cols(v["ssd_conv_w"][0]),
        cols(v["ssd_conv_b"][0]), cols(np.repeat(v["ssd_d"][0], 64)), cols(v["ssd_norm_w"][0]), pad], 1))
    return a


def kernel(**inputs):
    import concourse.bacc as _bacc
    from concourse.bass_utils import run_bass_kernel_spmd as _run

    nc = _bacc.Bacc("TRN2", target_bir_lowering=False, num_devices=1)
    laid = {k: v for k, v in _layout({k: np.asarray(v) for k, v in inputs.items()}).items() if v.size}
    arrays, aps = {}, {}
    for name, a in laid.items():
        arrays[f"in_{name}"] = a
        aps[name] = nc.dram_tensor(f"in_{name}", a.shape, F32, kind="ExternalInput").ap()
    out = nc.dram_tensor("out_T", (1024, T), F32, kind="ExternalOutput").ap()
    build_program(nc, aps, out)
    r = _run(nc, [arrays], core_ids=[0])
    return np.ascontiguousarray(r.results[0]["out_T"].T)[None]
```
